# Optimizing a Trainium2 kernel written in Bass

```python
import math
import jax
import jax.numpy as jnp
from jax import lax
import numpy as np

D_MODEL = 1024
BATCH = 1
SEQ = 2048
DEPTH = 1

GRID_W = 64
CTX_LEN = 256

DN_HEADS = 4
DN_HEAD_DIM = 128
DN_WIDTH = DN_HEADS * DN_HEAD_DIM
DN_CHUNK = 64
DN_CONV_W = 3
HY_WIDTH = 256
HY_BANDS = 16
HY_EMB = 1 + 2 * HY_BANDS
HY_ORDER = 64
HY_CONV_W = 3
HY_TARGET = 1e-2
HY_FAST = 0.3
HY_SLOW = 1.5
SC_WIDTH = 256
SC_CONV_W = 3
N_BRANCH = 3
A_COLS = 4 * DN_WIDTH + 4 * DN_HEADS
B_OFF = A_COLS
C_OFF = B_OFF + 3 * HY_WIDTH
G_OFF = C_OFF + 3 * SC_WIDTH
N_IN = G_OFF + N_BRANCH * D_MODEL
N_EXPERTS = 16
CAPACITY_FACTOR = 2
EXPERT_FF = 768
NORM_EPS = 1e-6

kernel_name = "hybrid_deltanet_hyena_shortconv_ecmoe_diffusion"

def rmsnorm(x, g):
    xf = x.astype(jnp.float32)
    y = xf * lax.rsqrt(jnp.mean(xf * xf, axis=-1, keepdims=True) + NORM_EPS)
    return (y * g.astype(jnp.float32)).astype(x.dtype)

def l2norm(t):
    return t * lax.rsqrt(jnp.sum(t * t, axis=-1, keepdims=True) + 1e-6)

def short_conv(u, w, rows):
    k = w.shape[0]
    pad = k // 2
    b, l, ch = u.shape
    v = u if rows is None else u.reshape(b, rows, GRID_W, ch)
    n = v.shape[-2]
    vp = jnp.pad(v, [(0, 0)] * (v.ndim - 2) + [(pad, pad), (0, 0)])
    y = sum(vp[..., j:j + n, :] * w[j] for j in range(k))
    return y.reshape(b, l, ch)

def gated_delta_chunked(q, k, v, g, beta, s0):
    b, l, h, _ = q.shape
    dv = v.shape[-1]
    n = l // DN_CHUNK

    def blk(t):
        t = t.reshape((b, n, DN_CHUNK, h) + t.shape[3:])
        return jnp.moveaxis(t, 3, 1)

    q, k, v, g, beta = [blk(t) for t in (q, k, v, g, beta)]
    gc = jnp.cumsum(g, axis=-1)
    incl = jnp.tril(jnp.ones((DN_CHUNK, DN_CHUNK), bool))
    strict = jnp.tril(jnp.ones((DN_CHUNK, DN_CHUNK), bool), -1)
    diff = gc[..., :, None] - gc[..., None, :]
    decay = jnp.where(incl, jnp.exp(jnp.where(incl, diff, 0.0)), 0.0)
    kb = k * beta[..., None]
    m = jnp.where(strict, jnp.einsum('bhncd,bhnsd->bhncs', kb, k) * decay, 0.0)
    a = m + jnp.eye(DN_CHUNK, dtype=m.dtype)
    u = lax.linalg.triangular_solve(a, v * beta[..., None], left_side=True, lower=True, unit_diagonal=True)
    w = lax.linalg.triangular_solve(a, kb * jnp.exp(gc)[..., None], left_side=True, lower=True,
                                    unit_diagonal=True)
    attn = jnp.where(incl, jnp.einsum('bhncd,bhnsd->bhncs', q, k) * decay, 0.0)
    q_dec = q * jnp.exp(gc)[..., None]
    g_last = gc[..., -1]
    k_dec = k * jnp.exp(g_last[..., None] - gc)[..., None]

    def step(s, inp):
        qd, kd, ui, wi, ai, gl = inp
        v_new = ui - jnp.einsum('bhck,bhkv->bhcv', wi, s)
        o = jnp.einsum('bhck,bhkv->bhcv', qd, s) + jnp.einsum('bhcs,bhsv->bhcv', ai, v_new)
        s = s * jnp.exp(gl)[..., None, None] + jnp.einsum('bhck,bhcv->bhkv', kd, v_new)
        return s, o

    xs = tuple(jnp.moveaxis(t, 2, 0) for t in (q_dec, k_dec, u, w, attn, g_last))
    s_fin, o = lax.scan(step, s0, xs)
    o = jnp.moveaxis(o, 0, 2).reshape(b, h, l, dv)
    return jnp.moveaxis(o, 1, 2), s_fin

def deltanet_branch(pa, lp, s0_f, s0_b, rows):
    b, l, _ = pa.shape
    f32 = jnp.float32
    qkv = jax.nn.silu(short_conv(pa[..., :3 * DN_WIDTH], lp['dn_conv_w'], rows)).astype(f32)
    q, k, v = [t.reshape(b, l, DN_HEADS, DN_HEAD_DIM) for t in jnp.split(qkv, 3, axis=-1)]
    q = l2norm(q) * (DN_HEAD_DIM ** -0.5)
    k = l2norm(k)
    z = pa[..., 3 * DN_WIDTH:4 * DN_WIDTH].astype(f32).reshape(b, l, DN_HEADS, DN_HEAD_DIM)
    gcols = pa[..., 4 * DN_WIDTH:].astype(f32).reshape(b, l, 2, 2, DN_HEADS)
    beta = jax.nn.sigmoid(gcols[:, :, 0])
    g = -jnp.exp(lp['dn_a_log'].astype(f32)) * jax.nn.softplus(gcols[:, :, 1] + lp['dn_dt_bias'].astype(f32))
    o_f, s_f = gated_delta_chunked(q, k, v, g[:, :, 0], beta[:, :, 0], s0_f)
    flip = lambda t: jnp.flip(t, axis=1)
    o_b, s_b = gated_delta_chunked(flip(q), flip(k), flip(v), flip(g[:, :, 1]), flip(beta[:, :, 1]), s0_b)
    o = rmsnorm(o_f + flip(o_b), lp['dn_norm_g']) * jax.nn.silu(z)
    return o.reshape(b, l, DN_WIDTH).astype(pa.dtype), s_f, s_b

def hyena_filter(l, lp):
    f32 = jnp.float32
    pos = jnp.arange(l, dtype=f32)
    t = (pos / max(l - 1, 1))[:, None]
    bands = jnp.linspace(1e-4, HY_BANDS - 1, HY_BANDS, dtype=f32)
    ang = (2.0 * math.pi / l) * pos[:, None] * bands[None, :]
    feats = jnp.concatenate([t, jnp.cos(ang), -jnp.sin(ang)], axis=-1)
    freq = lp['hy_freq'].astype(f32)
    hh = jnp.sin(freq * (feats @ lp['hy_w1'].astype(f32) + lp['hy_b1'].astype(f32)))
    hh = jnp.sin(freq * (hh @ lp['hy_w2'].astype(f32) + lp['hy_b2'].astype(f32)))
    hh = hh @ lp['hy_w3'].astype(f32)
    deltas = jnp.abs(jnp.linspace(math.log(HY_TARGET) / HY_SLOW, math.log(HY_TARGET) / HY_FAST,
                                  HY_WIDTH, dtype=f32))
    window = jnp.exp(-t * deltas[None, :])
    h_fwd = hh[:, :HY_WIDTH] * window
    h_bwd = hh[:, HY_WIDTH:] * window
    return jnp.concatenate([h_fwd, jnp.zeros((1, HY_WIDTH), f32), h_bwd[:0:-1]], axis=0)

def hyena_branch(pb, lp, rows):
    u = (short_conv(pb, lp['hy_conv_w'], rows) + lp['hy_conv_b']).astype(jnp.float32)
    x0, x1, v = jnp.split(u, 3, axis=-1)
    z = x1 * v
    l = z.shape[1]
    kern = hyena_filter(l, lp)
    y = jnp.fft.irfft(jnp.fft.rfft(z, n=2 * l, axis=1) * jnp.fft.rfft(kern, axis=0)[None],
                      n=2 * l, axis=1)[:, :l]
    y = x0 * (y + z * lp['hy_d_bias'].astype(jnp.float32))
    return y.astype(pb.dtype)

def shortconv_branch(pc, lp, rows):
    bg, cg, hx = jnp.split(pc, 3, axis=-1)
    return bg * short_conv(cg * hx, lp['sc_conv_w'], rows)

def token_mixer(h, lp, s0_f, s0_b, rows):
    p = h @ lp['w_in']
    ya, s_f, s_b = deltanet_branch(p[..., :A_COLS], lp, s0_f, s0_b, rows)
    yb = hyena_branch(p[..., B_OFF:C_OFF], lp, rows)
    yc = shortconv_branch(p[..., C_OFF:G_OFF], lp, rows)
    gates = jax.nn.sigmoid(p[..., G_OFF:]).reshape(p.shape[:2] + (N_BRANCH, D_MODEL))
    merged = (gates[..., 0, :] * (ya @ lp['w_branch_a'])
              + gates[..., 1, :] * (yb @ lp['w_branch_b'])
              + gates[..., 2, :] * (yc @ lp['w_branch_c']))
    return merged @ lp['w_out'], s_f, s_b

def expert_choice_moe(h, router_w, w_gate, w_up, w_down):
    b, n, _ = h.shape
    cap = CAPACITY_FACTOR * n // N_EXPERTS
    aff = jax.nn.softmax((h @ router_w).astype(jnp.float32), axis=-1)
    top_val, top_idx = lax.top_k(jnp.swapaxes(aff, 1, 2), cap)
    bidx = jnp.arange(b)[:, None, None]
    xe = h[bidx, top_idx]
    hid = jax.nn.silu(jnp.einsum('becd,edf->becf', xe, w_gate)) * jnp.einsum('becd,edf->becf', xe, w_up)
    ye = jnp.einsum('becf,efd->becd', hid, w_down) * top_val[..., None].astype(h.dtype)
    return jnp.zeros_like(h).at[bidx, top_idx].add(ye.astype(h.dtype))

def setup_inputs(seed: int = 0) -> dict:
    key = jax.random.key(seed)
    ks = jax.random.split(key, 40)
    D = D_MODEL

    def nrm(i, shape, scale):
        return jax.random.normal(ks[i], shape, jnp.float32) * scale

    dt = jnp.exp(jax.random.uniform(ks[10], (DEPTH, 2, DN_HEADS), jnp.float32, math.log(1e-3), math.log(1e-1)))
    return {
        "x": nrm(0, (BATCH, SEQ, D), 1.0),
        "c": nrm(1, (BATCH, D), 1.0),
        "ctx": nrm(2, (BATCH, CTX_LEN, D), 1.0),
        "c_ctx": nrm(3, (D,), 1.0),
        "ada_w": nrm(4, (DEPTH, D, 6 * D), D ** -0.5),
        "ada_b": nrm(5, (DEPTH, 6 * D), 0.02),
        "norm1_g": 1.0 + nrm(6, (DEPTH, D), 0.02),
        "norm2_g": 1.0 + nrm(7, (DEPTH, D), 0.02),
        "w_in": nrm(8, (DEPTH, D, N_IN), D ** -0.5),
        "dn_conv_w": nrm(9, (DEPTH, DN_CONV_W, 3 * DN_WIDTH), DN_CONV_W ** -0.5),
        "dn_a_log": jnp.log(jax.random.uniform(ks[11], (DEPTH, 2, DN_HEADS), jnp.float32, 1.0, 16.0)),
        "dn_dt_bias": dt + jnp.log(-jnp.expm1(-dt)),
        "dn_norm_g": 1.0 + nrm(12, (DEPTH, DN_HEAD_DIM), 0.02),
        "hy_conv_w": nrm(13, (DEPTH, HY_CONV_W, 3 * HY_WIDTH), HY_CONV_W ** -0.5),
        "hy_conv_b": nrm(14, (DEPTH, 3 * HY_WIDTH), 0.02),
        "hy_w1": nrm(15, (DEPTH, HY_EMB, HY_ORDER), HY_EMB ** -0.5),
        "hy_b1": nrm(16, (DEPTH, HY_ORDER), 0.1),
        "hy_w2": nrm(17, (DEPTH, HY_ORDER, HY_ORDER), HY_ORDER ** -0.5),
        "hy_b2": nrm(18, (DEPTH, HY_ORDER), 0.1),
        "hy_w3": nrm(19, (DEPTH, HY_ORDER, 2 * HY_WIDTH), 0.02),
        "hy_freq": 1.0 + nrm(20, (DEPTH, HY_ORDER), 0.02),
        "hy_d_bias": nrm(21, (DEPTH, HY_WIDTH), 1.0),
        "sc_conv_w": nrm(22, (DEPTH, SC_CONV_W, SC_WIDTH), SC_CONV_W ** -0.5),
        "w_branch_a": nrm(23, (DEPTH, DN_WIDTH, D), DN_WIDTH ** -0.5),
        "w_branch_b": nrm(24, (DEPTH, HY_WIDTH, D), HY_WIDTH ** -0.5),
        "w_branch_c": nrm(25, (DEPTH, SC_WIDTH, D), SC_WIDTH ** -0.5),
        "w_out": nrm(26, (DEPTH, D, D), D ** -0.5),
        "router_w": nrm(27, (DEPTH, D, N_EXPERTS), D ** -0.5),
        "exp_w_gate": nrm(28, (DEPTH, N_EXPERTS, D, EXPERT_FF), D ** -0.5),
        "exp_w_up": nrm(29, (DEPTH, N_EXPERTS, D, EXPERT_FF), D ** -0.5),
        "exp_w_down": nrm(30, (DEPTH, N_EXPERTS, EXPERT_FF, D), EXPERT_FF ** -0.5),
        "final_norm_g": 1.0 + nrm(31, (D,), 0.02),
    }

def reference(x, c, ctx, c_ctx, ada_w, ada_b, norm1_g, norm2_g, w_in, dn_conv_w, dn_a_log, dn_dt_bias,
              dn_norm_g, hy_conv_w, hy_conv_b, hy_w1, hy_b1, hy_w2, hy_b2, hy_w3, hy_freq, hy_d_bias,
              sc_conv_w, w_branch_a, w_branch_b, w_branch_c, w_out, router_w, exp_w_gate, exp_w_up,
              exp_w_down, final_norm_g):
    b = x.shape[0]
    rows = x.shape[1] // GRID_W
    silu_c = jax.nn.silu(c)
    silu_cc = jax.nn.silu(c_ctx)
    s0 = jnp.zeros((b, DN_HEADS, DN_HEAD_DIM, DN_HEAD_DIM), jnp.float32)
    for i in range(DEPTH):
        lp = {
            'w_in': w_in[i], 'dn_conv_w': dn_conv_w[i], 'dn_a_log': dn_a_log[i], 'dn_dt_bias': dn_dt_bias[i],
            'dn_norm_g': dn_norm_g[i], 'hy_conv_w': hy_conv_w[i], 'hy_conv_b': hy_conv_b[i],
            'hy_w1': hy_w1[i], 'hy_b1': hy_b1[i], 'hy_w2': hy_w2[i], 'hy_b2': hy_b2[i], 'hy_w3': hy_w3[i],
            'hy_freq': hy_freq[i], 'hy_d_bias': hy_d_bias[i], 'sc_conv_w': sc_conv_w[i],
            'w_branch_a': w_branch_a[i], 'w_branch_b': w_branch_b[i], 'w_branch_c': w_branch_c[i],
            'w_out': w_out[i],
        }
        mod_x = (silu_c @ ada_w[i] + ada_b[i])[:, None, :]
        mod_c = silu_cc @ ada_w[i] + ada_b[i]
        sh1x, sc1x, g1x, sh2x, sc2x, g2x = jnp.split(mod_x, 6, axis=-1)
        sh1c, sc1c, g1c, sh2c, sc2c, g2c = jnp.split(mod_c, 6, axis=-1)

        hc = rmsnorm(ctx, norm1_g[i]) * (1.0 + sc1c) + sh1c
        if i == DEPTH - 1:
            _, s_f, s_b = deltanet_branch(hc @ w_in[i][:, :A_COLS], lp, s0, s0, None)
        else:
            mix_c, s_f, s_b = token_mixer(hc, lp, s0, s0, None)
            ctx = ctx + g1c * mix_c
            hc2 = rmsnorm(ctx, norm2_g[i]) * (1.0 + sc2c) + sh2c
            ctx = ctx + g2c * expert_choice_moe(hc2, router_w[i], exp_w_gate[i], exp_w_up[i], exp_w_down[i])

        hx = rmsnorm(x, norm1_g[i]) * (1.0 + sc1x) + sh1x
        mix_x, _, _ = token_mixer(hx, lp, s_f, s_b, rows)
        x = x + g1x * mix_x
        hx2 = rmsnorm(x, norm2_g[i]) * (1.0 + sc2x) + sh2x
        x = x + g2x * expert_choice_moe(hx2, router_w[i], exp_w_gate[i], exp_w_up[i], exp_w_down[i])
    return rmsnorm(x, final_norm_g)


_drawn_inputs = setup_inputs


def setup_inputs(seed=0):
    import zlib

    import numpy as np

    out = dict(_drawn_inputs(seed))
    spreads = {}
    factors = {'ctx': 8.0,
     'c_ctx': 8.0,
     'norm2_g': 5.465,
     'dn_a_log': 3.076,
     'dn_dt_bias': 2.885,
     'dn_norm_g': 8.0,
     'hy_freq': 3.685,
     'final_norm_g': 2.875}
    for name, (base, spread) in spreads.items():
        noise = np.random.default_rng([zlib.crc32(name.encode()), seed]).standard_normal(out[name].shape)
        drawn = base * np.exp(spread * noise) if base else spread * noise
        out[name] = jnp.asarray(drawn.astype(out[name].dtype))
    for name, factor in factors.items():
        out[name] = (out[name] * factor).astype(out[name].dtype)
    return out
```

```python
import math
from contextlib import ExitStack

import numpy as np
import concourse.bass as bass
from concourse import mybir

F32 = mybir.dt.float32
U32 = mybir.dt.uint32
ALU = mybir.AluOpType
ACT = mybir.ActivationFunctionType
AXX = mybir.AxisListType.X
ds = bass.ds

P = 128
D = 1024
KD = D // P
SEQ, CTX = 2048, 256
TOK = CTX + SEQ
TW = 512
NT = SEQ // TW
GRID_W = 64
HEADS, HD = 4, 128
DNW = HEADS * HD
A_COLS = 4 * DNW + 4 * HEADS
HW = 256
B_OFF = A_COLS
C_OFF = B_OFF + 3 * HW
G_OFF = C_OFF + 3 * HW
NCH = 20
STEPS = (CTX + SEQ) // P
FN = 64
FK = FN // 2 + 1
FR = SEQ // FN
NE, CAP, FF = 16, 256, 768
FT = FF // P
EPS = 1e-6
LEVELS = [2, 4, 8, 16, 32, 64]
CLAMP = -44.0

R_C, R_CC, R_ADAB, R_N1, R_NG = 0, 8, 16, 32, 40
R_HYW, R_HYB, R_SCW, R_HYD, R_DNW, R_MLP = 41, 59, 65, 71, 73, 109
N_ROWS = 112


def shape_tables():
    i = np.arange(P)
    r, c = i[:, None], i[None, :]
    ui, li, su, sl = r <= c, r >= c, r < c, r > c
    tri = np.stack([ui, li, su, sl], 1).astype(np.float32)
    lv = []
    for b in [1] + LEVELS:
        m = (r // (2 * b) == c // (2 * b)) & (r % (2 * b) < b) & (c % (2 * b) >= b)
        lv += [m, m.T]
    lv = np.stack(lv, 1).astype(np.float32)
    n = FN * FN
    w = lambda e: np.exp(-2j * np.pi * (e % n) / n)
    n1, n2, k1 = np.arange(FR), np.arange(FN), np.arange(FK)
    a = w((k1[None, None, :] * (FN * n1[:, None, None] + n2[None, :, None])))
    fa = np.concatenate([a.real, a.imag], 2)
    k2 = np.arange(FN)
    g = w(FN * n2[:, None] * k2[None, :])
    gr, gi = g.real, g.imag
    top = lambda x, y: np.concatenate([np.concatenate(x, 1), np.concatenate(y, 1)], 0)
    g_z = top([gr, gi], [-gi, gr])
    g_zs = top([gi, gr], [gr, -gi])
    f_rr = top([gr, gr], [-gi, -gi])
    b_rr = f_rr
    f_ii = top([-gi, gi], [-gr, gr])
    b_ii = -f_ii
    ginv = top([gr, -gi], [gi, gr])
    gm = np.stack([g_z, g_zs, f_rr, b_rr, f_ii, b_ii, ginv], 1)
    ginv = np.conj(g.T)
    inv = np.concatenate([np.concatenate([ginv.real, ginv.imag], 1),
                          np.concatenate([-ginv.imag, ginv.real], 1)], 0)
    gm[:, 6] = inv
    wt = np.where((k1 == 0) | (k1 == FN // 2), 1.0, 2.0) / n
    dd = np.conj(a).transpose(2, 1, 0) * wt[:, None, None]
    fd = np.concatenate([dd.real, -dd.imag], 0)
    pos = np.arange(SEQ, dtype=np.float64)
    t = pos / (SEQ - 1)
    bands = np.linspace(1e-4, 15, 16)
    ang = (2.0 * math.pi / SEQ) * pos[:, None] * bands
    feats = np.concatenate([t[:, None], np.cos(ang), -np.sin(ang)], 1).T
    deltas = np.abs(np.linspace(math.log(1e-2) / 1.5, math.log(1e-2) / 0.3, HW))
    win = np.exp(-t[:, None] * deltas)
    win2 = np.concatenate([win, win], 1)
    win2[0, HW:] = 0.0
    f = lambda x: np.ascontiguousarray(x, dtype=np.float32)
    return {"t_tri": f(tri), "t_lv": f(lv), "t_eye": f(np.eye(P)), "t_fa": f(fa), "t_g": f(gm),
            "t_fd": f(fd), "t_feat": f(feats), "t_win": f(win2)}


def build(nc, A, out, stop=99):
    scr = lambda name, shape: nc.dram_tensor(name, shape, F32).ap()
    sz_d = scr("sz_d", (16, P, HEADS, P))
    kT_d, qT_d, kN_d, vN_d = [scr(n, (NCH, P, HEADS, P)) for n in ("kT_d", "qT_d", "kN_d", "vN_d")]
    o_d = [scr(n, (NCH, P, HEADS, P)) for n in ("of_d", "ob_d")]
    z_d, y_d = scr("z_d", (SEQ, HW)), scr("y_d", (SEQ, HW))
    h_d = scr("h_d", (SEQ, 2 * HW))
    fa_d = scr("fa_d", (3, 2, FK, FN, HW))
    fb_d = scr("fb_d", (2, FN, FK, HW))
    mg_d = scr("mg_d", (KD, P, SEQ))
    x1_d, h2_d, acc_d = scr("x1_d", (SEQ, D)), scr("h2_d", (SEQ, D)), scr("acc_d", (SEQ, D))

    with ExitStack() as top:
        used = []

        def sem(name):
            used.append(nc.alloc_semaphore(name))
            return used[-1]

        def recycle():
            nc.clear_and_free_semaphores(list(used))
            nc.all_engine_barrier()
            used.clear()

        def sbt(stack, name, shape, dt=F32):
            return stack.enter_context(nc.sbuf_tensor(name, shape, dt))

        PS = [top.enter_context(nc.psum_tensor(f"bank{i}", [P, 512], F32)) for i in range(8)]
        settled = top.enter_context(nc.semaphore("settled"))

        def plainly(eng):
            eng.sem_inc(settled, 1)

        eye = sbt(top, "eye", [P, P])
        ones = sbt(top, "ones", [P, P])
        epst = sbt(top, "epst", [P, 1])
        cols = sbt(top, "cols", [P, N_ROWS])
        modb = sbt(top, "modb", [P, 4, D])
        sh1 = sbt(top, "sh1", [P, KD, 2])
        gain1 = sbt(top, "gain1", [P, KD, 2])

        with ExitStack() as st:
            rows = sbt(st, "rows", [P, P])
            small = sbt(st, "small", [P, 16])
            csil = sbt(st, "csil", [P, 2, KD])
            csilb = sbt(st, "csilb", [P, KD, P])
            ada = sbt(st, "ada", [P, 2, KD, 512])
            n2g = sbt(st, "n2g", [P, D])
            zero = sbt(st, "zero", [P, 4096])
            rows_zero, rows_in, rows_T = sem("rows_zero"), sem("rows_in"), sem("rows_T")
            bcast_in, ada_in, ada_free = sem("bcast_in"), [sem("ada_in0"), sem("ada_in1")], sem("ada_free")
            a_chain, v_chain = sem("a_chain_m"), sem("v_chain_m")
            cols_ok, sil_e, sil_ok = sem("cols_ok"), sem("sil_e"), sem("sil_ok")
            mod_mm, mod_ev, zero_st = sem("mod_mm"), sem("mod_ev"), sem("zero_st")
            with nc.Block() as block:
                @block.sync
                def _(sp):
                    sp.dma_start(eye[:, :], A["t_eye"]).then_inc(rows_in, 16)
                    sp.wait_ge(rows_zero, 2)
                    k8 = lambda v: v.rearrange("(k p) -> k p", p=P)
                    parts = [(R_C, k8(A["c"][0, :])), (R_CC, k8(A["c_ctx"])), (R_ADAB, k8(A["ada_b"][0, 0:2 * D])),
                             (R_N1, k8(A["norm1_g"][0, :])), (R_NG, A["dn_norm_g"]),
                             (R_HYW, A["hy_conv_w"][0].rearrange("j (k p) -> (j k) p", p=P)),
                             (R_HYB, k8(A["hy_conv_b"][0, :])),
                             (R_SCW, A["sc_conv_w"][0].rearrange("j (k p) -> (j k) p", p=P)),
                             (R_HYD, k8(A["hy_d_bias"][0, :])),
                             (R_DNW, A["dn_conv_w"][0].rearrange("j (k p) -> (j k) p", p=P))]
                    for r, src in parts:
                        sp.dma_start(rows[r:r + src.shape[0], :], src).then_inc(rows_in, 16)
                    for r, name in enumerate(("hy_freq", "hy_b1", "hy_b2")):
                        sp.dma_start(rows[R_MLP + r:R_MLP + r + 1, 0:64], A[name]).then_inc(rows_in, 16)
                    sp.dma_start(modb[:, :, :].rearrange("p a b -> p (a b)"),
                                 A["ada_b"][:, 2 * D:6 * D].to_broadcast([P, 4 * D])).then_inc(bcast_in, 16)
                    sp.dma_start(n2g[:, :], A["norm2_g"].to_broadcast([P, D])).then_inc(bcast_in, 16)
                    with sp.Fori(0, 6) as i:
                        for b in range(2):
                            sp.wait_ge(ada_free, i * 2 + b + 1)
                            sp.dma_start(ada[:, b, :, :], A["ada_w"][0, :, ds(i * 1024 + b * 512, 512)]
                                         .rearrange("(k p) c -> p k c", p=P)).then_inc(ada_in[b], 16)
                    sp.wait_ge(rows_zero, 3)
                    for j in range(4):
                        sp.dma_start(acc_d[j * 512:(j + 1) * 512, :].rearrange("(p a) c -> p (a c)", p=P),
                                     zero[:, :]).then_inc(zero_st, 16)
                    sp.wait_ge(zero_st, 64)

                @block.gpsimd
                def _(pool):
                    pool.memset(rows[:, :], 0.0).then_inc(rows_zero, 1)
                    pool.memset(ones[:, :], 1.0).then_inc(rows_zero, 1)
                    pool.memset(zero[:, :], 0.0).then_inc(rows_zero, 1)
                    pool.memset(epst[:, :], EPS)

                @block.scalar
                def _(act):
                    act.wait_ge(cols_ok, 2)
                    act.activation(small[:, :], small[:, :], ACT.Exp, scale=-1.0).then_inc(sil_e, 1)

                @block.vector
                def _(dve):
                    n = [0]

                    def link(ins):
                        n[0] += 1
                        ins.then_inc(v_chain, 1)
                        dve.wait_ge(v_chain, n[0])

                    dve.sem_inc(ada_free, 2)
                    dve.wait_ge(rows_T, 1)
                    dve.tensor_copy(cols[:, :], PS[0][:, 0:N_ROWS]).then_inc(cols_ok, 1)
                    dve.tensor_scalar_max(small[:, :], PS[0][:, 0:16], CLAMP).then_inc(cols_ok, 1)
                    dve.wait_ge(sil_e, 1)
                    link(dve.tensor_scalar_add(small[:, :], small[:, :], 1.0))
                    link(dve.reciprocal(small[:, :], small[:, :]))
                    link(dve.tensor_tensor(csil[:, :, :].rearrange("p a b -> p (a b)"), small[:, :], cols[:, 0:16], ALU.mult))
                    dve.tensor_copy(csilb[:, :, :], csil[:, 0, :].unsqueeze(2).to_broadcast([P, KD, P])).then_inc(sil_ok, 1)
                    dve.wait_ge(bcast_in, 32)
                    mb = modb[:, :, :].rearrange("p a b -> p (a b)")
                    with dve.Fori(0, 4) as i:
                        for b in range(2):
                            dve.wait_ge(mod_mm, i * 2 + b + 5)
                            dst = mb[:, ds(i * 1024 + b * 512, 512)]
                            dve.tensor_tensor(dst, PS[2 + b][:, :], dst, ALU.add).then_inc(mod_ev, 1)
                    dve.wait_ge(mod_ev, 8)
                    link(dve.scalar_tensor_tensor(modb[:, 2, :], modb[:, 2, :], 1.0, n2g[:, :], ALU.add, ALU.mult))
                    m1 = PS[1][:, 0:32].rearrange("p (m s) -> p m s", s=2)
                    bias = cols[:, R_ADAB:R_ADAB + 16].unsqueeze(2).to_broadcast([P, 16, 2])
                    n1 = cols[:, R_N1:R_N1 + KD].unsqueeze(2).to_broadcast([P, KD, 2])
                    link(dve.tensor_tensor(sh1[:, :, :], m1[:, 0:8, :], bias[:, 0:8, :], ALU.add))
                    link(dve.tensor_tensor(gain1[:, :, :], m1[:, 8:16, :], bias[:, 8:16, :], ALU.add))
                    link(dve.scalar_tensor_tensor(gain1[:, :, :], gain1[:, :, :], 1.0, n1, ALU.add, ALU.mult))

                @block.tensor
                def _(pe):
                    pe.wait_ge(rows_in, 14 * 16)
                    pe.transpose(PS[0][:, 0:N_ROWS], rows[0:N_ROWS, :], eye[0:N_ROWS, 0:N_ROWS]).then_inc(rows_T, 1)
                    pe.wait_ge(sil_ok, 1)
                    with pe.Fori(0, 2) as i:
                        for b in range(2):
                            pe.wait_ge(ada_in[b], i * 16 + 16)
                            for m in range(4):
                                for k in range(KD):
                                    last = pe.matmul(PS[1][:, ds(i * 16 + b * 8 + m * 2, 2)],
                                                     ada[:, b, k, m * P:(m + 1) * P], csil[:, :, k],
                                                     start=(k == 0), stop=(k == KD - 1))
                                    if m == 3 and k == KD - 1:
                                        last.then_inc(mod_mm, 1)
                            pe.wait_ge(mod_mm, i * 2 + b + 1)
                            pe.sem_inc(ada_free, 1)
                    with pe.Fori(0, 4) as i:
                        for b in range(2):
                            pe.wait_ge(ada_in[b], i * 16 + 48)
                            if b == 0:
                                pe.wait_ge(mod_mm, i * 2 + 4)
                            for k in range(KD):
                                last = pe.matmul(PS[2 + b][:, :], csilb[:, k, :], ada[:, b, k, :],
                                                 start=(k == 0), stop=(k == KD - 1))
                            last.then_inc(mod_mm, 1)
                            pe.wait_ge(mod_mm, i * 2 + b + 5)
                            pe.wait_ge(mod_ev, i * 2 + b + 1)
                            pe.sem_inc(ada_free, 1)
        if stop == 1:
            return
        PH = top.enter_context(ExitStack())
        hT = sbt(PH, "hT", [P, KD, TOK])

        with ExitStack() as st:
            xb = sbt(st, "xb", [P, 2, 4, D])
            sq = sbt(st, "sq", [P, 4, D])
            ss = sbt(st, "ss", [P, 2, 4])
            x_in, x_free = [sem("x_in0"), sem("x_in1")], sem("x_free")
            ss_ok, rstd_ok, xn_ok = sem("ss_ok"), sem("rstd_ok"), sem("xn_ok")
            xT_mm, xT_ev, a_ch, l_ok, e_ok = sem("xT_mm"), sem("xT_ev"), sem("a_ch_b"), sem("l_ok_b"), sem("e_ok_b")
            with nc.Block() as block:
                @block.sync
                def _(sp):
                    sp.dma_start(xb[:, 1, 0:2, :], A["ctx"][0].rearrange("(j p) c -> p j c", p=P)).then_inc(x_in[1], 16)
                    with sp.Fori(0, 2) as i:
                        for b in range(2):
                            sp.wait_ge(x_free, i * 2 + b + 1)
                            sp.dma_start(xb[:, b, :, :], A["x"][0, ds(i * 1024 + b * 512, 512), :]
                                         .rearrange("(j p) c -> p j c", p=P)).then_inc(x_in[b], 16)

                @block.scalar
                def _(act):
                    def group(b, tiles, g, loads):
                        act.wait_ge(x_in[b], loads)
                        act.wait_ge(xn_ok, g + 1)
                        for j in range(tiles):
                            act.activation(sq[:, j, :], xb[:, b, j, :], ACT.Square,
                                           accum_out=ss[:, b, j:j + 1]).then_inc(ss_ok, 1)
                        return None

                    def root(b, tiles, g, squares):
                        act.wait_ge(ss_ok, squares)
                        act.wait_ge(l_ok, g + 1)
                        act.activation(ss[:, b, 0:tiles], ss[:, b, 0:tiles], ACT.Ln).then_inc(e_ok, 1)
                        act.wait_ge(e_ok, g + 1)
                        act.activation(ss[:, b, 0:tiles], ss[:, b, 0:tiles], ACT.Exp, scale=-0.5).then_inc(rstd_ok, 1)

                    group(1, 2, 0, 16)
                    root(1, 2, 0, 2)
                    with act.Fori(0, 2) as i:
                        for b in range(2):
                            group(b, 4, i * 2 + b + 1, i * 16 + b * 16 + 16)
                            root(b, 4, i * 2 + b + 1, i * 8 + b * 4 + 6)

                @block.vector
                def _(dve):
                    dve.sem_inc(xn_ok, 1)
                    dve.sem_inc(x_free, 1)
                    dve.sem_inc(xT_ev, 4)

                    def group(b, tiles, g, squares, off, s):
                        dve.wait_ge(ss_ok, squares)
                        dve.tensor_scalar(ss[:, b, 0:tiles], ss[:, b, 0:tiles], 1.0 / D, EPS, ALU.mult, ALU.add).then_inc(l_ok, 1)
                        dve.wait_ge(rstd_ok, g + 1)
                        for j in range(tiles):
                            last = dve.tensor_scalar(xb[:, b, j, :], xb[:, b, j, :], ss[:, b, j:j + 1], None, ALU.mult)
                        last.then_inc(xn_ok, 1)
                        for k in range(KD):
                            dve.wait_ge(xT_mm, g * 8 + k + 1)
                            dve.tensor_scalar(hT[:, k, ds(off, tiles * P)], PS[k % 4][:, 0:tiles * P],
                                              gain1[:, k, s:s + 1], sh1[:, k, s:s + 1], ALU.mult, ALU.add).then_inc(xT_ev, 1)

                    group(1, 2, 0, 2, 0, 1)
                    with dve.Fori(0, 2) as i:
                        for b in range(2):
                            group(b, 4, i * 2 + b + 1, i * 8 + b * 4 + 6, i * 1024 + b * 512 + CTX, 0)

                @block.tensor
                def _(pe):
                    def group(b, tiles, g):
                        pe.wait_ge(xn_ok, g + 2)
                        for k in range(KD):
                            pe.wait_ge(xT_ev, g * 8 + k + 1)
                            for j in range(tiles):
                                last = pe.transpose(PS[k % 4][:, j * P:(j + 1) * P], xb[:, b, j, k * P:(k + 1) * P], eye[:, :])
                            last.then_inc(xT_mm, 1)
                        pe.wait_ge(xT_mm, g * 8 + 8)
                        pe.sem_inc(x_free, 1)

                    group(1, 2, 0)
                    with pe.Fori(0, 2) as i:
                        for b in range(2):
                            group(b, 4, i * 2 + b + 1)
        if stop == 2:
            return

        gst = top.enter_context(ExitStack())
        g_all = sbt(gst, "g_all", [P, NCH, 8])
        beta = sbt(gst, "beta", [P, NCH, 8])
        egc = sbt(gst, "egc", [P, NCH, 8])
        erest = sbt(gst, "erest", [P, NCH, 8])
        etot = sbt(gst, "etot", [P, NCH, 8])
        tri = sbt(gst, "tri", [P, 4, P])
        UI, LI, SU, SL = range(4)

        NU = 19
        units = [(kind, n) for kind in range(3) for n in range(5)] + [(3, n) for n in range(1, 5)]
        width = lambda n: CTX if n == 0 else TW
        toff = lambda n: 0 if n == 0 else CTX + (n - 1) * TW
        with ExitStack() as st:
            wq = sbt(st, "wq", [P, 4, KD, P])
            tmp = sbt(st, "tmp", [P, 4, TW])
            sg = sbt(st, "sg", [P, 4, TW])
            yb = sbt(st, "yb", [P, 4, TW])
            s2 = sbt(st, "s2", [P, 4, TW])
            nat = sbt(st, "nat", [P, 4, TW])
            w_in_ok, w_free = [sem(f"w_ok{k}") for k in range(4)], sem("w_free_c")
            mm_ok, ps_free = sem("mm_ok_c"), sem("ps_free_c")
            conv1, conv2, conv3 = sem("conv1"), sem("conv2"), sem("conv3")
            clamp_ok, sig1, sig2, sig3 = sem("clamp_ok"), sem("sig1"), sem("sig2"), sem("sig3")
            y_ok, sq_ok, sum_mm, rn1, rn2 = sem("y_ok"), sem("sq_ok"), sem("sum_mm"), sem("rn1"), sem("rn2")
            yn_ok, tr_mm, nat_ok = sem("yn_ok"), sem("tr_mm"), sem("nat_ok")
            unit_st, unit_done = [sem("unit_st0"), sem("unit_st1")], sem("unit_done")
            def back(u):
                return u - 3 if u >= 4 else min(u - 2, 0)

            with nc.Block() as block:
                @block.sync
                def _(sp):
                    with sp.Fori(0, HEADS) as h:
                        for kind in range(4):
                            sp.wait_ge(w_free, h * 4 + kind + 1)
                            sp.dma_start(wq[:, kind, :, :], A["w_in"][0, :, ds(h * P + kind * DNW, P)]
                                         .rearrange("(k p) c -> p k c", p=P)).then_inc(w_in_ok[kind], 16)

                @block.tensor
                def _(pe):
                    def project(h, u):
                        kind, n = units[u]
                        if u % 5 == 0:
                            pe.wait_ge(w_in_ok[kind], h * 16 + 16)
                        pe.wait_ge(ps_free, h * NU + back(u) + 3)
                        for k in range(KD):
                            last = pe.matmul(PS[u % 4][:, 0:width(n)], wq[:, kind, k, :],
                                             hT[:, k, toff(n):toff(n) + width(n)], start=(k == 0), stop=(k == KD - 1))
                        last.then_inc(mm_ok, 1)
                        if n == 4:
                            pe.wait_ge(mm_ok, h * NU + u + 1)
                            pe.sem_inc(w_free, 1)

                    def norm_sum(h, u):
                        w = width(units[u][1])
                        pe.wait_ge(sq_ok, h * 10 + u + 1)
                        pe.wait_ge(rn1, h * 10 + u + 1)
                        pe.matmul(PS[4 + u % 2][:, 0:w], ones[:, :], s2[:, u % 4, 0:w], start=True, stop=True).then_inc(sum_mm, 1)

                    def turn(h, u):
                        n = units[u][1]
                        if u < 10:
                            pe.wait_ge(yn_ok, h * 10 + u + 1)
                        else:
                            pe.wait_ge(y_ok, h * NU + u + 1)
                        pe.wait_ge(nat_ok, h * 10 + u - 5 + 1)
                        for j in range(width(n) // P):
                            last = pe.transpose(PS[6 + u % 2][:, j * P:(j + 1) * P], yb[:, u % 4, j * P:(j + 1) * P], eye[:, :])
                        last.then_inc(tr_mm, 1)

                    with pe.Fori(0, HEADS) as h:
                        for u in range(NU + 2):
                            if u < NU:
                                project(h, u)
                            if 1 <= u < 11:
                                norm_sum(h, u - 1)
                            if 7 <= u < 17:
                                turn(h, u - 2)

                @block.scalar
                def _(act):
                    act.preload_act_table_set("natural_log_exp_and_others")
                    act.sem_inc(rn1, 2)
                    act.sem_inc(nat_ok, 2)

                    def centre(h, u):
                        kind, n = units[u]
                        w = width(n)
                        act.wait_ge(mm_ok, h * NU + u + 1)
                        act.wait_ge(unit_done, h * NU + back(u) + 3)
                        plainly(act)
                        if kind < 3:
                            act.activation(tmp[:, u % 4, 0:w], PS[u % 4][:, 0:w], ACT.Copy,
                                           scale=cols[:, ds(h + R_DNW + 12 + kind * 4, 1)]).then_inc(conv1, 1)
                        else:
                            act.activation(tmp[:, u % 4, 0:w], PS[u % 4][:, 0:w], ACT.Copy).then_inc(conv1, 1)

                    def logistic(h, u):
                        w = width(units[u][1])
                        s = sg[:, u % 4, 0:w]
                        at = h * NU + u + 1
                        act.wait_ge(clamp_ok, at)
                        act.activation(s, s, ACT.Exp, scale=-1.0).then_inc(sig1, 1)
                        act.wait_ge(sig1, at)
                        act.activation(s, s, ACT.Ln, bias=1.0).then_inc(sig2, 1)
                        act.wait_ge(sig2, at)
                        act.activation(s, s, ACT.Exp, scale=-1.0).then_inc(sig3, 1)

                    def square(h, u):
                        w = width(units[u][1])
                        act.wait_ge(y_ok, h * NU + u + 1)
                        act.activation(s2[:, u % 4, 0:w], yb[:, u % 4, 0:w], ACT.Square).then_inc(sq_ok, 1)

                    def root(h, u):
                        w = width(units[u][1])
                        at = h * 10 + u + 1
                        act.wait_ge(sum_mm, at)
                        act.activation(s2[:, u % 4, 0:w], PS[4 + u % 2][:, 0:w], ACT.Ln, bias=epst[:, 0:1]).then_inc(rn1, 1)
                        act.wait_ge(rn1, at + 2)
                        act.activation(s2[:, u % 4, 0:w], s2[:, u % 4, 0:w], ACT.Exp, scale=-0.5).then_inc(rn2, 1)

                    def to_nat(h, u):
                        w = width(units[u][1])
                        act.wait_ge(tr_mm, h * 10 + u - 5 + 1)
                        act.activation(nat[:, u % 4, 0:w], PS[6 + u % 2][:, 0:w], ACT.Copy).then_inc(nat_ok, 1)

                    with act.Fori(0, HEADS) as h:
                        for u in range(NU + 2):
                            if u < NU:
                                centre(h, u)
                                logistic(h, u)
                                if u < 10:
                                    square(h, u)
                            if 1 <= u < 11:
                                root(h, u - 1)
                            if 7 <= u < 17:
                                to_nat(h, u - 2)

                @block.gpsimd
                def _(pool):
                    def clamp(h, u):
                        w = width(units[u][1])
                        pool.wait_ge(conv3, h * NU + u + 1)
                        plainly(pool)
                        pool.tensor_scalar_max(sg[:, u % 4, 0:w], tmp[:, u % 4, 0:w], CLAMP).then_inc(clamp_ok, 1)

                    def store(h, u):
                        kind, n = units[u]
                        w = width(n)
                        chunks = w // P
                        places = [0, 18] if n == 0 else [2 + (n - 1) * 4]
                        ready = []
                        if kind in (0, 1):
                            pool.wait_ge(yn_ok, h * 10 + u + 1)
                            ready.append((yb, (qT_d, kT_d)[kind]))
                        if kind in (1, 2):
                            pool.wait_ge(nat_ok, h * 10 + u - 5 + 3)
                            ready.append((nat, (None, kN_d, vN_d)[kind]))
                        if kind == 3:
                            pool.wait_ge(y_ok, h * NU + u + 1)
                            ready.append((yb, sz_d))
                            places = [(n - 1) * 4]
                        plainly(pool)
                        for src, dst in ready:
                            for c in places:
                                pool.dma_start(dst[c:c + chunks, :, ds(h, 1), :].rearrange("c p a t -> p c (a t)"),
                                               src[:, u % 4, 0:w].rearrange("p (c t) -> p c t", t=P)).then_inc(unit_st[u % 2], 16)

                    pool.sem_inc(unit_done, 3)
                    per_unit = []
                    for u in range(NU):
                        kind, n = units[u]
                        per_unit.append(16 * (2 if kind == 1 else 1) * (2 if n == 0 else 1))
                    with pool.Fori(0, HEADS) as h:
                        for u in range(NU + 4):
                            if 4 <= u:
                                pool.wait_ge(unit_st[u % 2], h * sum(per_unit[u % 2::2]) + sum(per_unit[u % 2:u - 3:2]))
                                pool.sem_inc(unit_done, 1)
                            if u < NU:
                                clamp(h, u)
                            if 3 <= u < NU + 3:
                                store(h, u - 3)

                @block.vector
                def _(dve):
                    dve.sem_inc(w_free, 4)
                    dve.sem_inc(ps_free, 3)

                    def conv(h, u):
                        kind, n = units[u]
                        w = width(n)
                        row = CTX if n == 0 else GRID_W
                        p = PS[u % 4][:, 0:w].rearrange("p (r c) -> p r c", c=row)
                        t = tmp[:, u % 4, 0:w].rearrange("p (r c) -> p r c", c=row)
                        at = h * NU + u + 1
                        dve.wait_ge(conv1, at)
                        if kind == 3:
                            dve.sem_inc(ps_free, 1)
                            dve.sem_inc(conv2, 1)
                            dve.sem_inc(conv3, 1)
                            return
                        tap = lambda j: cols[:, ds(h + R_DNW + 12 * j + kind * 4, 1)]
                        dve.scalar_tensor_tensor(t[:, :, 1:row], p[:, :, 0:row - 1], tap(0), t[:, :, 1:row],
                                                 ALU.mult, ALU.add).then_inc(conv2, 1)
                        dve.wait_ge(conv2, at)
                        dve.scalar_tensor_tensor(t[:, :, 0:row - 1], p[:, :, 1:row], tap(2), t[:, :, 0:row - 1],
                                                 ALU.mult, ALU.add).then_inc(conv3, 1)
                        dve.wait_ge(conv3, at)
                        dve.sem_inc(ps_free, 1)

                    def silu(h, u):
                        w = width(units[u][1])
                        dve.wait_ge(sig3, h * NU + u + 1)
                        dve.tensor_tensor(yb[:, u % 4, 0:w], tmp[:, u % 4, 0:w], sg[:, u % 4, 0:w], ALU.mult).then_inc(y_ok, 1)

                    def normed(h, u):
                        w = width(units[u][1])
                        scale = HD ** -0.5 if units[u][0] == 0 else 1.0
                        dve.wait_ge(rn2, h * 10 + u + 1)
                        dve.scalar_tensor_tensor(yb[:, u % 4, 0:w], yb[:, u % 4, 0:w], scale, s2[:, u % 4, 0:w],
                                                 ALU.mult, ALU.mult).then_inc(yn_ok, 1)

                    with dve.Fori(0, HEADS) as h:
                        for u in range(NU + 1):
                            if u < NU:
                                conv(h, u)
                                silu(h, u)
                            if 1 <= u < 11:
                                normed(h, u - 1)
        if stop == 3:
            return

        with ExitStack() as st:
            wg = sbt(st, "wg", [P, KD, 16])
            gT = sbt(st, "gT", [16, TOK])
            gl = sbt(st, "gl", [P, NCH, 16])
            dtb, alog = sbt(st, "dtb", [P, 8]), sbt(st, "alog", [P, 8])
            gx, ge, gt = [sbt(st, n, [P, NCH, 8]) for n in ("gx", "ge", "gt")]
            gw_in, gates_mm, gates_T, gates_tr = sem("gw_in"), sem("gates_mm"), sem("gates_T"), sem("gates_tr")
            gd, ga, sums_mm, sums_ok = sem("gd"), sem("ga"), sem("sums_mm"), sem("sums_ok")
            GD_DONE = 22
            with nc.Block() as block:
                @block.sync
                def _(sp):
                    sp.dma_start(wg[:, :, :], A["w_in"][0, :, 4 * DNW:A_COLS].rearrange("(k p) c -> p k c", p=P)).then_inc(gw_in, 16)
                    sp.dma_start(dtb[:, :], A["dn_dt_bias"].rearrange("a d h -> a (d h)").to_broadcast([P, 8])).then_inc(gw_in, 16)
                    sp.dma_start(alog[:, :], A["dn_a_log"].rearrange("a d h -> a (d h)").to_broadcast([P, 8])).then_inc(gw_in, 16)
                    sp.dma_start(tri[:, :, :], A["t_tri"]).then_inc(gw_in, 16)

                @block.tensor
                def _(pe):
                    pe.wait_ge(gw_in, 64)
                    for n in range(5):
                        for k in range(KD):
                            last = pe.matmul(PS[n][0:16, 0:width(n)], wg[:, k, :], hT[:, k, toff(n):toff(n) + width(n)],
                                             start=(k == 0), stop=(k == KD - 1))
                        last.then_inc(gates_mm, 1)
                    pe.wait_ge(gates_T, 5)
                    for c in range(STEPS):
                        last = pe.transpose(PS[5][:, c * 16:(c + 1) * 16], gT[0:16, c * P:(c + 1) * P], eye[0:16, 0:16])
                    last.then_inc(gates_tr, 1)
                    pe.wait_ge(gd, GD_DONE)
                    for i, m in enumerate((UI, LI, SL, SU, None, None)):
                        d = i % 2
                        last = pe.matmul(PS[6][:, i * 80:(i + 1) * 80], ones[:, :] if m is None else tri[:, m, :],
                                         g_all[:, :, d * 4:d * 4 + 4], start=True, stop=True)
                    last.then_inc(sums_mm, 1)

                @block.scalar
                def _(act):
                    act.preload_act_table_set("natural_log_exp_and_others")
                    act.wait_ge(gd, 3)
                    act.activation(beta[:, :, :], beta[:, :, :], ACT.Exp, scale=-1.0).then_inc(ga, 1)
                    act.wait_ge(gw_in, 64)
                    act.activation(alog[:, :], alog[:, :], ACT.Exp).then_inc(ga, 1)
                    act.wait_ge(gd, 4)
                    act.activation(ge[:, :, :], gx[:, :, :], ACT.Abs).then_inc(ga, 1)
                    act.wait_ge(ga, 3)
                    act.activation(ge[:, :, :], ge[:, :, :], ACT.Exp, scale=-1.0).then_inc(ga, 1)
                    act.wait_ge(sums_mm, 1)
                    for i, dst in enumerate((egc, egc, erest, erest, etot, etot)):
                        d = i % 2
                        act.activation(dst[:, :, d * 4:d * 4 + 4], PS[6][:, i * 80:(i + 1) * 80].rearrange("p (c h) -> p c h", h=4),
                                       ACT.Exp).then_inc(sums_ok, 1)

                @block.vector
                def _(dve):
                    n = [0]

                    def link(ins):
                        n[0] += 1
                        ins.then_inc(gd, 1)
                        dve.wait_ge(gd, n[0])

                    for u in range(5):
                        dve.wait_ge(gates_mm, u + 1)
                        dve.tensor_copy(gT[0:16, toff(u):toff(u) + width(u)], PS[u][0:16, 0:width(u)]).then_inc(gates_T, 1)
                    dve.wait_ge(gates_tr, 1)
                    link(dve.tensor_copy(gl[:, 0:STEPS, :].rearrange("p c g -> p (c g)"), PS[5][:, 0:STEPS * 16]))
                    link(dve.tensor_copy(gl[:, STEPS:NCH, :], gl[:, 0:2, :]))
                    link(dve.tensor_scalar_max(beta[:, :, :], gl[:, :, 0:8], CLAMP))
                    over = lambda v: v[:, :].unsqueeze(1).to_broadcast([P, NCH, 8])
                    dve.wait_ge(gw_in, 64)
                    link(dve.tensor_tensor(gx[:, :, :], gl[:, :, 8:16], over(dtb), ALU.add))
                    dve.wait_ge(ga, 1)
                    link(dve.tensor_scalar_add(beta[:, :, :], beta[:, :, :], 1.0))
                    link(dve.reciprocal(beta[:, :, :], beta[:, :, :]))
                    dve.wait_ge(ga, 4)
                    link(dve.tensor_scalar_add(gt[:, :, :], ge[:, :, :], 2.0))
                    link(dve.reciprocal(gt[:, :, :], gt[:, :, :]))
                    link(dve.tensor_tensor(ge[:, :, :], ge[:, :, :], gt[:, :, :], ALU.mult))
                    link(dve.tensor_tensor(gt[:, :, :], ge[:, :, :], ge[:, :, :], ALU.mult))
                    ser = g_all[:, :, :]
                    link(dve.tensor_scalar(ser, gt[:, :, :], 1.0 / 17, None, ALU.mult))
                    for k in range(7, 0, -1):
                        link(dve.scalar_tensor_tensor(ser, ser, 1.0 / (2 * k + 1), gt[:, :, :], ALU.add, ALU.mult))
                    link(dve.scalar_tensor_tensor(ser, ser, 1.0, ge[:, :, :], ALU.add, ALU.mult))
                    link(dve.tensor_scalar(gx[:, :, :], gx[:, :, :], 0.0, None, ALU.max))
                    link(dve.scalar_tensor_tensor(ser, ser, 2.0, gx[:, :, :], ALU.mult, ALU.add))
                    dve.wait_ge(ga, 2)
                    link(dve.scalar_tensor_tensor(ser, ser, -1.0, over(alog), ALU.mult, ALU.mult))
                    assert n[0] == GD_DONE
        if stop == 4:
            return

        with ExitStack() as st:
            lv = sbt(st, "lv", [P, 14, P])
            big = lambda name, n: sbt(st, name, [P, n, HEADS, P])
            kT, qT, kN, vN = big("kT", 4), big("qT", 4), big("kN", 4), big("vN", 4)
            Tb, Eb, AT, N2, off, TT = [big(n, 4) for n in ("Tb", "Eb", "AT", "N2", "off", "TT")]
            S, R, V, O = big("S", 2), big("R", 2), big("V", 2), big("O", 4)
            lv_in, ld, item_free, o_st = sem("lv_in"), [sem(f"ld{q}") for q in range(4)], [sem(f"item_free{q}") for q in range(4)], [sem(f"o_st{q}") for q in range(4)]
            gS_ok, diff_mm, E_ok, Em_ok, G_mm = sem("gS_ok"), sem("diff_mm"), sem("E_ok"), sem("Em_ok"), sem("G_mm")
            at_ok, n_ok, nb_ok, off_ok, tt0_ok = sem("at_ok"), sem("n_ok"), sem("nb_ok"), sem("off_ok"), sem("tt0_ok")
            T0_mm, T0_ok, P_mm, P_ok, TT_mm, up_ok = sem("T0_mm"), sem("T0_ok"), sem("P_mm"), sem("P_ok"), sem("TT_mm"), sem("up_ok")
            kd_ok, kS_mm, r1_ok, o1_ok, r_ok = sem("kd_ok"), sem("kS_mm"), sem("r1_ok"), sem("o1_ok"), sem("r_ok")
            TR_mm, v_ok, upd_mm, sx_ok, s_ok, o_ok = sem("TR_mm"), sem("v_ok"), sem("upd_mm"), sem("sx_ok"), sem("s_ok"), sem("o_ok")
            NL = len(LEVELS)
            UPS = 2 * NL - 1
            QS = range(4)
            heads = range(HEADS)
            b4 = lambda bank: PS[bank][:, :].rearrange("p (h c) -> p h c", c=P)
            mask4 = lambda m: m.unsqueeze(1).to_broadcast([P, HEADS, P])

            def chunk(it, q, ahead=0):
                s, d = q // 2, q % 2
                return it * 2 + (s + 2 * ahead) if d == 0 else it * -2 + (NCH - 1 - s - 2 * ahead)

            def per_token(v, it, q):
                d = q % 2
                return (v[:, ds(chunk(it, q), 1), d * 4:d * 4 + 4].rearrange("p a h -> p (a h)")
                        .unsqueeze(2).to_broadcast([P, HEADS, P]))

            with nc.Block() as block:
                @block.sync
                def _(sp):
                    def load(it, q, ahead):
                        c = chunk(it, q, ahead)
                        for buf, src in ((kT, kT_d), (qT, qT_d), (kN, kN_d), (vN, vN_d)):
                            sp.dma_start(buf[:, q, :, :], src[ds(c, 1), :, :, :].rearrange("a p h t -> p (a h) t")).then_inc(ld[q], 16)

                    sp.dma_start(lv[:, :, :], A["t_lv"]).then_inc(lv_in, 16)
                    for q in QS:
                        load(0, q, 0)
                    with sp.Fori(0, STEPS // 2) as it:
                        for q in QS:
                            sp.wait_ge(o_ok, it * 4 + q + 2)
                            sp.dma_start(o_d[q % 2][ds(chunk(it, q), 1), :, :, :].rearrange("a p h t -> p (a h) t"),
                                         O[:, q, :, :]).then_inc(o_st[q], 16)
                            sp.wait_ge(item_free[q], it + 1)
                            load(it, q, 1)
                    for q in QS:
                        sp.wait_ge(o_st[q], 16 * (STEPS // 2 + 1))
                        sp.wait_ge(ld[q], 64 * (STEPS // 2 + 1))

                @block.tensor
                def _(pe):
                    def mm4(bank, lhsT, rhs, **kw):
                        for h in heads:
                            last = pe.matmul(b4(bank)[:, h, :], lhsT[:, h, :], rhs[:, h, :] if len(rhs.shape) == 3 else rhs,
                                             start=True, stop=True)
                        return last

                    with pe.Fori(0, STEPS // 2) as it:
                        for q in QS:
                            d = q % 2
                            pe.wait_ge(gS_ok, it * 4 + q + 1)
                            if q == 0:
                                pe.wait_ge(s_ok, it * 4 + 2)
                                pe.wait_ge(o_ok, it * 4 + 1)
                            mm4(2 * q, Tb[:, q], tri[:, UI + d, :]).then_inc(diff_mm, 1)
                        for q in QS:
                            pe.wait_ge(ld[q], it * 64 + 64)
                            pe.wait_ge(E_ok, it * 4 + q + 1)
                            mm4(2 * q, kT[:, q], kT[:, q])
                            mm4(2 * q + 1, kT[:, q], qT[:, q]).then_inc(G_mm, 1)
                        for q in QS:
                            pe.wait_ge(tt0_ok, it * 4 + q + 1)
                            pe.wait_ge(at_ok, it * 4 + q + 1)
                            for h in heads:
                                last = pe.transpose(b4(2 * q + 1)[:, h, :], TT[:, q, h, :], eye[:, :])
                            last.then_inc(T0_mm, 1)
                        for l in range(NL):
                            end = l == NL - 1
                            for q in QS:
                                pe.wait_ge(off_ok, it * 4 * (NL + 1) + 4 * (l + 1) + q + 1)
                                if l == 0:
                                    pe.wait_ge(T0_ok, it * 4 + q + 1)
                                else:
                                    pe.wait_ge(up_ok, it * 4 * UPS + 8 * (l - 1) + 2 * q + 6)
                                mm4(2 * q, off[:, q], Tb[:, q]).then_inc(P_mm, 1)
                            for q in QS:
                                pe.wait_ge(P_ok, it * 4 * NL + 4 * l + q + 1)
                                if not end:
                                    mm4(2 * q + 1, TT[:, q], Eb[:, q])
                                mm4(2 * q, Eb[:, q], TT[:, q]).then_inc(TT_mm, 1)
                        for s in range(2):
                            for q in (2 * s, 2 * s + 1):
                                d = q % 2
                                if s == 0:
                                    pe.wait_ge(up_ok, it * 4 * UPS + 4 * UPS + 4)
                                pe.wait_ge(s_ok, it * 4 + q + 1)
                                if s == 1:
                                    pe.wait_ge(o_ok, it * 4 + q)
                                mm4(4 * d, kT[:, q], S[:, d])
                                mm4(4 * d + 1, qT[:, q], S[:, d]).then_inc(kS_mm, 1)
                            for q in (2 * s, 2 * s + 1):
                                d = q % 2
                                pe.wait_ge(r_ok, it * 4 + q + 1)
                                mm4(4 * d + 2, TT[:, q], R[:, d]).then_inc(TR_mm, 1)
                            for q in (2 * s, 2 * s + 1):
                                d = q % 2
                                pe.wait_ge(v_ok, it * 4 + q + 1)
                                pe.wait_ge(kd_ok, it * 4 + q + 1)
                                mm4(4 * d + 3, kN[:, q], V[:, d])
                                mm4(4 * d, AT[:, q], V[:, d]).then_inc(upd_mm, 1)

                @block.scalar
                def _(act):
                    act.preload_act_table_set("natural_log_exp_and_others")
                    flat = lambda t, q: t[:, q, :, :].rearrange("p h c -> p (h c)")
                    with act.Fori(0, STEPS // 2) as it:
                        for q in QS:
                            act.wait_ge(diff_mm, it * 4 + q + 1)
                            act.activation(flat(Eb, q), PS[2 * q][:, :], ACT.Exp).then_inc(E_ok, 1)
                        for q in QS:
                            act.wait_ge(T0_mm, it * 4 + q + 1)
                            act.activation(flat(Tb, q), PS[2 * q + 1][:, :], ACT.Copy).then_inc(T0_ok, 1)
                        for l in range(NL):
                            for q in QS:
                                act.wait_ge(P_mm, it * 4 * NL + 4 * l + q + 1)
                                act.activation(flat(Eb, q), PS[2 * q][:, :], ACT.Copy).then_inc(P_ok, 1)

                @block.gpsimd
                def _(pool):
                    pool.wait_ge(lv_in, 16)
                    with pool.Fori(0, STEPS // 2) as it:
                        for q in QS:
                            d = q % 2
                            pool.wait_ge(up_ok, it * 4 * UPS + 4)
                            plainly(pool)
                            pool.tensor_tensor(Tb[:, q], mask4(tri[:, SL - d, :]), per_token(g_all, it, q), ALU.mult).then_inc(gS_ok, 1)
                        for q in QS:
                            d = q % 2
                            pool.wait_ge(E_ok, it * 4 + q + 1)
                            pool.tensor_tensor(Eb[:, q], Eb[:, q], mask4(tri[:, UI + d, :]), ALU.mult).then_inc(Em_ok, 1)
                        for q in QS:
                            pool.wait_ge(n_ok, it * 4 + q + 1)
                            plainly(pool)
                            pool.tensor_tensor(N2[:, q], N2[:, q], per_token(beta, it, q), ALU.mult).then_inc(nb_ok, 1)
                            pool.wait_ge(nb_ok, it * 4 + q + 1)
                            pool.tensor_tensor(off[:, q], N2[:, q], mask4(lv[:, q % 2, :]), ALU.mult).then_inc(off_ok, 1)
                        for l in range(NL):
                            for q in QS:
                                if l == 0:
                                    pool.wait_ge(tt0_ok, it * 4 + q + 1)
                                else:
                                    pool.wait_ge(P_mm, it * 4 * NL + 4 * (l - 1) + q + 1)
                                pool.tensor_tensor(off[:, q], N2[:, q], mask4(lv[:, 2 * (l + 1) + q % 2, :]), ALU.mult).then_inc(off_ok, 1)
                        for q in QS:
                            pool.wait_ge(ld[q], it * 64 + 64)
                            plainly(pool)
                            pool.tensor_tensor(kN[:, q], kN[:, q], per_token(erest, it, q), ALU.mult).then_inc(kd_ok, 1)
                        for q in QS:
                            d = q % 2
                            pool.wait_ge(r1_ok, it * 4 + q + 1)
                            pool.tensor_tensor(R[:, d], vN[:, q], R[:, d], ALU.subtract).then_inc(r_ok, 1)
                            plainly(pool)
                            pool.tensor_tensor(S[:, d], S[:, d], per_token(etot, it, q), ALU.mult).then_inc(sx_ok, 1)

                @block.vector
                def _(dve):
                    dve.sem_inc(up_ok, 4)
                    dve.sem_inc(o_ok, 1)
                    for q in QS:
                        dve.sem_inc(o_st[q], 16)
                    for d in range(2):
                        dve.memset(S[:, d], 0.0).then_inc(s_ok, 1)
                    with dve.Fori(0, STEPS // 2) as it:
                        for q in QS:
                            dve.wait_ge(G_mm, it * 4 + q + 1)
                            dve.wait_ge(Em_ok, it * 4 + q + 1)
                            dve.tensor_tensor(N2[:, q], Eb[:, q], b4(2 * q), ALU.mult).then_inc(n_ok, 1)
                            dve.tensor_tensor(AT[:, q], Eb[:, q], b4(2 * q + 1), ALU.mult).then_inc(at_ok, 1)
                        for q in QS:
                            dve.wait_ge(off_ok, it * 4 * (NL + 1) + q + 1)
                            dve.tensor_tensor(TT[:, q], mask4(eye[:, :]), off[:, q], ALU.subtract).then_inc(tt0_ok, 1)
                        for l in range(NL):
                            for q in QS:
                                dve.wait_ge(TT_mm, it * 4 * NL + 4 * l + q + 1)
                                if l < NL - 1:
                                    dve.tensor_tensor(Tb[:, q], Tb[:, q], b4(2 * q + 1), ALU.subtract).then_inc(up_ok, 1)
                                dve.tensor_tensor(TT[:, q], TT[:, q], b4(2 * q), ALU.subtract).then_inc(up_ok, 1)
                        for s in range(2):
                            qs = (2 * s, 2 * s + 1)
                            for q in qs:
                                d = q % 2
                                dve.wait_ge(kS_mm, it * 4 + q + 1)
                                dve.tensor_tensor(R[:, d], b4(4 * d), per_token(egc, it, q), ALU.mult).then_inc(r1_ok, 1)
                                dve.wait_ge(o_st[q], it * 16 + 16)
                                dve.tensor_tensor(O[:, q], b4(4 * d + 1), per_token(egc, it, q), ALU.mult).then_inc(o1_ok, 1)
                            for q in qs:
                                d = q % 2
                                dve.wait_ge(TR_mm, it * 4 + q + 1)
                                dve.tensor_tensor(V[:, d], b4(4 * d + 2), per_token(beta, it, q), ALU.mult).then_inc(v_ok, 1)
                            for q in qs:
                                d = q % 2
                                dve.wait_ge(upd_mm, it * 4 + q + 1)
                                dve.wait_ge(sx_ok, it * 4 + q + 1)
                                dve.tensor_tensor(S[:, d], S[:, d], b4(4 * d + 3), ALU.add).then_inc(s_ok, 1)
                                dve.wait_ge(o1_ok, it * 4 + q + 1)
                                dve.tensor_tensor(O[:, q], O[:, q], b4(4 * d), ALU.add).then_inc(o_ok, 1)
                                dve.sem_inc(item_free[q], 1)
        if stop == 5:
            return
        gst.close()
        recycle()

        with ExitStack() as st:
            feat, hw, win = sbt(st, "feat", [33, TW]), sbt(st, "hw", [P, 4, TW]), sbt(st, "win", [P, 4, TW])
            w1, w2, w3 = sbt(st, "w1", [33, 64]), sbt(st, "w2", [64, 64]), sbt(st, "w3", [64, 2 * HW])
            arg, turns, hid = sbt(st, "arg", [64, TW]), sbt(st, "turns", [64, TW]), sbt(st, "hid", [64, 2, TW])
            mw_in, f_in, f_free, f_st = sem("mw_in"), sem("f_in"), sem("f_free"), sem("f_st")
            l_mm, l_arg, l_sin, l3_mm, l3_ok, f_ch = sem("l_mm"), sem("l_arg"), sem("l_sin"), sem("l3_mm"), sem("l3_ok"), sem("f_ch")
            MAGIC = 1.5 * 2 ** 23
            PI2_HI = 6.28125
            PI2_LO = 2 * math.pi - PI2_HI
            STEPS_SIN = 6
            with nc.Block() as block:
                @block.sync
                def _(sp):
                    for buf, name in ((w1, "hy_w1"), (w2, "hy_w2"), (w3, "hy_w3")):
                        sp.dma_start(buf[:, :], A[name][0]).then_inc(mw_in, 16)
                    with sp.Fori(0, NT) as i:
                        sp.wait_ge(f_free, i + 1)
                        sp.dma_start(feat[:, :], A["t_feat"][:, ds(i * TW, TW)]).then_inc(f_in, 16)
                        sp.dma_start(win[:, :, :], A["t_win"][ds(i * TW, TW), :].rearrange("(j p) c -> p j c", p=P)).then_inc(f_in, 16)
                        sp.wait_ge(l3_ok, i * 4 + 4)
                        sp.dma_start(h_d[ds(i * TW, TW), :].rearrange("(j p) c -> p j c", p=P), hw[:, :, :]).then_inc(f_st, 16)
                        sp.wait_ge(f_st, i * 16 + 16)
                        plainly(sp)

                @block.tensor
                def _(pe):
                    pe.wait_ge(mw_in, 48)
                    with pe.Fori(0, NT) as i:
                        pe.wait_ge(f_in, i * 32 + 32)
                        plainly(pe)
                        pe.matmul(PS[0][0:64, :], w1[:, :], feat[:, :], start=True, stop=True).then_inc(l_mm, 1)
                        pe.wait_ge(l_sin, i * 2 + 1)
                        plainly(pe)
                        pe.matmul(PS[1][0:64, :], w2[:, :], hid[:, 0, :], start=True, stop=True).then_inc(l_mm, 1)
                        pe.wait_ge(l_sin, i * 2 + 2)
                        for j in range(4):
                            pe.matmul(PS[2 + j][:, :], hid[:, 1, j * P:(j + 1) * P], w3[:, :], start=True, stop=True).then_inc(l3_mm, 1)

                @block.scalar
                def _(act):
                    with act.Fori(0, NT) as i:
                        for l in range(2):
                            act.wait_ge(l_arg, i * 2 + l + 1)
                            act.activation(hid[:, l, :], arg[:, :], ACT.Sin).then_inc(l_sin, 1)

                @block.vector
                def _(dve):
                    dve.sem_inc(f_free, 1)
                    with dve.Fori(0, NT) as i:
                        for l in range(2):
                            at = lambda n: i * 2 * STEPS_SIN + l * STEPS_SIN + n
                            dve.wait_ge(l_mm, i * 2 + l + 1)
                            dve.tensor_scalar(arg[:, :], PS[l][0:64, :], cols[0:64, R_MLP + 1 + l:R_MLP + 2 + l],
                                              cols[0:64, R_MLP:R_MLP + 1], ALU.add, ALU.mult).then_inc(f_ch, 1)
                            dve.wait_ge(f_ch, at(1))
                            dve.tensor_scalar(turns[:, :], arg[:, :], 1 / (2 * math.pi), MAGIC, ALU.mult, ALU.add).then_inc(f_ch, 1)
                            dve.wait_ge(f_ch, at(2))
                            dve.tensor_scalar(turns[:, :], turns[:, :], -MAGIC, None, ALU.add).then_inc(f_ch, 1)
                            dve.wait_ge(f_ch, at(3))
                            dve.scalar_tensor_tensor(arg[:, :], turns[:, :], -PI2_HI, arg[:, :], ALU.mult, ALU.add).then_inc(f_ch, 1)
                            dve.wait_ge(f_ch, at(4))
                            dve.scalar_tensor_tensor(arg[:, :], turns[:, :], -PI2_LO, arg[:, :], ALU.mult, ALU.add).then_inc(f_ch, 1)
                            dve.wait_ge(f_ch, at(5))
                            dve.tensor_scalar(arg[:, :], arg[:, :], 3.1415925, -3.1415925, ALU.min, ALU.max).then_inc(f_ch, 1)
                            dve.wait_ge(f_ch, at(6))
                            dve.sem_inc(l_arg, 1)
                        for j in range(4):
                            dve.wait_ge(l3_mm, i * 4 + j + 1)
                            dve.tensor_tensor(hw[:, j, :], PS[2 + j][:, :], win[:, j, :], ALU.mult).then_inc(l3_ok, 1)
                        dve.wait_ge(l3_ok, i * 4 + 4)
                        dve.sem_inc(f_free, 1)
        if stop == 6:
            return

        yst = top.enter_context(ExitStack())
        x0T = sbt(yst, "x0T", [P, 2, SEQ])
        ycT = sbt(yst, "ycT", [P, 2, SEQ])
        yaT = sbt(yst, "yaT", [P, HEADS, SEQ])
        zT = yaT[:, 0:2, :]

        with ExitStack() as st:
            wh = sbt(st, "wh", [P, 6, KD, P])
            x1s, cs = sbt(st, "x1s", [P, SEQ]), sbt(st, "cs", [P, SEQ])
            tmp, tm2 = sbt(st, "tmp_h", [P, 2, TW]), sbt(st, "tm2", [P, TW])
            nat = sbt(st, "nat_h", [P, 2, TW])
            NH2 = 24
            w_ok, w_free = [sem(f"wh_ok{k}") for k in range(6)], sem("wh_free")
            mm_ok, ps_free, c1, c2, c3 = sem("mm_ok_h"), sem("ps_free_h"), sem("c1_h"), sem("c2_h"), sem("c3_h")
            z_ok, z_tr, znat_ok, z_st, ch_ok, yc_ok, zc_ok = sem("z_ok"), sem("z_tr"), sem("znat_ok"), [sem("z_st0"), sem("z_st1")], sem("ch_ok"), sem("yc_ok"), sem("zc_ok")
            kinds = [(kind, n) for kind in range(6) for n in range(NT)]
            with nc.Block() as block:
                @block.sync
                def _(sp):
                    with sp.Fori(0, 2) as h:
                        for kind in range(6):
                            sp.wait_ge(w_free, h * 6 + kind + 1)
                            sp.dma_start(wh[:, kind, :, :], A["w_in"][0, :, ds(h * P + (B_OFF + kind * HW), P)]
                                         .rearrange("(k p) c -> p k c", p=P)).then_inc(w_ok[kind], 16)

                @block.tensor
                def _(pe):
                    def turn(h, n):
                        pe.wait_ge(z_ok, h * NT + n + 1)
                        pe.wait_ge(znat_ok, h * NT + n + 1)
                        for j in range(4):
                            last = pe.transpose(PS[4 + n % 2][:, j * P:(j + 1) * P], tmp[:, n % 2, j * P:(j + 1) * P], eye[:, :])
                        last.then_inc(z_tr, 1)

                    with pe.Fori(0, 2) as h:
                        for u, (kind, n) in enumerate(kinds):
                            if n == 0:
                                pe.wait_ge(w_ok[kind], h * 16 + 16)
                            pe.wait_ge(ps_free, h * NH2 + u + 1)
                            for k in range(KD):
                                last = pe.matmul(PS[u % 4][:, :], wh[:, kind, k, :], hT[:, k, toff(n + 1):toff(n + 1) + TW],
                                                 start=(k == 0), stop=(k == KD - 1))
                            last.then_inc(mm_ok, 1)
                            if n == NT - 1:
                                pe.wait_ge(mm_ok, h * NH2 + u + 1)
                                pe.sem_inc(w_free, 1)
                            if 9 <= u < 13:
                                turn(h, u - 9)

                @block.scalar
                def _(act):
                    act.sem_inc(znat_ok, 2)
                    for b in range(2):
                        act.sem_inc(z_st[b], 16)
                    with act.Fori(0, 2) as h:
                        for u, (kind, n) in enumerate(kinds):
                            sl = slice(n * TW, (n + 1) * TW)
                            if kind == 5:
                                act.wait_ge(ch_ok, h * NT + n + 1)
                                act.wait_ge(yc_ok, h * NT + n + 1)
                                plainly(act)
                                act.activation(tm2[:, :], tmp[:, n % 2, :], ACT.Copy,
                                               scale=cols[:, ds(h + (R_SCW + 2), 1)]).then_inc(c1, 1)
                                continue
                            act.wait_ge(mm_ok, h * NH2 + u + 1)
                            plainly(act)
                            src = PS[u % 4][:, :]
                            if kind < 3:
                                if kind == 2:
                                    act.wait_ge(zc_ok, h * NT + n + 1)
                                    act.wait_ge(z_tr, h * NT + n) if n else None
                                    plainly(act)
                                dst = (x0T[:, ds(h, 1), sl].rearrange("p a t -> p (a t)"), x1s[:, sl], tmp[:, n % 2, :])[kind]
                                act.activation(dst, src, ACT.Identity, bias=cols[:, ds(h + (R_HYB + kind * 2), 1)],
                                               scale=cols[:, ds(h + (R_HYW + 6 + kind * 2), 1)]).then_inc(c1, 1)
                            elif kind == 3:
                                act.activation(ycT[:, ds(h, 1), sl].rearrange("p a t -> p (a t)"), src, ACT.Copy).then_inc(c1, 1)
                            else:
                                act.activation(cs[:, sl], src, ACT.Copy).then_inc(c1, 1)
                            if 10 <= u < 14:
                                m = u - 10
                                act.wait_ge(z_tr, h * NT + m + 1)
                                act.wait_ge(z_st[m % 2], h * 32 + (m // 2) * 16 + 16)
                                act.activation(nat[:, m % 2, :], PS[4 + m % 2][:, :], ACT.Copy).then_inc(znat_ok, 1)
                                act.wait_ge(znat_ok, h * NT + m + 3)
                                act.dma_start(z_d[m * TW:(m + 1) * TW, ds(h * P, P)].rearrange("(j p) c -> p j c", p=P),
                                              nat[:, m % 2, :].rearrange("p (j c) -> p j c", c=P)).then_inc(z_st[m % 2], 16)
                    for b in range(2):
                        act.wait_ge(z_st[b], 80)

                @block.gpsimd
                def _(pool):
                    pool.sem_inc(zc_ok, 2)
                    with pool.Fori(0, 2) as h:
                        for n in range(NT):
                            pool.wait_ge(z_ok, h * NT + n + 1)
                            plainly(pool)
                            pool.tensor_copy(zT[:, ds(h, 1), n * TW:(n + 1) * TW].rearrange("p a t -> p (a t)"),
                                             tmp[:, n % 2, :]).then_inc(zc_ok, 1)

                @block.vector
                def _(dve):
                    dve.sem_inc(w_free, 6)
                    dve.sem_inc(yc_ok, 1)
                    dve.sem_inc(ps_free, 4)
                    with dve.Fori(0, 2) as h:
                        for u, (kind, n) in enumerate(kinds):
                            at = h * NH2 + u + 1
                            sl = slice(n * TW, (n + 1) * TW)
                            if kind in (3, 4):
                                dve.wait_ge(c1, at)
                                dve.sem_inc(ps_free, 1)
                                dve.sem_inc(c2, 1)
                                dve.sem_inc(c3, 1)
                                continue
                            grid = lambda v: v.rearrange("p (r c) -> p r c", c=GRID_W)
                            if kind == 5:
                                dve.wait_ge(mm_ok, at)
                                if n == 0:
                                    dve.wait_ge(zc_ok, h * NT + NT + 2)
                                dve.tensor_tensor(tmp[:, n % 2, :], cs[:, sl], PS[u % 4][:, :], ALU.mult).then_inc(ch_ok, 1)
                                src, t, base, step = grid(tmp[:, n % 2, :]), grid(tm2[:, :]), R_SCW, 2
                                dve.wait_ge(ch_ok, h * NT + n + 1)
                                dve.sem_inc(ps_free, 1)
                            else:
                                dst = (x0T[:, ds(h, 1), sl].rearrange("p a t -> p (a t)"), x1s[:, sl], tmp[:, n % 2, :])[kind]
                                src, t, base, step = grid(PS[u % 4][:, :]), grid(dst), R_HYW + kind * 2, 6
                            dve.wait_ge(c1, at)
                            dve.scalar_tensor_tensor(t[:, :, 1:GRID_W], src[:, :, 0:GRID_W - 1], cols[:, ds(h + base, 1)],
                                                     t[:, :, 1:GRID_W], ALU.mult, ALU.add).then_inc(c2, 1)
                            dve.wait_ge(c2, at)
                            dve.scalar_tensor_tensor(t[:, :, 0:GRID_W - 1], src[:, :, 1:GRID_W], cols[:, ds(h + (base + 2 * step), 1)],
                                                     t[:, :, 0:GRID_W - 1], ALU.mult, ALU.add).then_inc(c3, 1)
                            dve.wait_ge(c3, at)
                            if kind < 3:
                                dve.sem_inc(ps_free, 1)
                            if kind == 2:
                                dve.tensor_tensor(tmp[:, n % 2, :], tmp[:, n % 2, :], x1s[:, sl], ALU.mult).then_inc(z_ok, 1)
                            if kind == 5:
                                yc = ycT[:, ds(h, 1), sl].rearrange("p a t -> p (a t)")
                                dve.tensor_tensor(yc, yc, tm2[:, :], ALU.mult).then_inc(yc_ok, 1)
                                dve.wait_ge(yc_ok, h * NT + n + 2)
        if stop == 7:
            return

        NB = 4
        EV = NB + NB // 2
        with ExitStack() as st:
            zb = sbt(st, "zb", [FR, 2, NB, HW])
            hb = sbt(st, "hb", [FR, 2, NB, 2 * HW])
            fw = sbt(st, "fw", [FR, 2, NB, 2 * FK])
            az = sbt(st, "az", [2 * FK, 2, 3, NB, HW])
            b_in, b_free, a_mm, a_ev, a_st = [sem("b_in0"), sem("b_in1")], sem("b_free"), sem("a_mm"), sem("a_ev"), [sem("a_st0"), sem("a_st1")]
            NBLK = FN // NB
            with nc.Block() as block:
                @block.sync
                def _(sp):
                    with sp.Fori(0, NBLK // 2) as i:
                        for b in range(2):
                            blk = ds(i * 2 * NB + b * NB, NB)
                            sp.wait_ge(b_free, i * 2 + b + 1)
                            sp.dma_start(zb[:, b], z_d.rearrange("(a n) c -> a n c", n=FN)[:, blk, :]).then_inc(b_in[b], 16)
                            sp.dma_start(hb[:, b], h_d.rearrange("(a n) c -> a n c", n=FN)[:, blk, :]).then_inc(b_in[b], 16)
                            sp.dma_start(fw[:, b], A["t_fa"][:, blk, :]).then_inc(b_in[b], 16)

                @block.tensor
                def _(pe):
                    with pe.Fori(0, NBLK // 2) as i:
                        for b in range(2):
                            pe.wait_ge(b_in[b], i * 48 + 48)
                            for n in range(NB):
                                pe.wait_ge(a_ev, i * (2 * EV) + b * EV + n + n // 2 + 1)
                                last = pe.matmul(PS[n % 4][0:2 * FK, :], fw[:, b, n, :], hb[:, b, n, :], start=True, stop=True)
                                last.then_inc(a_mm, 1)
                                last = pe.matmul(PS[4 + n // 2 % 2][0:2 * FK, n % 2 * HW:(n % 2 + 1) * HW], fw[:, b, n, :], zb[:, b, n, :],
                                                 start=True, stop=True)
                                if n % 2:
                                    last.then_inc(a_mm, 1)
                            pe.wait_ge(a_mm, i * (2 * EV) + b * EV + EV)
                            pe.sem_inc(b_free, 1)

                @block.vector
                def _(dve):
                    dve.sem_inc(b_free, 2)
                    dve.sem_inc(a_ev, 4)
                    for b in range(2):
                        dve.sem_inc(a_st[b], 48)
                    with dve.Fori(0, NBLK // 2) as i:
                        for b in range(2):
                            dve.wait_ge(a_st[b], i * 48 + 48)
                            m = 0
                            for n in range(NB):
                                m += 1
                                dve.wait_ge(a_mm, i * (2 * EV) + b * EV + m)
                                dve.tensor_copy(az[:, b, 1:3, n, :], PS[n % 4][0:2 * FK, :].rearrange("p (s c) -> p s c", s=2)).then_inc(a_ev, 1)
                                if n % 2:
                                    m += 1
                                    dve.wait_ge(a_mm, i * (2 * EV) + b * EV + m)
                                    dve.tensor_copy(az[:, b, 0, n - 1:n + 1, :], PS[4 + n // 2 % 2][0:2 * FK, :].rearrange("p (s c) -> p s c", s=2)).then_inc(a_ev, 1)

                @block.scalar
                def _(act):
                    with act.Fori(0, NBLK // 2) as i:
                        for b in range(2):
                            blk = ds(i * 2 * NB + b * NB, NB)
                            act.wait_ge(a_ev, i * (2 * EV) + b * EV + EV + 4)
                            for s in range(3):
                                act.dma_start(fa_d[s].rearrange("r k n c -> (r k) n c")[:, blk, :], az[:, b, s]).then_inc(a_st[b], 16)
                    for b in range(2):
                        act.wait_ge(a_st[b], 48 * (NBLK // 2 + 1))
        if stop == 8:
            return

        CW = 3 * HW // 2
        with ExitStack() as st:
            gm = sbt(st, "gm", [P, 7, P])
            sp_in = sbt(st, "sp_in", [P, 2, 3, 3, HW])
            xs = sbt(st, "xs", [P, 2, 2, CW])
            yp = sbt(st, "yp", [P, 2, 2, CW])
            bk = sbt(st, "bk", [P, 2, CW])
            g_in, s_in, s_free = sem("g_in"), [sem("s_in0"), sem("s_in1")], sem("s_free")
            sx_mm, sx_cp, sp_pr, sp_y, c_mm, c_cp, c_st = sem("sx_mm"), sem("sx_cp"), sem("sp_pr"), sem("sp_y"), sem("c_mm"), sem("c_cp"), [sem("c_st0"), sem("c_st1")]
            with nc.Block() as block:
                def blocks(eng, body):
                    with eng.Fori(0, FK // 6) as i:
                        for b in range(2):
                            body(i * 2 + b, b, i * 6 + b * 3)
                    body(FK // 6 * 2, 0, FK // 6 * 6)

                @block.sync
                def _(sp):
                    sp.dma_start(gm[:, :, :], A["t_g"]).then_inc(g_in, 16)

                    def body(n, b, k):
                        sp.wait_ge(s_free, n + 1)
                        for s in range(3):
                            for r in range(2):
                                sp.dma_start(sp_in[r * FN:(r + 1) * FN, b, s], fa_d[s, r, ds(k, 3), :, :].rearrange("k n c -> n k c")).then_inc(s_in[b], 16)

                    blocks(sp, body)

                @block.tensor
                def _(pe):
                    pe.wait_ge(g_in, 16)

                    def back(m, v):
                        pe.wait_ge(sp_y, m)
                        pe.wait_ge(c_cp, m)
                        pe.matmul(PS[6 + v][:, 0:CW], gm[:, 6, :], yp[:, v, 0, :], start=True, stop=True).then_inc(c_mm, 1)

                    def body(n, b, k):
                        loads = n * 48 + (96 - 48 * b)
                        pe.wait_ge(s_in[b], loads)
                        for v in range(2):
                            col = slice(v * CW, (v + 1) * CW)
                            sig = [sp_in[:, b, s].rearrange("p k c -> p (k c)")[:, col] for s in range(3)]
                            at = n * 2 + v
                            pe.wait_ge(sx_cp, at * 2 + 1)
                            pe.matmul(PS[0][:, 0:CW], gm[:, 0, :], sig[0], start=True, stop=True)
                            pe.matmul(PS[1][:, 0:CW], gm[:, 1, :], sig[0], start=True, stop=True).then_inc(sx_mm, 1)
                            pe.wait_ge(sp_pr, at * 2 + 1)
                            pe.matmul(PS[2 + 2 * v][:, 0:CW], gm[:, 2, :], sig[1], start=True, stop=False)
                            pe.matmul(PS[2 + 2 * v][:, 0:CW], gm[:, 3, :], sig[2], start=False, stop=True)
                            pe.matmul(PS[3 + 2 * v][:, 0:CW], gm[:, 4, :], sig[1], start=True, stop=False)
                            pe.matmul(PS[3 + 2 * v][:, 0:CW], gm[:, 5, :], sig[2], start=False, stop=True).then_inc(sx_mm, 1)
                            if v == 1:
                                pe.wait_ge(sx_mm, n * 4 + 4)
                                pe.sem_inc(s_free, 1)
                                back(n * 2 + 1, 0)
                        back(n * 2 + 2, 1)

                    blocks(pe, body)

                @block.scalar
                def _(act):
                    act.sem_inc(sx_cp, 1)
                    act.sem_inc(c_cp, 2)
                    for b in range(2):
                        act.sem_inc(c_st[b], 16)

                    def body(n, b, k):
                        for v in range(2):
                            at = n * 2 + v
                            act.wait_ge(sx_mm, at * 2 + 1)
                            for j in range(2):
                                act.activation(xs[:, v, j, :], PS[j][:, 0:CW], ACT.Copy).then_inc(sx_cp, 1)
                        for v in range(2):
                            act.wait_ge(c_mm, n * 2 + v + 1)
                            act.wait_ge(c_st[v], n * 16 + 16)
                            act.activation(bk[:, v, :], PS[6 + v][:, 0:CW], ACT.Copy).then_inc(c_cp, 1)
                            act.wait_ge(c_cp, n * 2 + v + 3)
                            act.dma_start(dst[:, ds(k * HW + v * CW, CW)], bk[:, v, :]).then_inc(c_st[v], 16)

                    dst = fb_d.rearrange("r n k c -> (r n) (k c)")
                    blocks(act, body)
                    for v in range(2):
                        act.wait_ge(c_st[v], 16 * (FK // 3 + 1))

                @block.vector
                def _(dve):
                    dve.sem_inc(s_free, 2)
                    dve.sem_inc(sp_pr, 3)

                    def body(n, b, k):
                        for v in range(2):
                            at = n * 2 + v
                            dve.wait_ge(sx_cp, at * 2 + 3)
                            dve.wait_ge(sx_mm, at * 2 + 2)
                            for j in range(2):
                                dve.tensor_tensor(yp[:, v, j, :], xs[:, v, j, :], PS[2 + 2 * v + j][:, 0:CW], ALU.mult).then_inc(sp_pr, 1)

                    blocks(dve, body)

                @block.gpsimd
                def _(pool):
                    def body(n, b, k):
                        for v in range(2):
                            pool.wait_ge(sp_pr, n * 4 + v * 2 + 5)
                            pool.tensor_tensor(yp[:, v, 0, :], yp[:, v, 0, :], yp[:, v, 1, :], ALU.add).then_inc(sp_y, 1)

                    blocks(pool, body)
        if stop == 9:
            return

        with ExitStack() as st:
            bb = sbt(st, "bb", [2 * FK, 2, NB, HW])
            fd = sbt(st, "fd", [2 * FK, 2, NB, FR])
            ys = sbt(st, "ys", [FR, 2, NB, HW])
            d_in, d_free, d_mm, d_ev, d_st = [sem("d_in0"), sem("d_in1")], sem("d_free"), sem("d_mm"), sem("d_ev"), [sem("d_st0"), sem("d_st1")]
            with nc.Block() as block:
                @block.sync
                def _(sp):
                    with sp.Fori(0, NBLK // 2) as i:
                        for b in range(2):
                            blk = ds(i * 2 * NB + b * NB, NB)
                            sp.wait_ge(d_free, i * 2 + b + 1)
                            for r in range(2):
                                sp.dma_start(bb[r * FK:(r + 1) * FK, b], fb_d[r, blk, :, :].rearrange("n k c -> k n c")).then_inc(d_in[b], 16)
                            sp.dma_start(fd[:, b], A["t_fd"][:, blk, :]).then_inc(d_in[b], 16)

                @block.tensor
                def _(pe):
                    with pe.Fori(0, NBLK // 2) as i:
                        for b in range(2):
                            pe.wait_ge(d_in[b], i * 48 + 48)
                            for n in range(NB):
                                if n % 2 == 0:
                                    pe.wait_ge(d_ev, i * NB + b * (NB // 2) + n // 2 + 1)
                                last = pe.matmul(PS[(b * NB // 2 + n // 2) % 4][0:FR, n % 2 * HW:(n % 2 + 1) * HW], fd[:, b, n, :], bb[:, b, n, :],
                                                 start=True, stop=True)
                                if n % 2:
                                    last.then_inc(d_mm, 1)
                            pe.wait_ge(d_mm, i * NB + b * (NB // 2) + NB // 2)
                            pe.sem_inc(d_free, 1)

                @block.vector
                def _(dve):
                    dve.sem_inc(d_free, 2)
                    dve.sem_inc(d_ev, 4)
                    for b in range(2):
                        dve.sem_inc(d_st[b], 16)
                    with dve.Fori(0, NBLK // 2) as i:
                        for b in range(2):
                            dve.wait_ge(d_st[b], i * 16 + 16)
                            for m in range(NB // 2):
                                dve.wait_ge(d_mm, i * NB + b * (NB // 2) + m + 1)
                                dve.tensor_copy(ys[:, b, 2 * m:2 * m + 2, :], PS[(b * NB // 2 + m) % 4][0:FR, :].rearrange("p (s c) -> p s c", s=2)).then_inc(d_ev, 1)

                @block.scalar
                def _(act):
                    with act.Fori(0, NBLK // 2) as i:
                        for b in range(2):
                            act.wait_ge(d_ev, i * NB + b * (NB // 2) + NB // 2 + 4)
                            act.dma_start(y_d.rearrange("(a n) c -> a n c", n=FN)[:, ds(i * 2 * NB + b * NB, NB), :], ys[:, b]).then_inc(d_st[b], 16)
                    for b in range(2):
                        act.wait_ge(d_st[b], 16 * (NBLK // 2 + 1))
        if stop == 10:
            return

        recycle()
        TILES = SEQ // P
        with ExitStack() as st:
            ofb, obb, szb, sqb = [sbt(st, n, [P, 2, HEADS, P]) for n in ("ofb", "obb", "szb", "sqb")]
            ss = sbt(st, "ss_o", [P, 2, HEADS])
            yn, ty = sbt(st, "yn", [P, 2, 4, HW]), sbt(st, "ty", [P, 2, TW])
            o_in, o_free, sum_ok, osq_ok, oss_ok = [sem("o_in0"), sem("o_in1")], sem("o_free"), sem("sum_ok"), sem("osq_ok"), sem("oss_ok")
            oln, ort, on_ok, o_tr, ya_ok = sem("oln"), sem("ort"), sem("on_ok"), sem("o_tr"), sem("ya_ok")
            y_in, y_free, y_tr, y_ok1, y_ok2 = [sem("y_in0"), sem("y_in1")], sem("y_free"), sem("y_tr"), sem("y_ok1"), sem("y_ok2")
            with nc.Block() as block:
                @block.sync
                def _(sp):
                    with sp.Fori(0, 2) as i:
                        for b in range(2):
                            sp.wait_ge(y_free, i * 2 + b + 1)
                            sp.dma_start(yn[:, b], y_d[ds(i * 1024 + b * TW, TW), :].rearrange("(j p) c -> p j c", p=P)).then_inc(y_in[b], 16)

                    with sp.Fori(0, TILES // 2) as i:
                        for b in range(2):
                            sp.wait_ge(o_free, i * 2 + b + 1)
                            for buf, src, lead in ((ofb, o_d[0], CTX // P), (obb, o_d[1], CTX // P), (szb, sz_d, 0)):
                                sp.dma_start(buf[:, b], src[ds(i * 2 + (b + lead), 1)].rearrange("a p h t -> p (a h) t")).then_inc(o_in[b], 16)
                @block.gpsimd
                def _(pool):
                    with pool.Fori(0, 2) as i:
                        for b in range(2):
                            for h in range(2):
                                pool.wait_ge(y_ok1, i * 4 + b * 2 + h + 3)
                                plainly(pool)
                                v = x0T[:, h, ds(i * 1024 + b * TW, TW)]
                                pool.tensor_tensor(v, v, ty[:, h, :], ALU.mult).then_inc(y_ok2, 1)

                    with pool.Fori(0, TILES // 2) as i:
                        for b in range(2):
                            pool.wait_ge(o_in[b], i * 48 + 48)
                            pool.tensor_tensor(ofb[:, b], ofb[:, b], obb[:, b], ALU.add).then_inc(sum_ok, 1)
                @block.scalar
                def _(act):
                    act.preload_act_table_set("natural_log_exp_and_others")
                    with act.Fori(0, TILES // 2) as i:
                        for b in range(2):
                            at = i * 2 + b + 1
                            act.wait_ge(sum_ok, at)
                            act.activation(sqb[:, b], ofb[:, b], ACT.Square).then_inc(osq_ok, 1)
                            act.wait_ge(oss_ok, at)
                            act.activation(ss[:, b, :], ss[:, b, :], ACT.Ln, bias=epst[:, 0:1], scale=1.0 / HD).then_inc(oln, 1)
                            act.wait_ge(oln, at)
                            act.activation(ss[:, b, :], ss[:, b, :], ACT.Exp, scale=-0.5).then_inc(ort, 1)

                @block.vector
                def _(dve):
                    dve.sem_inc(o_free, 2)
                    dve.sem_inc(y_free, 2)
                    dve.sem_inc(y_ok1, 2)
                    with dve.Fori(0, 2) as i:
                        for b in range(2):
                            for h in range(2):
                                dve.wait_ge(y_tr, i * 4 + b * 2 + h + 1)
                                dve.wait_ge(y_ok2, i * 4 + b * 2 + h + 1)
                                dve.scalar_tensor_tensor(ty[:, h, :], zT[:, h, ds(i * 1024 + b * TW, TW)], cols[:, R_HYD + h:R_HYD + h + 1],
                                                         PS[4 + h][:, :], ALU.mult, ALU.add).then_inc(y_ok1, 1)

                    with dve.Fori(0, TILES // 2) as i:
                        for b in range(2):
                            at = i * 2 + b + 1
                            dve.wait_ge(osq_ok, at)
                            dve.reduce_sum(ss[:, b, :], sqb[:, b], axis=AXX).then_inc(oss_ok, 1)
                            dve.wait_ge(ort, at)
                            dve.tensor_tensor(ofb[:, b], ofb[:, b], ss[:, b, :].unsqueeze(2).to_broadcast([P, HEADS, P]), ALU.mult).then_inc(on_ok, 1)
                            dve.wait_ge(o_tr, at)
                            dve.scalar_tensor_tensor(yaT[:, :, ds(i * 2 * P + b * P, P)], PS[b][:, :].rearrange("p (h t) -> p h t", t=P),
                                                     cols[:, R_NG:R_NG + 1], szb[:, b], ALU.mult, ALU.mult).then_inc(ya_ok, 1)
                            dve.wait_ge(ya_ok, at)
                            dve.sem_inc(o_free, 1)
                @block.tensor
                def _(pe):
                    pe.sem_inc(y_ok2, 2)
                    with pe.Fori(0, 2) as i:
                        for b in range(2):
                            pe.wait_ge(y_in[b], i * 16 + 16)
                            for h in range(2):
                                pe.wait_ge(y_ok1, i * 4 + b * 2 + h + 1)
                                for j in range(4):
                                    last = pe.transpose(PS[4 + h][:, j * P:(j + 1) * P], yn[:, b, j, h * P:(h + 1) * P], eye[:, :])
                                last.then_inc(y_tr, 1)
                            pe.wait_ge(y_tr, i * 4 + b * 2 + 2)
                            pe.sem_inc(y_free, 1)
                    with pe.Fori(0, TILES // 2) as i:
                        for b in range(2):
                            pe.wait_ge(on_ok, i * 2 + b + 1)
                            for h in range(HEADS):
                                last = pe.transpose(PS[b][:, h * P:(h + 1) * P], ofb[:, b, h, :], eye[:, :])
                            last.then_inc(o_tr, 1)
        if stop == 11:
            return

        with ExitStack() as st:
            gw = sbt(st, "gw", [P, 2, 3, KD, P])
            bw = sbt(st, "bw", [P, 2, 8, P])
            sg, pr = sbt(st, "sg_m", [P, 2, TW]), sbt(st, "pr", [P, 4, TW])
            mg = sbt(st, "mg", [P, 2, TW])
            m_in, m_free, g_mm, sg_ok, pr_ok, add1, add2 = [sem("m_in0"), sem("m_in1")], sem("m_free"), sem("g_mm"), sem("sg_ok"), sem("pr_ok"), sem("add1"), sem("add2")
            mg_st = [sem("mg_st0"), sem("mg_st1")]
            branch = [(yaT, 0, 4), (x0T, 4, 2), (ycT, 6, 2)]
            UM = 3 * NT
            with nc.Block() as block:
                @block.sync
                def _(sp):
                    for b in range(2):
                        sp.sem_inc(mg_st[b], 16)

                    def load(m, b):
                        for j in range(3):
                            sp.dma_start(gw[:, b, j], A["w_in"][0, :, ds(m * P + (G_OFF + j * D), P)].rearrange("(k p) c -> p k c", p=P)).then_inc(m_in[b], 16)
                        for name, at, k in (("w_branch_a", 0, 4), ("w_branch_b", 4, 2), ("w_branch_c", 6, 2)):
                            sp.dma_start(bw[:, b, at:at + k], A[name][0, :, ds(m * P, P)].rearrange("(k p) c -> p k c", p=P)).then_inc(m_in[b], 16)

                    load(0, 0)
                    with sp.Fori(0, KD // 2) as i:
                        for b in range(2):
                            sp.wait_ge(m_free, i * 2 + b + 1)
                            load((i * 2 + b + 1) % KD, 1 - b)
                            for n in range(NT):
                                sp.wait_ge(add2, i * (2 * NT) + b * NT + n + 3)
                                sp.dma_start(mg_d[ds(i * 2 + b, 1), :, n * TW:(n + 1) * TW].rearrange("a p t -> p (a t)"),
                                             mg[:, n % 2, :]).then_inc(mg_st[n % 2], 16)
                    for b in range(2):
                        sp.wait_ge(mg_st[b], 16 * (KD * NT // 2 + 1))
                    sp.wait_ge(m_in[0], 96 * (KD // 2 + 1))

                @block.tensor
                def _(pe):
                    with pe.Fori(0, KD // 2) as i:
                        for b in range(2):
                            pe.wait_ge(m_in[b], i * 96 + 96)
                            for u in range(UM):
                                n, j = u // 3, u % 3
                                at = i * (2 * UM) + b * UM + u
                                g, o = PS[u % 4 * 2], PS[u % 4 * 2 + 1]
                                pe.wait_ge(pr_ok, at + 1)
                                for k in range(KD):
                                    pe.matmul(g[:, :], gw[:, b, j, k, :], hT[:, k, toff(n + 1):toff(n + 1) + TW], start=(k == 0), stop=(k == KD - 1))
                                src, w0, nk = branch[j]
                                for k in range(nk):
                                    last = pe.matmul(o[:, :], bw[:, b, w0 + k, :], src[:, k, n * TW:(n + 1) * TW], start=(k == 0), stop=(k == nk - 1))
                                last.then_inc(g_mm, 1)
                            pe.wait_ge(g_mm, i * (2 * UM) + b * UM + UM)
                            pe.sem_inc(m_free, 1)

                @block.scalar
                def _(act):
                    with act.Fori(0, KD // 2) as i:
                        for b in range(2):
                            for u in range(UM):
                                at = i * (2 * UM) + b * UM + u
                                act.wait_ge(g_mm, at + 1)
                                act.wait_ge(pr_ok, at + 3)
                                act.activation(sg[:, u % 2, :], PS[u % 4 * 2][:, :], ACT.Sigmoid).then_inc(sg_ok, 1)

                @block.vector
                def _(dve):
                    dve.sem_inc(m_free, 1)
                    dve.sem_inc(pr_ok, 4)
                    dve.sem_inc(add2, 2)
                    with dve.Fori(0, KD // 2) as i:
                        for b in range(2):
                            for u in range(UM):
                                n, j = u // 3, u % 3
                                at = i * (2 * UM) + b * UM + u
                                dve.wait_ge(sg_ok, at + 1)
                                dve.wait_ge(add2, i * (2 * NT) + b * NT + (u - 1) // 3 + 2)
                                dve.tensor_tensor(pr[:, u % 4, :], sg[:, u % 2, :], PS[u % 4 * 2 + 1][:, :], ALU.mult).then_inc(pr_ok, 1)

                @block.gpsimd
                def _(pool):
                    with pool.Fori(0, KD // 2) as i:
                        for b in range(2):
                            for n in range(NT):
                                at = i * (2 * NT) + b * NT + n
                                u = 3 * n
                                pool.wait_ge(pr_ok, at * 3 + 6)
                                pool.wait_ge(mg_st[n % 2], i * (16 * NT) + (b * NT // 2 + n // 2) * 16 + 16)
                                pool.tensor_tensor(mg[:, n % 2, :], pr[:, u % 4, :], pr[:, (u + 1) % 4, :], ALU.add).then_inc(add1, 1)
                                pool.wait_ge(pr_ok, at * 3 + 7)
                                pool.wait_ge(add1, at + 1)
                                pool.tensor_tensor(mg[:, n % 2, :], mg[:, n % 2, :], pr[:, (u + 2) % 4, :], ALU.add).then_inc(add2, 1)
        if stop == 12:
            return
        yst.close()
        PH.close()

        fst = top.enter_context(ExitStack())
        affT = sbt(fst, "affT", [NE, SEQ])
        fgb = sbt(fst, "fgb", [P, D])
        with ExitStack() as st:
            wo, rw = sbt(st, "wo", [P, KD, D]), sbt(st, "rw", [P, KD, NE])
            mt = sbt(st, "mt", [P, 2, KD, 2 * P])
            xt, x1 = sbt(st, "xt", [P, 2, D]), sbt(st, "x1", [P, 2, D])
            sqx, h2, h2T = sbt(st, "sqx", [P, 2, D]), sbt(st, "h2", [P, 2, D]), sbt(st, "h2T", [P, 2, KD, P])
            s1 = sbt(st, "s1", [P, 2, 1])
            mx, ex, sm = sbt(st, "mx", [P, 2, 1]), sbt(st, "ex", [P, 2, NE]), sbt(st, "sm", [P, 2, 1])
            wo_in, mt_in, mt_free, xt_in = sem("wo_in"), [sem("mt_in0"), sem("mt_in1")], sem("mt_free"), [sem("xt_in0"), sem("xt_in1")]
            wo_mm, g_ok, x1_ok, x1_st, h2_st = sem("wo_mm"), sem("g_ok"), sem("x1_ok"), [sem("x1_st0"), sem("x1_st1")], [sem("h2_st0"), sem("h2_st1")]
            s_sq, s_ln, s_rt, hm_ok, h2_ok, h2_tr, h2_cp = sem("s_sq"), sem("s_ln"), sem("s_rt"), sem("hm_ok"), sem("h2_ok"), sem("h2_tr"), sem("h2_cp")
            lg_mm, mx_ch, ex_ok, rc_ch, aff_ok, aff_tr, affT_ok = sem("lg_mm"), sem("mx_ch"), sem("ex_ok"), sem("rc_ch"), sem("aff_ok"), sem("aff_tr"), sem("affT_ok")
            with nc.Block() as block:
                @block.sync
                def _(sp):
                    sp.dma_start(wo[:, :, :], A["w_out"][0].rearrange("(k p) c -> p k c", p=P)).then_inc(wo_in, 16)
                    sp.dma_start(rw[:, :, :], A["router_w"][0].rearrange("(k p) c -> p k c", p=P)).then_inc(wo_in, 16)
                    sp.dma_start(fgb[:, :], A["final_norm_g"].unsqueeze(0).to_broadcast([P, D])).then_inc(wo_in, 16)
                    with sp.Fori(0, TILES // 4) as i:
                        for j in range(4):
                            if j % 2 == 0:
                                sp.wait_ge(mt_free, i * 2 + j // 2 + 1)
                                sp.dma_start(mt[:, j // 2], mg_d[:, :, ds(i * 512 + j * P, 2 * P)].rearrange("k p t -> p k t")).then_inc(mt_in[j // 2], 16)
                            sp.wait_ge(x1_ok, i * 4 + j + 1)
                            sp.dma_start(xt[:, j % 2], A["x"][0, ds(i * 512 + j * P, P), :]).then_inc(xt_in[j % 2], 16)

                @block.tensor
                def _(pe):
                    def tail(i, j, at):
                        b = j % 2
                        pe.wait_ge(h2_ok, at)
                        pe.wait_ge(h2_cp, at)
                        for k in range(KD):
                            last = pe.transpose(PS[4 + k // 4][:, k % 4 * P:(k % 4 + 1) * P], h2[:, b, k * P:(k + 1) * P], eye[:, :])
                        last.then_inc(h2_tr, 1)
                        pe.wait_ge(h2_cp, at + 1)
                        for k in range(KD):
                            last = pe.matmul(PS[6][:, 0:NE], h2T[:, b, k, :], rw[:, k, :], start=(k == 0), stop=(k == KD - 1))
                        last.then_inc(lg_mm, 1)
                        pe.wait_ge(aff_ok, at)
                        pe.transpose(PS[7][0:NE, 0:P], ex[:, b, :], eye[:, :]).then_inc(aff_tr, 1)

                    pe.wait_ge(wo_in, 48)
                    with pe.Fori(0, TILES // 4) as i:
                        for j in range(4):
                            at = i * 4 + j
                            b = j % 2
                            if b == 0:
                                pe.wait_ge(mt_in[j // 2], i * 16 + 16)
                            pe.wait_ge(g_ok, at * 2 + 1)
                            for c in range(2):
                                for k in range(KD):
                                    last = pe.matmul(PS[2 * b + c][:, :], mt[:, j // 2, k, b * P:(b + 1) * P], wo[:, k, c * 512:(c + 1) * 512],
                                                     start=(k == 0), stop=(k == KD - 1))
                                last.then_inc(wo_mm, 1)
                            if b == 1:
                                pe.wait_ge(wo_mm, at * 2 + 2)
                                pe.sem_inc(mt_free, 1)
                            tail(i, j, at + 1)

                @block.vector
                def _(dve):
                    dve.sem_inc(mt_free, 2)
                    dve.sem_inc(g_ok, 4)
                    dve.sem_inc(x1_ok, 2)
                    with dve.Fori(0, TILES // 4) as i:
                        for j in range(4):
                            at = i * 4 + j
                            b = j % 2
                            dve.wait_ge(x1_st[b], i * 32 + j // 2 * 16 + 16)
                            for c in range(2):
                                dve.wait_ge(wo_mm, at * 2 + c + 1)
                                dve.tensor_tensor(x1[:, b, c * 512:(c + 1) * 512], PS[2 * b + c][:, :], modb[:, 0, c * 512:(c + 1) * 512],
                                                  ALU.mult).then_inc(g_ok, 1)
                            dve.wait_ge(s_rt, at + 1)
                            dve.wait_ge(h2_st[b], i * 32 + j // 2 * 16 + 16)
                            dve.scalar_tensor_tensor(h2[:, b, :], x1[:, b, :], s1[:, b, :], modb[:, 2, :], ALU.mult, ALU.mult).then_inc(hm_ok, 1)
                            dve.wait_ge(lg_mm, at + 1)
                            dve.reduce_max(mx[:, b, :], PS[6][:, 0:NE], axis=AXX).then_inc(mx_ch, 1)
                            dve.wait_ge(mx_ch, at * 2 + 1)
                            dve.tensor_scalar(mx[:, b, :], mx[:, b, :], -1.0, None, ALU.mult).then_inc(mx_ch, 1)
                            dve.wait_ge(ex_ok, at + 1)
                            dve.reciprocal(sm[:, b, :], sm[:, b, :]).then_inc(rc_ch, 1)
                            dve.wait_ge(rc_ch, at + 1)
                            dve.tensor_scalar(ex[:, b, :], ex[:, b, :], sm[:, b, :], None, ALU.mult).then_inc(aff_ok, 1)
                            dve.wait_ge(aff_tr, at + 1)
                            dve.tensor_copy(affT[:, ds(i * 512 + j * P, P)], PS[7][0:NE, 0:P]).then_inc(affT_ok, 1)

                @block.scalar
                def _(act):
                    act.preload_act_table_set("natural_log_exp_and_others")
                    act.sem_inc(h2_cp, 1)
                    for b in range(2):
                        act.sem_inc(x1_st[b], 16)
                        act.sem_inc(h2_st[b], 16)
                    with act.Fori(0, TILES // 4) as i:
                        for j in range(4):
                            at = i * 4 + j
                            b = j % 2
                            act.wait_ge(x1_ok, at + 3)
                            act.dma_start(x1_d[ds(i * 512 + j * P, P), :], x1[:, b, :]).then_inc(x1_st[b], 16)
                            act.activation(sqx[:, b, :], x1[:, b, :], ACT.Square, accum_out=s1[:, b, :]).then_inc(s_sq, 1)
                            act.wait_ge(s_sq, at + 1)
                            act.activation(s1[:, b, :], s1[:, b, :], ACT.Ln, bias=epst[:, 0:1], scale=1.0 / D).then_inc(s_ln, 1)
                            act.wait_ge(s_ln, at + 1)
                            act.activation(s1[:, b, :], s1[:, b, :], ACT.Exp, scale=-0.5).then_inc(s_rt, 1)
                            act.wait_ge(h2_ok, at + 1)
                            act.dma_start(h2_d[ds(i * 512 + j * P, P), :], h2[:, b, :]).then_inc(h2_st[b], 16)
                            act.wait_ge(h2_tr, at + 1)
                            act.activation(h2T[:, b, 0:4, :].rearrange("p k t -> p (k t)"), PS[4][:, :], ACT.Copy)
                            act.activation(h2T[:, b, 4:8, :].rearrange("p k t -> p (k t)"), PS[5][:, :], ACT.Copy).then_inc(h2_cp, 1)
                            act.wait_ge(mx_ch, at * 2 + 2)
                            act.activation(ex[:, b, :], PS[6][:, 0:NE], ACT.Exp, bias=mx[:, b, :], accum_out=sm[:, b, :]).then_inc(ex_ok, 1)
                    for b in range(2):
                        act.wait_ge(x1_st[b], 16 * (TILES // 2 + 1))
                        act.wait_ge(h2_st[b], 16 * (TILES // 2 + 1))

                @block.gpsimd
                def _(pool):
                    with pool.Fori(0, TILES // 4) as i:
                        for j in range(4):
                            at = i * 4 + j
                            b = j % 2
                            pool.wait_ge(g_ok, at * 2 + 6)
                            pool.wait_ge(xt_in[b], i * 32 + j // 2 * 16 + 16)
                            pool.tensor_tensor(x1[:, b, :], x1[:, b, :], xt[:, b, :], ALU.add).then_inc(x1_ok, 1)
                            pool.wait_ge(hm_ok, at + 1)
                            pool.tensor_tensor(h2[:, b, :], h2[:, b, :], modb[:, 1, :], ALU.add).then_inc(h2_ok, 1)
        if stop == 13:
            return

        idxP, valP = sbt(fst, "idxP", [P, 2, NE], U32), sbt(fst, "valP", [P, 2, NE])
        with ExitStack() as st:
            m8, i8 = sbt(st, "m8", [NE, 2, 8]), sbt(st, "i8", [NE, 2, 8], U32)
            vals, idxf = sbt(st, "vals", [NE, CAP]), sbt(st, "idxf", [NE, CAP])
            k_mx, k_ix, k_rp, k_cp, k_tr = sem("k_mx"), sem("k_ix"), sem("k_rp"), sem("k_cp"), sem("k_tr")
            with nc.Block() as block:
                @block.vector
                def _(dve):
                    dve.sem_inc(k_rp, 1)
                    with dve.Fori(0, CAP // 16) as i:
                        for b in range(2):
                            at = i * 2 + b
                            dve.wait_ge(k_rp, at + 1)
                            dve.wait_ge(k_cp, at * 2 + 2)
                            plainly(dve)
                            dve.max(m8[:, b, :], affT[:, :]).then_inc(k_mx, 1)
                            dve.wait_ge(k_mx, at + 1)
                            plainly(dve)
                            dve.max_index(i8[:, b, :], m8[:, b, :], affT[:, :]).then_inc(k_ix, 1)
                            dve.wait_ge(k_ix, at + 1)
                            plainly(dve)
                            dve.match_replace(affT[:, :], m8[:, b, :], affT[:, :], -1.0).then_inc(k_rp, 1)
                    dve.wait_ge(k_tr, 1)
                    dve.tensor_copy(idxP[:, :, :].rearrange("p j e -> p (j e)"), PS[0][:, 0:32])
                    dve.tensor_copy(valP[:, :, :].rearrange("p j e -> p (j e)"), PS[0][:, 32:64])

                @block.scalar
                def _(act):
                    act.sem_inc(k_cp, 4)
                    with act.Fori(0, CAP // 16) as i:
                        for b in range(2):
                            at = i * 2 + b
                            act.wait_ge(k_ix, at + 1)
                            plainly(act)
                            act.activation(vals[:, ds(i * 16 + b * 8, 8)], m8[:, b, :], ACT.Copy).then_inc(k_cp, 1)
                            act.activation(idxf[:, ds(i * 16 + b * 8, 8)], i8[:, b, :], ACT.Copy).then_inc(k_cp, 1)

                @block.tensor
                def _(pe):
                    pe.wait_ge(k_cp, 4 + 2 * (CAP // 8))
                    for j in range(2):
                        pe.transpose(PS[0][:, j * NE:(j + 1) * NE], idxf[:, j * P:(j + 1) * P], eye[0:NE, 0:NE])
                        last = pe.transpose(PS[0][:, 32 + j * NE:32 + (j + 1) * NE], vals[:, j * P:(j + 1) * P], eye[0:NE, 0:NE])
                    last.then_inc(k_tr, 1)
        if stop == 14:
            return

        with ExitStack() as st:
            wgu = sbt(st, "wgu", [P, 2, 2, KD, FF])
            wd = sbt(st, "wd", [P, FT, D])
            xe, xeT = sbt(st, "xe", [P, 2, 2, D]), sbt(st, "xeT", [P, KD, CAP])
            hid, sgm, gm1 = sbt(st, "hid_e", [P, FT, CAP]), sbt(st, "sgm", [P, 2, CAP]), sbt(st, "gm1", [P, 2, CAP])
            ye = sbt(st, "ye", [P, 2, D])
            idc = sbt(st, "idc", [P, 2, 2], U32)
            wgu_in, wgu_free, wd_in, wd_free = [sem("wgu_in0"), sem("wgu_in1")], sem("wgu_free"), sem("wd_in"), sem("wd_free")
            id_ok, xe_in, xe_tr, xe_cp, gu_mm, sg_ok, gs_ok, hid_ok = sem("id_ok"), [sem("xe_in0"), sem("xe_in1")], sem("xe_tr"), sem("xe_cp"), sem("gu_mm"), sem("sg_e"), sem("gs_ok"), sem("hid_ok")
            dn_mm, ye_ok, ye_st, ye_free = sem("dn_mm"), sem("ye_ok"), sem("ye_st"), sem("ye_free")
            with nc.Block() as block:
                @block.sync
                def _(sp):
                    with sp.Fori(0, NE // 2) as i:
                        for b in range(2):
                            e = ds(i * 2 + b, 1)
                            sp.wait_ge(wgu_free, i * 2 + b + 1)
                            for g, name in enumerate(("exp_w_gate", "exp_w_up")):
                                sp.dma_start(wgu[:, b, g], A[name][0, e, :, :].rearrange("a (k p) f -> p (a k) f", p=P)).then_inc(wgu_in[b], 16)
                            sp.wait_ge(wd_free, i * 2 + b + 1)
                            sp.dma_start(wd[:, :, :], A["exp_w_down"][0, e, :, :].rearrange("a (k p) f -> p (a k) f", p=P)).then_inc(wd_in, 16)

                @block.gpsimd
                def _(pool):
                    def gather(at, b, ready):
                        pool.wait_ge(id_ok, ready)
                        plainly(pool)
                        for j in range(2):
                            pool.indirect_dma_start(xe[:, b, j, :], None, h2_d, bass.IndirectOffsetOnAxis(idc[:, b, j:j + 1], 0)).then_inc(xe_in[b], 16)

                    gather(0, 0, 1)
                    with pool.Fori(0, NE // 2) as i:
                        for b in range(2):
                            at = i * 2 + b
                            gather(at + 1, 1 - b, at + 2)
                            for j in range(2):
                                pool.wait_ge(ye_ok, at * 4 + j * 2 + 2)
                                plainly(pool)
                                pool.indirect_dma_start(acc_d, bass.IndirectOffsetOnAxis(idc[:, b, j:j + 1], 0), ye[:, j, :], None,
                                                        compute_op=ALU.add).then_inc(ye_st, 16)
                            pool.wait_ge(ye_st, at * 32 + 32)
                            pool.sem_inc(ye_free, 1)
                    pool.wait_ge(xe_in[0], 32 * (NE // 2 + 1))

                @block.tensor
                def _(pe):
                    with pe.Fori(0, NE // 2) as i:
                        for b in range(2):
                            at = i * 2 + b
                            pe.wait_ge(xe_in[b], i * 32 + 32)
                            for k2 in range(KD // 2):
                                pe.wait_ge(xe_cp, at * 4 + k2 + 1)
                                for k in (2 * k2, 2 * k2 + 1):
                                    for j in range(2):
                                        last = pe.transpose(PS[k2][:, (k % 2 * 2 + j) * P:(k % 2 * 2 + j + 1) * P], xe[:, b, j, k * P:(k + 1) * P], eye[:, :])
                                last.then_inc(xe_tr, 1)
                            pe.wait_ge(xe_cp, at * 4 + 8)
                            pe.wait_ge(wgu_in[b], i * 32 + 32)
                            for f in range(FT):
                                pe.wait_ge(hid_ok, at * FT + f + 1)
                                for g in range(2):
                                    for k in range(KD):
                                        last = pe.matmul(PS[4 + f % 2][:, g * CAP:(g + 1) * CAP], wgu[:, b, g, k, f * P:(f + 1) * P], xeT[:, k, :],
                                                         start=(k == 0), stop=(k == KD - 1))
                                last.then_inc(gu_mm, 1)
                            pe.wait_ge(gu_mm, at * FT + FT)
                            pe.sem_inc(wgu_free, 1)
                            pe.wait_ge(wd_in, at * 16 + 16)
                            pe.wait_ge(hid_ok, at * FT + FT + 2)
                            for m in range(4):
                                j, c = m // 2, m % 2
                                pe.wait_ge(ye_ok, at * 4 + m - 1) if m >= 2 else None
                                for f in range(FT):
                                    last = pe.matmul(PS[6 + c][:, :], hid[:, f, j * P:(j + 1) * P], wd[:, f, c * 512:(c + 1) * 512],
                                                     start=(f == 0), stop=(f == FT - 1))
                                last.then_inc(dn_mm, 1)
                            pe.wait_ge(dn_mm, at * 4 + 4)
                            pe.sem_inc(wd_free, 1)

                @block.scalar
                def _(act):
                    act.sem_inc(xe_cp, 4)
                    with act.Fori(0, NE // 2) as i:
                        for b in range(2):
                            at = i * 2 + b
                            for k2 in range(KD // 2):
                                act.wait_ge(xe_tr, at * 4 + k2 + 1)
                                act.activation(xeT[:, 2 * k2:2 * k2 + 2, :].rearrange("p k t -> p (k t)"), PS[k2][:, :], ACT.Copy).then_inc(xe_cp, 1)
                            for f in range(FT):
                                act.wait_ge(gu_mm, at * FT + f + 1)
                                act.wait_ge(gs_ok, at * FT + f + 1)
                                act.activation(sgm[:, f % 2, :], PS[4 + f % 2][:, 0:CAP], ACT.Sigmoid).then_inc(sg_ok, 1)

                @block.vector
                def _(dve):
                    dve.sem_inc(wgu_free, 2)
                    dve.sem_inc(wd_free, 1)
                    dve.sem_inc(ye_free, 1)
                    dve.sem_inc(hid_ok, 2)
                    dve.sem_inc(gs_ok, 2)
                    dve.tensor_copy(idc[:, 0, :], idxP[:, :, 0]).then_inc(id_ok, 1)
                    with dve.Fori(0, NE // 2) as i:
                        for b in range(2):
                            at = i * 2 + b
                            dve.wait_ge(ye_free, at + 1)
                            e = ds((at + 1) % NE, 1)
                            dve.tensor_copy(idc[:, 1 - b, :], idxP[:, :, e].rearrange("p j a -> p (j a)")).then_inc(id_ok, 1)
                            for f in range(FT):
                                dve.wait_ge(sg_ok, at * FT + f + 1)
                                dve.tensor_tensor(gm1[:, f % 2, :], sgm[:, f % 2, :], PS[4 + f % 2][:, 0:CAP], ALU.mult).then_inc(gs_ok, 1)
                                dve.wait_ge(gs_ok, at * FT + f + 3)
                                dve.tensor_tensor(hid[:, f, :], gm1[:, f % 2, :], PS[4 + f % 2][:, CAP:2 * CAP], ALU.mult).then_inc(hid_ok, 1)
                            for m in range(4):
                                j, c = m // 2, m % 2
                                dve.wait_ge(dn_mm, at * 4 + m + 1)
                                dve.tensor_scalar(ye[:, j, c * 512:(c + 1) * 512], PS[6 + c][:, :], valP[:, j, ds(at, 1)], None, ALU.mult).then_inc(ye_ok, 1)
        if stop == 15:
            return

        with ExitStack() as st:
            ac, x1b, sqf = sbt(st, "ac", [P, 2, D]), sbt(st, "x1b", [P, 2, D]), sbt(st, "sqf", [P, 2, D])
            sf = sbt(st, "sf", [P, 2, 1])
            n_in, n_m, n_a, n_sq, n_ln, n_rt, n_ok, n_st = [sem("n_in0"), sem("n_in1")], sem("n_m"), sem("n_a"), sem("n_sq"), sem("n_ln"), sem("n_rt"), sem("nf_ok"), [sem("n_st0"), sem("n_st1")]
            with nc.Block() as block:
                @block.sync
                def _(sp):
                    for b in range(2):
                        sp.sem_inc(n_st[b], 16)
                    with sp.Fori(0, TILES // 2) as i:
                        for b in range(2):
                            rows_ = ds(i * 256 + b * P, P)
                            sp.wait_ge(n_st[b], i * 16 + 16)
                            sp.dma_start(ac[:, b, :], acc_d[rows_, :]).then_inc(n_in[b], 16)
                            sp.dma_start(x1b[:, b, :], x1_d[rows_, :]).then_inc(n_in[b], 16)

                @block.vector
                def _(dve):
                    with dve.Fori(0, TILES // 2) as i:
                        for b in range(2):
                            at = i * 2 + b
                            dve.wait_ge(n_in[b], i * 32 + 32)
                            dve.tensor_tensor(ac[:, b, :], ac[:, b, :], modb[:, 3, :], ALU.mult).then_inc(n_m, 1)
                            dve.wait_ge(n_rt, at + 1)
                            dve.scalar_tensor_tensor(ac[:, b, :], x1b[:, b, :], sf[:, b, :], fgb[:, :], ALU.mult, ALU.mult).then_inc(n_ok, 1)

                @block.gpsimd
                def _(pool):
                    with pool.Fori(0, TILES // 2) as i:
                        for b in range(2):
                            pool.wait_ge(n_m, i * 2 + b + 1)
                            pool.tensor_tensor(x1b[:, b, :], x1b[:, b, :], ac[:, b, :], ALU.add).then_inc(n_a, 1)

                @block.scalar
                def _(act):
                    act.preload_act_table_set("natural_log_exp_and_others")
                    with act.Fori(0, TILES // 2) as i:
                        for b in range(2):
                            at = i * 2 + b
                            act.wait_ge(n_a, at + 1)
                            act.activation(sqf[:, b, :], x1b[:, b, :], ACT.Square, accum_out=sf[:, b, :]).then_inc(n_sq, 1)
                            act.wait_ge(n_sq, at + 1)
                            act.activation(sf[:, b, :], sf[:, b, :], ACT.Ln, bias=epst[:, 0:1], scale=1.0 / D).then_inc(n_ln, 1)
                            act.wait_ge(n_ln, at + 1)
                            act.activation(sf[:, b, :], sf[:, b, :], ACT.Exp, scale=-0.5).then_inc(n_rt, 1)
                            act.wait_ge(n_ok, at + 1)
                            act.dma_start(out[0, ds(i * 256 + b * P, P), :], ac[:, b, :]).then_inc(n_st[b], 16)
                    for b in range(2):
                        act.wait_ge(n_st[b], 16 * (TILES // 2 + 1))


_INS = ["x", "c", "ctx", "c_ctx", "ada_w", "ada_b", "norm1_g", "norm2_g", "w_in", "dn_conv_w", "dn_a_log", "dn_dt_bias",
        "dn_norm_g", "hy_conv_w", "hy_conv_b", "hy_w1", "hy_b1", "hy_w2", "hy_b2", "hy_w3", "hy_freq", "hy_d_bias",
        "sc_conv_w", "w_branch_a", "w_branch_b", "w_branch_c", "w_out", "router_w", "exp_w_gate", "exp_w_up",
        "exp_w_down", "final_norm_g"]


def kernel(**inputs):
    import concourse.bacc as bacc
    from concourse.bass_utils import run_bass_kernel_spmd

    nc = bacc.Bacc("TRN2", target_bir_lowering=False, num_devices=1)
    given = {n: np.ascontiguousarray(inputs[n]) for n in _INS}
    given.update(shape_tables())
    A = {n: nc.dram_tensor(f"in_{n}", a.shape, F32, kind="ExternalInput").ap() for n, a in given.items()}
    out = nc.dram_tensor("out_x", (1, SEQ, D), F32, kind="ExternalOutput").ap()
    build(nc, A, out)
    r = run_bass_kernel_spmd(nc, [{f"in_{n}": a for n, a in given.items()}], core_ids=[0])
    return r.results[0]["out_x"]
```

```python
import math
from contextlib import ExitStack

import numpy as np
import concourse.bass as bass
from concourse import mybir

F32 = mybir.dt.float32
U32 = mybir.dt.uint32
ALU = mybir.AluOpType
ACT = mybir.ActivationFunctionType
AXX = mybir.AxisListType.X
ds = bass.ds

P = 128
D = 1024
KD = D // P
SEQ, CTX = 2048, 256
TOK = CTX + SEQ
TW = 512
NT = SEQ // TW
GRID_W = 64
HEADS, HD = 4, 128
DNW = HEADS * HD
A_COLS = 4 * DNW + 4 * HEADS
HW = 256
B_OFF = A_COLS
C_OFF = B_OFF + 3 * HW
G_OFF = C_OFF + 3 * HW
NCH = 20
STEPS = (CTX + SEQ) // P
FN = 64
FK = FN // 2 + 1
FR = SEQ // FN
NB = P // FR
NE, CAP, FF = 16, 256, 768
FT = FF // P
EPS = 1e-6
LEVELS = [2, 4, 8, 16, 32, 64]
CLAMP = -44.0

R_C, R_CC, R_ADAB, R_N1, R_NG = 0, 8, 16, 32, 40
R_HYW, R_HYB, R_SCW, R_HYD, R_DNW, R_MLP = 41, 59, 65, 71, 73, 109
N_ROWS = 112


def shape_tables():
    i = np.arange(P)
    r, c = i[:, None], i[None, :]
    ui, li, su, sl = r <= c, r >= c, r < c, r > c
    tri = np.stack([ui, li, su, sl], 1).astype(np.float32)
    m = (r // 2 == c // 2) & (r % 2 < 1) & (c % 2 >= 1)
    pair = np.stack([m, m.T], 1).astype(np.float32)
    lv = []
    j = np.arange(P // 2)[None, :]
    for b in LEVELS:
        for d in range(2):
            lv.append((r // (2 * b) == j // b) & ((r % (2 * b) >= b) == (d == 0)))
    lv = np.stack(lv, 1).astype(np.float32)
    n = FN * FN
    w = lambda e: np.exp(-2j * np.pi * (e % n) / n)
    n1, n2, k1 = np.arange(FR), np.arange(FN), np.arange(FK)
    a = w((k1[None, None, :] * (FN * n1[:, None, None] + n2[None, :, None])))
    fa1 = np.concatenate([a.real, a.imag], 2).reshape(FR, FN // NB, NB, 2 * FK)
    fa = np.zeros((NB, FR, FN // NB, NB, 2 * FK))
    for j in range(NB):
        fa[j, :, :, j] = fa1[:, :, j]
    fa = fa.reshape(P, FN // NB, NB, 2 * FK)
    k2 = np.arange(FN)
    g = w(FN * n2[:, None] * k2[None, :])
    gr, gi = g.real, g.imag
    top = lambda x, y: np.concatenate([np.concatenate(x, 1), np.concatenate(y, 1)], 0)
    g_z = top([gr, gi], [-gi, gr])
    g_zs = top([gi, gr], [gr, -gi])
    f_rr = top([gr, gr], [-gi, -gi])
    b_rr = f_rr
    f_ii = top([-gi, gi], [-gr, gr])
    b_ii = -f_ii
    ginv = top([gr, -gi], [gi, gr])
    gm = np.stack([g_z, g_zs, f_rr, b_rr, f_ii, b_ii, ginv], 1)
    ginv = np.conj(g.T)
    inv = np.concatenate([np.concatenate([ginv.real, ginv.imag], 1),
                          np.concatenate([-ginv.imag, ginv.real], 1)], 0)
    gm[:, 6] = inv
    wt = np.where((k1 == 0) | (k1 == FN // 2), 1.0, 2.0) / n
    dd = np.conj(a).transpose(2, 1, 0) * wt[:, None, None]
    fd = np.concatenate([dd.real, -dd.imag], 0)
    pos = np.arange(SEQ, dtype=np.float64)
    t = pos / (SEQ - 1)
    bands = np.linspace(1e-4, 15, 16)
    ang = (2.0 * math.pi / SEQ) * pos[:, None] * bands
    feats = np.concatenate([t[:, None], np.cos(ang), -np.sin(ang)], 1).T
    deltas = np.abs(np.linspace(math.log(1e-2) / 1.5, math.log(1e-2) / 0.3, HW))
    win = np.exp(-t[:, None] * deltas)
    win2 = np.concatenate([win, win], 1)
    win2[0, HW:] = 0.0
    f = lambda x: np.ascontiguousarray(x, dtype=np.float32)
    return {"t_tri": f(tri), "t_lv": f(lv), "t_pair": f(pair), "t_eye": f(np.eye(P)), "t_fa": f(fa), "t_g": f(gm),
            "t_fd": f(fd), "t_feat": f(feats), "t_win": f(win2)}


def build(nc, A, out, stop=99):
    scr = lambda name, shape: nc.dram_tensor(name, shape, F32).ap()
    sz_d = scr("sz_d", (16, P, HEADS, P))
    kT_d, qT_d, kN_d, vN_d = [scr(n, (NCH, P, HEADS, P)) for n in ("kT_d", "qT_d", "kN_d", "vN_d")]
    o_d = [scr(n, (NCH, P, HEADS, P)) for n in ("of_d", "ob_d")]
    z_d, y_d = scr("z_d", (SEQ, HW)), scr("y_d", (SEQ, HW))
    h_d = scr("h_d", (SEQ, 2 * HW))
    fa_d = scr("fa_d", (3, 2, FK, FN, HW))
    fb_d = scr("fb_d", (2, FN, FK, HW))
    mg_d = scr("mg_d", (KD, P, SEQ))
    x1_d, h2_d = scr("x1_d", (SEQ, D)), scr("h2_d", (SEQ, D))

    with ExitStack() as top:
        used = []

        def sem(name):
            used.append(nc.alloc_semaphore(name))
            return used[-1]

        def recycle():
            nc.clear_and_free_semaphores(list(used))
            nc.all_engine_barrier()
            used.clear()

        def sbt(stack, name, shape, dt=F32):
            return stack.enter_context(nc.sbuf_tensor(name, shape, dt))

        PS = [top.enter_context(nc.psum_tensor(f"bank{i}", [P, 512], F32)) for i in range(8)]
        settled = top.enter_context(nc.semaphore("settled"))

        def plainly(eng):
            eng.sem_inc(settled, 1)

        eye = sbt(top, "eye", [P, P])
        ones = sbt(top, "ones", [P, P])
        epst = sbt(top, "epst", [P, 1])
        cols = sbt(top, "cols", [P, N_ROWS])
        modb = sbt(top, "modb", [P, 4, D])
        sh1 = sbt(top, "sh1", [P, KD, 2])
        gain1 = sbt(top, "gain1", [P, KD, 2])

        with ExitStack() as st:
            rows = sbt(st, "rows", [P, P])
            small = sbt(st, "small", [P, 16])
            csil = sbt(st, "csil", [P, 2, KD])
            csilb = sbt(st, "csilb", [P, KD, P])
            ada = sbt(st, "ada", [P, 4, KD, 512])
            n2g = sbt(st, "n2g", [P, D])
            rows_zero, rows_in, rows_T = sem("rows_zero"), sem("rows_in"), sem("rows_T")
            bcast_in, ada_in, ada_free = sem("bcast_in"), [sem(f"ada_in{b}") for b in range(4)], sem("ada_free")
            a_chain, v_chain = sem("a_chain_m"), sem("v_chain_m")
            cols_ok, sil_e, sil_ok = sem("cols_ok"), sem("sil_e"), sem("sil_ok")
            mod_mm, mod_ev = sem("mod_mm"), sem("mod_ev")
            feat, hw, win = sbt(st, "feat", [33, 2, TW]), sbt(st, "hw", [P, 2, 4, TW]), sbt(st, "win", [P, 2, 4, TW])
            w1, w2, w3 = sbt(st, "w1", [33, 64]), sbt(st, "w2", [64, 64]), sbt(st, "w3", [64, 2 * HW])
            arg, turns, hid = sbt(st, "arg", [64, TW]), sbt(st, "turns", [64, TW]), sbt(st, "hid", [64, 2, TW])
            mw_in, f_in, f_st, hw_free = sem("mw_in"), [sem("f_in0"), sem("f_in1")], [sem("f_st0"), sem("f_st1")], sem("hw_free")
            l_mm, l_arg, l_sin, l3_mm, l3_ok, f_ch = sem("l_mm"), sem("l_arg"), sem("l_sin"), sem("l3_mm"), sem("l3_ok"), sem("f_ch")
            L3 = [PS[6], PS[7], PS[0], PS[4]]
            MAGIC = 1.5 * 2 ** 23
            PI2_HI = 6.28125
            PI2_LO = 2 * math.pi - PI2_HI
            STEPS_SIN = 6
            with nc.Block() as block:
                @block.sync
                def _(sp):
                    sp.dma_start(eye[:, :], A["t_eye"]).then_inc(rows_in, 16)
                    sp.wait_ge(rows_zero, 2)
                    k8 = lambda v: v.rearrange("(k p) -> k p", p=P)
                    parts = [(R_C, k8(A["c"][0, :])), (R_CC, k8(A["c_ctx"])), (R_ADAB, k8(A["ada_b"][0, 0:2 * D])),
                             (R_N1, k8(A["norm1_g"][0, :])), (R_NG, A["dn_norm_g"]),
                             (R_HYW, A["hy_conv_w"][0].rearrange("j (k p) -> (j k) p", p=P)),
                             (R_HYB, k8(A["hy_conv_b"][0, :])),
                             (R_SCW, A["sc_conv_w"][0].rearrange("j (k p) -> (j k) p", p=P)),
                             (R_HYD, k8(A["hy_d_bias"][0, :])),
                             (R_DNW, A["dn_conv_w"][0].rearrange("j (k p) -> (j k) p", p=P))]
                    for r, src in parts:
                        sp.dma_start(rows[r:r + src.shape[0], :], src).then_inc(rows_in, 16)
                    for r, name in enumerate(("hy_freq", "hy_b1", "hy_b2")):
                        sp.dma_start(rows[R_MLP + r:R_MLP + r + 1, 0:64], A[name]).then_inc(rows_in, 16)
                    sp.dma_start(modb[:, :, :].rearrange("p a b -> p (a b)"),
                                 A["ada_b"][:, 2 * D:6 * D].to_broadcast([P, 4 * D])).then_inc(bcast_in, 16)
                    sp.dma_start(n2g[:, :], A["norm2_g"].to_broadcast([P, D])).then_inc(bcast_in, 16)
                    with sp.Fori(0, 3) as i:
                        for b in range(4):
                            sp.wait_ge(ada_free, i * 4 + b + 1)
                            sp.dma_start(ada[:, b, :, :], A["ada_w"][0, :, ds(i * 2048 + b * 512, 512)]
                                         .rearrange("(k p) c -> p k c", p=P)).then_inc(ada_in[b], 16)

                @block.gpsimd
                def _(pool):
                    pool.memset(rows[:, :], 0.0).then_inc(rows_zero, 1)
                    pool.memset(ones[:, :], 1.0).then_inc(rows_zero, 1)
                    pool.memset(epst[:, :], EPS)
                    for buf, name in ((w1, "hy_w1"), (w2, "hy_w2"), (w3, "hy_w3")):
                        pool.dma_start(buf[:, :], A[name][0]).then_inc(mw_in, 16)

                    def load(u, v):
                        pool.dma_start(feat[:, v, :], A["t_feat"][:, ds(u * TW, TW)]).then_inc(f_in[v], 16)
                        pool.dma_start(win[:, v], A["t_win"][ds(u * TW, TW), :].rearrange("(j p) c -> p j c", p=P)).then_inc(f_in[v], 16)

                    for v in range(2):
                        load(v, v)
                    with pool.Fori(0, NT // 2) as i:
                        for v in range(2):
                            pool.wait_ge(l3_ok, i * 8 + v * 4 + 8)
                            pool.dma_start(h_d[ds(i * (2 * TW) + v * TW, TW), :].rearrange("(j p) c -> p j c", p=P), hw[:, v]).then_inc(f_st[v], 16)
                            load((i * 2 + v + 2) % NT, v)
                            pool.wait_ge(f_st[v], i * 16 + 16)
                            pool.sem_inc(hw_free, 1)
                    for v in range(2):
                        pool.wait_ge(f_in[v], 32 * (NT // 2 + 1))

                @block.scalar
                def _(act):
                    act.wait_ge(cols_ok, 2)
                    act.activation(small[:, :], small[:, :], ACT.Exp, scale=-1.0).then_inc(sil_e, 1)
                    with act.Fori(0, NT // 2) as i:
                        for v in range(2):
                            for l in range(2):
                                act.wait_ge(l_arg, i * 4 + v * 2 + l + 1)
                                act.activation(hid[:, l, :], arg[:, :], ACT.Sin).then_inc(l_sin, 1)

                @block.vector
                def _(dve):
                    n = [0]

                    def link(ins):
                        n[0] += 1
                        ins.then_inc(v_chain, 1)
                        dve.wait_ge(v_chain, n[0])

                    dve.sem_inc(ada_free, 4)
                    dve.wait_ge(rows_T, 1)
                    dve.tensor_copy(cols[:, :], PS[0][:, 0:N_ROWS]).then_inc(cols_ok, 1)
                    dve.tensor_scalar_max(small[:, :], PS[0][:, 0:16], CLAMP).then_inc(cols_ok, 1)
                    dve.wait_ge(sil_e, 1)
                    link(dve.tensor_scalar_add(small[:, :], small[:, :], 1.0))
                    link(dve.reciprocal(small[:, :], small[:, :]))
                    link(dve.tensor_tensor(csil[:, :, :].rearrange("p a b -> p (a b)"), small[:, :], cols[:, 0:16], ALU.mult))
                    dve.tensor_copy(csilb[:, :, :], csil[:, 0, :].unsqueeze(2).to_broadcast([P, KD, P])).then_inc(sil_ok, 1)
                    dve.wait_ge(bcast_in, 32)
                    mb = modb[:, :, :].rearrange("p a b -> p (a b)")

                    def layer(i, v, l):
                        at = lambda n: i * 4 * STEPS_SIN + (v * 2 + l) * STEPS_SIN + n
                        dve.wait_ge(l_mm, i * 4 + v * 2 + l + 1)
                        dve.tensor_scalar(arg[:, :], PS[4 + l][0:64, :], cols[0:64, R_MLP + 1 + l:R_MLP + 2 + l],
                                          cols[0:64, R_MLP:R_MLP + 1], ALU.add, ALU.mult).then_inc(f_ch, 1)
                        dve.wait_ge(f_ch, at(1))
                        dve.tensor_scalar(turns[:, :], arg[:, :], 1 / (2 * math.pi), MAGIC, ALU.mult, ALU.add).then_inc(f_ch, 1)
                        dve.wait_ge(f_ch, at(2))
                        dve.tensor_scalar(turns[:, :], turns[:, :], -MAGIC, None, ALU.add).then_inc(f_ch, 1)
                        dve.wait_ge(f_ch, at(3))
                        dve.scalar_tensor_tensor(arg[:, :], turns[:, :], -PI2_HI, arg[:, :], ALU.mult, ALU.add).then_inc(f_ch, 1)
                        dve.wait_ge(f_ch, at(4))
                        dve.scalar_tensor_tensor(arg[:, :], turns[:, :], -PI2_LO, arg[:, :], ALU.mult, ALU.add).then_inc(f_ch, 1)
                        dve.wait_ge(f_ch, at(5))
                        dve.tensor_scalar(arg[:, :], arg[:, :], 3.1415925, -3.1415925, ALU.min, ALU.max).then_inc(f_ch, 1)
                        dve.wait_ge(f_ch, at(6))
                        dve.sem_inc(l_arg, 1)

                    dve.sem_inc(hw_free, 2)
                    dve.sem_inc(l3_ok, 4)
                    with dve.Fori(0, 2) as i:
                        for c in range(4):
                            v, l = c // 2, c % 2
                            layer(i, v, l)
                            dve.wait_ge(mod_mm, i * 4 + c + 5)
                            dst = mb[:, ds(i * 2048 + c * 512, 512)]
                            dve.tensor_tensor(dst, PS[2 + c % 2][:, :], dst, ALU.add).then_inc(mod_ev, 1)
                            if l == 1:
                                dve.wait_ge(hw_free, i * 2 + v + 1)
                                for j in range(4):
                                    dve.wait_ge(l3_mm, i * 8 + v * 4 + j + 1)
                                    dve.tensor_tensor(hw[:, v, j, :], L3[j][:, :], win[:, v, j, :], ALU.mult).then_inc(l3_ok, 1)
                    dve.wait_ge(mod_ev, 8)
                    link(dve.scalar_tensor_tensor(modb[:, 2, :], modb[:, 2, :], 1.0, n2g[:, :], ALU.add, ALU.mult))
                    m1 = PS[1][:, 0:32].rearrange("p (m s) -> p m s", s=2)
                    bias = cols[:, R_ADAB:R_ADAB + 16].unsqueeze(2).to_broadcast([P, 16, 2])
                    n1 = cols[:, R_N1:R_N1 + KD].unsqueeze(2).to_broadcast([P, KD, 2])
                    link(dve.tensor_tensor(sh1[:, :, :], m1[:, 0:8, :], bias[:, 0:8, :], ALU.add))
                    link(dve.tensor_tensor(gain1[:, :, :], m1[:, 8:16, :], bias[:, 8:16, :], ALU.add))
                    link(dve.scalar_tensor_tensor(gain1[:, :, :], gain1[:, :, :], 1.0, n1, ALU.add, ALU.mult))

                @block.tensor
                def _(pe):
                    pe.wait_ge(rows_in, 14 * 16)
                    pe.transpose(PS[0][:, 0:N_ROWS], rows[0:N_ROWS, :], eye[0:N_ROWS, 0:N_ROWS]).then_inc(rows_T, 1)
                    pe.wait_ge(sil_ok, 1)
                    for b in range(4):
                        pe.wait_ge(ada_in[b], 16)
                        for m in range(4):
                            for k in range(KD):
                                last = pe.matmul(PS[1][:, b * 8 + m * 2:b * 8 + m * 2 + 2],
                                                 ada[:, b, k, m * P:(m + 1) * P], csil[:, :, k],
                                                 start=(k == 0), stop=(k == KD - 1))
                        last.then_inc(mod_mm, 1)
                        pe.wait_ge(mod_mm, b + 1)
                        pe.sem_inc(ada_free, 1)
                    pe.wait_ge(mw_in, 48)
                    with pe.Fori(0, 2) as i:
                        for c in range(4):
                            b, v, l = c % 2, c // 2, c % 2
                            if l == 0:
                                pe.wait_ge(f_in[v], i * 32 + 32)
                                pe.wait_ge(l3_ok, i * 8 + v * 4 + 4)
                                plainly(pe)
                                pe.matmul(PS[4][0:64, :], w1[:, :], feat[:, v, :], start=True, stop=True).then_inc(l_mm, 1)
                            else:
                                pe.wait_ge(l_sin, i * 4 + v * 2 + 1)
                                plainly(pe)
                                pe.matmul(PS[5][0:64, :], w2[:, :], hid[:, 0, :], start=True, stop=True).then_inc(l_mm, 1)
                            pe.wait_ge(ada_in[c], i * 16 + 32)
                            if b == 0:
                                pe.wait_ge(mod_mm, i * 4 + c + 4)
                            for k in range(KD):
                                last = pe.matmul(PS[2 + b][:, :], csilb[:, k, :], ada[:, c, k, :],
                                                 start=(k == 0), stop=(k == KD - 1))
                            last.then_inc(mod_mm, 1)
                            if l == 1:
                                pe.wait_ge(l_sin, i * 4 + v * 2 + 2)
                                for j in range(4):
                                    pe.matmul(L3[j][:, :], hid[:, 1, j * P:(j + 1) * P], w3[:, :], start=True, stop=True).then_inc(l3_mm, 1)
                            pe.wait_ge(mod_mm, i * 4 + c + 5)
                            pe.wait_ge(mod_ev, i * 4 + c + 1)
                            pe.sem_inc(ada_free, 1)
        if stop == 1:
            return
        PH = top.enter_context(ExitStack())
        hT = sbt(PH, "hT", [P, KD, TOK])

        with ExitStack() as st:
            xb = sbt(st, "xb", [P, 2, 4, D])
            sq = sbt(st, "sq", [P, 4, D])
            ss = sbt(st, "ss", [P, 2, 4])
            x_in, x_free = [sem("x_in0"), sem("x_in1")], sem("x_free")
            ss_ok, rstd_ok, xn_ok = sem("ss_ok"), sem("rstd_ok"), sem("xn_ok")
            xT_mm, xT_ev, a_ch, l_ok, e_ok = sem("xT_mm"), sem("xT_ev"), sem("a_ch_b"), sem("l_ok_b"), sem("e_ok_b")
            with nc.Block() as block:
                @block.sync
                def _(sp):
                    sp.dma_start(xb[:, 1, 0:2, :], A["ctx"][0].rearrange("(j p) c -> p j c", p=P)).then_inc(x_in[1], 16)
                    with sp.Fori(0, 2) as i:
                        for b in range(2):
                            sp.wait_ge(x_free, i * 2 + b + 1)
                            sp.dma_start(xb[:, b, :, :], A["x"][0, ds(i * 1024 + b * 512, 512), :]
                                         .rearrange("(j p) c -> p j c", p=P)).then_inc(x_in[b], 16)

                @block.scalar
                def _(act):
                    def group(b, tiles, g, loads):
                        act.wait_ge(x_in[b], loads)
                        act.wait_ge(xn_ok, g + 1)
                        for j in range(tiles):
                            act.activation(sq[:, j, :], xb[:, b, j, :], ACT.Square,
                                           accum_out=ss[:, b, j:j + 1]).then_inc(ss_ok, 1)
                        return None

                    def root(b, tiles, g, squares):
                        act.wait_ge(ss_ok, squares)
                        act.wait_ge(l_ok, g + 1)
                        act.activation(ss[:, b, 0:tiles], ss[:, b, 0:tiles], ACT.Ln).then_inc(e_ok, 1)
                        act.wait_ge(e_ok, g + 1)
                        act.activation(ss[:, b, 0:tiles], ss[:, b, 0:tiles], ACT.Exp, scale=-0.5).then_inc(rstd_ok, 1)

                    group(1, 2, 0, 16)
                    root(1, 2, 0, 2)
                    with act.Fori(0, 2) as i:
                        for b in range(2):
                            group(b, 4, i * 2 + b + 1, i * 16 + b * 16 + 16)
                            root(b, 4, i * 2 + b + 1, i * 8 + b * 4 + 6)

                @block.vector
                def _(dve):
                    dve.sem_inc(xn_ok, 1)
                    dve.sem_inc(x_free, 1)
                    dve.sem_inc(xT_ev, 4)

                    def group(b, tiles, g, squares, off, s):
                        dve.wait_ge(ss_ok, squares)
                        dve.tensor_scalar(ss[:, b, 0:tiles], ss[:, b, 0:tiles], 1.0 / D, EPS, ALU.mult, ALU.add).then_inc(l_ok, 1)
                        dve.wait_ge(rstd_ok, g + 1)
                        for j in range(tiles):
                            last = dve.tensor_scalar(xb[:, b, j, :], xb[:, b, j, :], ss[:, b, j:j + 1], None, ALU.mult)
                        last.then_inc(xn_ok, 1)
                        for k in range(KD):
                            dve.wait_ge(xT_mm, g * 8 + k + 1)
                            dve.tensor_scalar(hT[:, k, ds(off, tiles * P)], PS[k % 4][:, 0:tiles * P],
                                              gain1[:, k, s:s + 1], sh1[:, k, s:s + 1], ALU.mult, ALU.add).then_inc(xT_ev, 1)

                    group(1, 2, 0, 2, 0, 1)
                    with dve.Fori(0, 2) as i:
                        for b in range(2):
                            group(b, 4, i * 2 + b + 1, i * 8 + b * 4 + 6, i * 1024 + b * 512 + CTX, 0)

                @block.tensor
                def _(pe):
                    def group(b, tiles, g):
                        pe.wait_ge(xn_ok, g + 2)
                        for k in range(KD):
                            pe.wait_ge(xT_ev, g * 8 + k + 1)
                            for j in range(tiles):
                                last = pe.transpose(PS[k % 4][:, j * P:(j + 1) * P], xb[:, b, j, k * P:(k + 1) * P], eye[:, :])
                            last.then_inc(xT_mm, 1)
                        pe.wait_ge(xT_mm, g * 8 + 8)
                        pe.sem_inc(x_free, 1)

                    group(1, 2, 0)
                    with pe.Fori(0, 2) as i:
                        for b in range(2):
                            group(b, 4, i * 2 + b + 1)
        if stop == 2:
            return

        gst = top.enter_context(ExitStack())
        g_all = sbt(gst, "g_all", [P, NCH, 8])
        beta = sbt(gst, "beta", [P, NCH, 8])
        egc = sbt(gst, "egc", [P, NCH, 8])
        erest = sbt(gst, "erest", [P, NCH, 8])
        etot = sbt(gst, "etot", [P, NCH, 8])
        tri = sbt(gst, "tri", [P, 4, P])
        UI, LI, SU, SL = range(4)

        NU = 19
        units = [(kind, n) for kind in range(3) for n in range(5)] + [(3, n) for n in range(1, 5)]
        width = lambda n: CTX if n == 0 else TW
        toff = lambda n: 0 if n == 0 else CTX + (n - 1) * TW
        with ExitStack() as st:
            wq = sbt(st, "wq", [P, 4, KD, P])
            tmp = sbt(st, "tmp", [P, 4, TW])
            sg = sbt(st, "sg", [P, 4, TW])
            yb = sbt(st, "yb", [P, 4, TW])
            s2 = sbt(st, "s2", [P, 4, TW])
            nat = sbt(st, "nat", [P, 4, TW])
            w_in_ok, w_free = [sem(f"w_ok{k}") for k in range(4)], sem("w_free_c")
            mm_ok, ps_free = sem("mm_ok_c"), sem("ps_free_c")
            conv1, conv2, conv3 = sem("conv1"), sem("conv2"), sem("conv3")
            clamp_ok, sig1, sig2, sig3 = sem("clamp_ok"), sem("sig1"), sem("sig2"), sem("sig3")
            y_ok, sq_ok, sum_mm, rn1, rn2 = sem("y_ok"), sem("sq_ok"), sem("sum_mm"), sem("rn1"), sem("rn2")
            yn_ok, tr_mm, nat_ok = sem("yn_ok"), sem("tr_mm"), sem("nat_ok")
            unit_st, unit_done = [sem("unit_st0"), sem("unit_st1")], sem("unit_done")
            def back(u):
                return u - 3 if u >= 4 else min(u - 2, 0)

            with nc.Block() as block:
                @block.sync
                def _(sp):
                    with sp.Fori(0, HEADS) as h:
                        for kind in range(4):
                            sp.wait_ge(w_free, h * 4 + kind + 1)
                            sp.dma_start(wq[:, kind, :, :], A["w_in"][0, :, ds(h * P + kind * DNW, P)]
                                         .rearrange("(k p) c -> p k c", p=P)).then_inc(w_in_ok[kind], 16)

                @block.tensor
                def _(pe):
                    def project(h, u):
                        kind, n = units[u]
                        if u % 5 == 0:
                            pe.wait_ge(w_in_ok[kind], h * 16 + 16)
                        pe.wait_ge(ps_free, h * NU + back(u) + 3)
                        for k in range(KD):
                            last = pe.matmul(PS[u % 4][:, 0:width(n)], wq[:, kind, k, :],
                                             hT[:, k, toff(n):toff(n) + width(n)], start=(k == 0), stop=(k == KD - 1))
                        last.then_inc(mm_ok, 1)
                        if n == 4:
                            pe.wait_ge(mm_ok, h * NU + u + 1)
                            pe.sem_inc(w_free, 1)

                    def norm_sum(h, u):
                        w = width(units[u][1])
                        pe.wait_ge(sq_ok, h * 10 + u + 1)
                        pe.wait_ge(rn1, h * 10 + u + 1)
                        pe.matmul(PS[4 + u % 2][:, 0:w], ones[:, :], s2[:, u % 4, 0:w], start=True, stop=True).then_inc(sum_mm, 1)

                    def turn(h, u):
                        n = units[u][1]
                        if u < 10:
                            pe.wait_ge(yn_ok, h * 10 + u + 1)
                        else:
                            pe.wait_ge(y_ok, h * NU + u + 1)
                        pe.wait_ge(nat_ok, h * 10 + u - 5 + 1)
                        for j in range(width(n) // P):
                            last = pe.transpose(PS[6 + u % 2][:, j * P:(j + 1) * P], yb[:, u % 4, j * P:(j + 1) * P], eye[:, :])
                        last.then_inc(tr_mm, 1)

                    with pe.Fori(0, HEADS) as h:
                        for u in range(NU + 2):
                            if u < NU:
                                project(h, u)
                            if 1 <= u < 11:
                                norm_sum(h, u - 1)
                            if 7 <= u < 17:
                                turn(h, u - 2)

                @block.scalar
                def _(act):
                    act.preload_act_table_set("natural_log_exp_and_others")
                    act.sem_inc(rn1, 2)
                    act.sem_inc(nat_ok, 2)

                    def centre(h, u):
                        kind, n = units[u]
                        w = width(n)
                        act.wait_ge(mm_ok, h * NU + u + 1)
                        act.wait_ge(unit_done, h * NU + back(u) + 3)
                        plainly(act)
                        if kind < 3:
                            act.activation(tmp[:, u % 4, 0:w], PS[u % 4][:, 0:w], ACT.Copy,
                                           scale=cols[:, ds(h + R_DNW + 12 + kind * 4, 1)]).then_inc(conv1, 1)
                        else:
                            act.activation(tmp[:, u % 4, 0:w], PS[u % 4][:, 0:w], ACT.Copy).then_inc(conv1, 1)

                    def logistic(h, u):
                        w = width(units[u][1])
                        s = sg[:, u % 4, 0:w]
                        at = h * NU + u + 1
                        act.wait_ge(clamp_ok, at)
                        act.activation(s, s, ACT.Exp, scale=-1.0).then_inc(sig1, 1)
                        act.wait_ge(sig1, at)
                        act.activation(s, s, ACT.Ln, bias=1.0).then_inc(sig2, 1)
                        act.wait_ge(sig2, at)
                        act.activation(s, s, ACT.Exp, scale=-1.0).then_inc(sig3, 1)

                    def square(h, u):
                        w = width(units[u][1])
                        act.wait_ge(y_ok, h * NU + u + 1)
                        act.activation(s2[:, u % 4, 0:w], yb[:, u % 4, 0:w], ACT.Square).then_inc(sq_ok, 1)

                    def root(h, u):
                        w = width(units[u][1])
                        at = h * 10 + u + 1
                        act.wait_ge(sum_mm, at)
                        act.activation(s2[:, u % 4, 0:w], PS[4 + u % 2][:, 0:w], ACT.Ln, bias=epst[:, 0:1]).then_inc(rn1, 1)
                        act.wait_ge(rn1, at + 2)
                        act.activation(s2[:, u % 4, 0:w], s2[:, u % 4, 0:w], ACT.Exp, scale=-0.5).then_inc(rn2, 1)

                    def to_nat(h, u):
                        w = width(units[u][1])
                        act.wait_ge(tr_mm, h * 10 + u - 5 + 1)
                        act.activation(nat[:, u % 4, 0:w], PS[6 + u % 2][:, 0:w], ACT.Copy).then_inc(nat_ok, 1)

                    with act.Fori(0, HEADS) as h:
                        for u in range(NU + 2):
                            if u < NU:
                                centre(h, u)
                                logistic(h, u)
                                if u < 10:
                                    square(h, u)
                            if 1 <= u < 11:
                                root(h, u - 1)
                            if 7 <= u < 17:
                                to_nat(h, u - 2)

                @block.gpsimd
                def _(pool):
                    def clamp(h, u):
                        w = width(units[u][1])
                        pool.wait_ge(conv3, h * NU + u + 1)
                        plainly(pool)
                        pool.tensor_scalar_max(sg[:, u % 4, 0:w], tmp[:, u % 4, 0:w], CLAMP).then_inc(clamp_ok, 1)

                    def store(h, u):
                        kind, n = units[u]
                        w = width(n)
                        chunks = w // P
                        places = [0, 18] if n == 0 else [2 + (n - 1) * 4]
                        ready = []
                        if kind in (0, 1):
                            pool.wait_ge(yn_ok, h * 10 + u + 1)
                            ready.append((yb, (qT_d, kT_d)[kind]))
                        if kind in (1, 2):
                            pool.wait_ge(nat_ok, h * 10 + u - 5 + 3)
                            ready.append((nat, (None, kN_d, vN_d)[kind]))
                        if kind == 3:
                            pool.wait_ge(y_ok, h * NU + u + 1)
                            ready.append((yb, sz_d))
                            places = [(n - 1) * 4]
                        plainly(pool)
                        for src, dst in ready:
                            for c in places:
                                pool.dma_start(dst[c:c + chunks, :, ds(h, 1), :].rearrange("c p a t -> p c (a t)"),
                                               src[:, u % 4, 0:w].rearrange("p (c t) -> p c t", t=P)).then_inc(unit_st[u % 2], 16)

                    pool.sem_inc(unit_done, 3)
                    per_unit = []
                    for u in range(NU):
                        kind, n = units[u]
                        per_unit.append(16 * (2 if kind == 1 else 1) * (2 if n == 0 else 1))
                    with pool.Fori(0, HEADS) as h:
                        for u in range(NU + 4):
                            if 4 <= u:
                                pool.wait_ge(unit_st[u % 2], h * sum(per_unit[u % 2::2]) + sum(per_unit[u % 2:u - 3:2]))
                                pool.sem_inc(unit_done, 1)
                            if u < NU:
                                clamp(h, u)
                            if 3 <= u < NU + 3:
                                store(h, u - 3)

                @block.vector
                def _(dve):
                    dve.sem_inc(w_free, 4)
                    dve.sem_inc(ps_free, 3)

                    def conv(h, u):
                        kind, n = units[u]
                        w = width(n)
                        row = CTX if n == 0 else GRID_W
                        p = PS[u % 4][:, 0:w].rearrange("p (r c) -> p r c", c=row)
                        t = tmp[:, u % 4, 0:w].rearrange("p (r c) -> p r c", c=row)
                        at = h * NU + u + 1
                        dve.wait_ge(conv1, at)
                        if kind == 3:
                            dve.sem_inc(ps_free, 1)
                            dve.sem_inc(conv2, 1)
                            dve.sem_inc(conv3, 1)
                            return
                        tap = lambda j: cols[:, ds(h + R_DNW + 12 * j + kind * 4, 1)]
                        dve.scalar_tensor_tensor(t[:, :, 1:row], p[:, :, 0:row - 1], tap(0), t[:, :, 1:row],
                                                 ALU.mult, ALU.add).then_inc(conv2, 1)
                        dve.wait_ge(conv2, at)
                        dve.scalar_tensor_tensor(t[:, :, 0:row - 1], p[:, :, 1:row], tap(2), t[:, :, 0:row - 1],
                                                 ALU.mult, ALU.add).then_inc(conv3, 1)
                        dve.wait_ge(conv3, at)
                        dve.sem_inc(ps_free, 1)

                    def silu(h, u):
                        w = width(units[u][1])
                        dve.wait_ge(sig3, h * NU + u + 1)
                        dve.tensor_tensor(yb[:, u % 4, 0:w], tmp[:, u % 4, 0:w], sg[:, u % 4, 0:w], ALU.mult).then_inc(y_ok, 1)

                    def normed(h, u):
                        w = width(units[u][1])
                        scale = HD ** -0.5 if units[u][0] == 0 else 1.0
                        dve.wait_ge(rn2, h * 10 + u + 1)
                        dve.scalar_tensor_tensor(yb[:, u % 4, 0:w], yb[:, u % 4, 0:w], scale, s2[:, u % 4, 0:w],
                                                 ALU.mult, ALU.mult).then_inc(yn_ok, 1)

                    with dve.Fori(0, HEADS) as h:
                        for u in range(NU + 1):
                            if u < NU:
                                conv(h, u)
                                silu(h, u)
                            if 1 <= u < 11:
                                normed(h, u - 1)
        if stop == 3:
            return

        with ExitStack() as st:
            wg = sbt(st, "wg", [P, KD, 16])
            gT = sbt(st, "gT", [16, TOK])
            gl = sbt(st, "gl", [P, NCH, 16])
            dtb, alog = sbt(st, "dtb", [P, 8]), sbt(st, "alog", [P, 8])
            gx, ge, gt = [sbt(st, n, [P, NCH, 8]) for n in ("gx", "ge", "gt")]
            gw_in, gates_mm, gates_T, gates_tr = sem("gw_in"), sem("gates_mm"), sem("gates_T"), sem("gates_tr")
            gd, ga, sums_mm, sums_ok = sem("gd"), sem("ga"), sem("sums_mm"), sem("sums_ok")
            GD_DONE = 22
            with nc.Block() as block:
                @block.sync
                def _(sp):
                    sp.dma_start(wg[:, :, :], A["w_in"][0, :, 4 * DNW:A_COLS].rearrange("(k p) c -> p k c", p=P)).then_inc(gw_in, 16)
                    sp.dma_start(dtb[:, :], A["dn_dt_bias"].rearrange("a d h -> a (d h)").to_broadcast([P, 8])).then_inc(gw_in, 16)
                    sp.dma_start(alog[:, :], A["dn_a_log"].rearrange("a d h -> a (d h)").to_broadcast([P, 8])).then_inc(gw_in, 16)
                    sp.dma_start(tri[:, :, :], A["t_tri"]).then_inc(gw_in, 16)

                @block.tensor
                def _(pe):
                    pe.wait_ge(gw_in, 64)
                    for n in range(5):
                        for k in range(KD):
                            last = pe.matmul(PS[n][0:16, 0:width(n)], wg[:, k, :], hT[:, k, toff(n):toff(n) + width(n)],
                                             start=(k == 0), stop=(k == KD - 1))
                        last.then_inc(gates_mm, 1)
                    pe.wait_ge(gates_T, 5)
                    for c in range(STEPS):
                        last = pe.transpose(PS[5][:, c * 16:(c + 1) * 16], gT[0:16, c * P:(c + 1) * P], eye[0:16, 0:16])
                    last.then_inc(gates_tr, 1)
                    pe.wait_ge(gd, GD_DONE)
                    for i, m in enumerate((UI, LI, SL, SU, None, None)):
                        d = i % 2
                        last = pe.matmul(PS[6][:, i * 80:(i + 1) * 80], ones[:, :] if m is None else tri[:, m, :],
                                         g_all[:, :, d * 4:d * 4 + 4], start=True, stop=True)
                    last.then_inc(sums_mm, 1)

                @block.scalar
                def _(act):
                    act.preload_act_table_set("natural_log_exp_and_others")
                    act.wait_ge(gd, 3)
                    act.activation(beta[:, :, :], beta[:, :, :], ACT.Exp, scale=-1.0).then_inc(ga, 1)
                    act.wait_ge(gw_in, 64)
                    act.activation(alog[:, :], alog[:, :], ACT.Exp).then_inc(ga, 1)
                    act.wait_ge(gd, 4)
                    act.activation(ge[:, :, :], gx[:, :, :], ACT.Abs).then_inc(ga, 1)
                    act.wait_ge(ga, 3)
                    act.activation(ge[:, :, :], ge[:, :, :], ACT.Exp, scale=-1.0).then_inc(ga, 1)
                    act.wait_ge(sums_mm, 1)
                    for i, dst in enumerate((egc, egc, erest, erest, etot, etot)):
                        d = i % 2
                        act.activation(dst[:, :, d * 4:d * 4 + 4], PS[6][:, i * 80:(i + 1) * 80].rearrange("p (c h) -> p c h", h=4),
                                       ACT.Exp).then_inc(sums_ok, 1)

                @block.vector
                def _(dve):
                    n = [0]

                    def link(ins):
                        n[0] += 1
                        ins.then_inc(gd, 1)
                        dve.wait_ge(gd, n[0])

                    for u in range(5):
                        dve.wait_ge(gates_mm, u + 1)
                        dve.tensor_copy(gT[0:16, toff(u):toff(u) + width(u)], PS[u][0:16, 0:width(u)]).then_inc(gates_T, 1)
                    dve.wait_ge(gates_tr, 1)
                    link(dve.tensor_copy(gl[:, 0:STEPS, :].rearrange("p c g -> p (c g)"), PS[5][:, 0:STEPS * 16]))
                    link(dve.tensor_copy(gl[:, STEPS:NCH, :], gl[:, 0:2, :]))
                    link(dve.tensor_scalar_max(beta[:, :, :], gl[:, :, 0:8], CLAMP))
                    over = lambda v: v[:, :].unsqueeze(1).to_broadcast([P, NCH, 8])
                    dve.wait_ge(gw_in, 64)
                    link(dve.tensor_tensor(gx[:, :, :], gl[:, :, 8:16], over(dtb), ALU.add))
                    dve.wait_ge(ga, 1)
                    link(dve.tensor_scalar_add(beta[:, :, :], beta[:, :, :], 1.0))
                    link(dve.reciprocal(beta[:, :, :], beta[:, :, :]))
                    dve.wait_ge(ga, 4)
                    link(dve.tensor_scalar_add(gt[:, :, :], ge[:, :, :], 2.0))
                    link(dve.reciprocal(gt[:, :, :], gt[:, :, :]))
                    link(dve.tensor_tensor(ge[:, :, :], ge[:, :, :], gt[:, :, :], ALU.mult))
                    link(dve.tensor_tensor(gt[:, :, :], ge[:, :, :], ge[:, :, :], ALU.mult))
                    ser = g_all[:, :, :]
                    link(dve.tensor_scalar(ser, gt[:, :, :], 1.0 / 17, None, ALU.mult))
                    for k in range(7, 0, -1):
                        link(dve.scalar_tensor_tensor(ser, ser, 1.0 / (2 * k + 1), gt[:, :, :], ALU.add, ALU.mult))
                    link(dve.scalar_tensor_tensor(ser, ser, 1.0, ge[:, :, :], ALU.add, ALU.mult))
                    link(dve.tensor_scalar(gx[:, :, :], gx[:, :, :], 0.0, None, ALU.max))
                    link(dve.scalar_tensor_tensor(ser, ser, 2.0, gx[:, :, :], ALU.mult, ALU.add))
                    dve.wait_ge(ga, 2)
                    link(dve.scalar_tensor_tensor(ser, ser, -1.0, over(alog), ALU.mult, ALU.mult))
                    assert n[0] == GD_DONE
        if stop == 4:
            return

        with ExitStack() as st:
            NL = len(LEVELS)
            lv, pair = sbt(st, "lv", [P, 2 * NL, P // 2]), sbt(st, "pair", [P, 2, P])
            big = lambda name, n: sbt(st, name, [P, n, HEADS, P])
            kT, qT, kN, vN = big("kT", 4), big("qT", 4), big("kN", 4), big("vN", 4)
            Tb, Eb, AT, N2, TT = [big(n, 4) for n in ("Tb", "Eb", "AT", "N2", "TT")]
            off = sbt(st, "off", [P, 2, HEADS, P // 2])
            S, R, V, O = big("S", 2), big("R", 2), big("V", 2), big("O", 4)
            lv_in, ldk, ldv, o_st = sem("lv_in"), [sem(f"ldk{q}") for q in range(4)], [sem(f"ldv{q}") for q in range(4)], [sem(f"o_st{q}") for q in range(4)]
            gS_ok, diff_mm, E_ok, Em_ok, G_mm = sem("gS_ok"), sem("diff_mm"), sem("E_ok"), sem("Em_ok"), sem("G_mm")
            at_ok, n_ok, eye_ok, off_ok, tt0_ok = sem("at_ok"), sem("n_ok"), sem("eye_ok"), sem("off_ok"), sem("tt0_ok")
            T0_mm, T0_ok, P_mm, P_ok, U_mm, up_ok, T_tr, TT_ok = sem("T0_mm"), sem("T0_ok"), sem("P_mm"), sem("P_ok"), sem("U_mm"), sem("up_ok"), sem("T_tr"), sem("TT_ok")
            kd_ok, kS_mm, r1_ok, o1_ok, r_ok = sem("kd_ok"), sem("kS_mm"), sem("r1_ok"), sem("o1_ok"), sem("r_ok")
            TR_mm, v_ok, upd_mm, sx_ok, s_ok, o_ok = sem("TR_mm"), sem("v_ok"), sem("upd_mm"), sem("sx_ok"), sem("s_ok"), sem("o_ok")
            heads = range(HEADS)
            b4 = lambda bank: PS[bank][:, :].rearrange("p (h c) -> p h c", c=P)
            mask4 = lambda m: m.unsqueeze(1).to_broadcast([P, HEADS, m.shape[-1]])

            def half(v, d, l):
                return v.rearrange("p h (n t b) -> p h n t b", t=2, b=LEVELS[l] if l >= 0 else 1)[:, :, :, d, :]

            def item(it, e):
                return it * 4 + (e + 1)

            def merge(it, l, e):
                return it * (4 * NL) + (e // 2 * 2 * NL + 2 * l + e % 2 + 1)

            def TT_before(it, l, e):
                return merge(it, l, e) + 2 * NL

            def chunk(it, e):
                return it * 2 + e // 2 if e % 2 == 0 else it * -2 + (NCH - 1 - e // 2)

            def per_token(v, it, e):
                d = e % 2
                return (v[:, ds(chunk(it, e), 1), d * 4:d * 4 + 4].rearrange("p a h -> p (a h)")
                        .unsqueeze(2).to_broadcast([P, HEADS, P]))

            def all_steps(eng, scan_and_inverse):
                with eng.Fori(0, STEPS // 2 - 1) as it:
                    for w in range(2):
                        scan_and_inverse(it, w, True, True)
                scan_and_inverse(STEPS // 2 - 1, 0, True, False)
                scan_and_inverse(STEPS // 2 - 1, 1, False, False)

            with nc.Block() as block:
                @block.sync
                def _(sp):
                    def load(it, e, bufs, ld):
                        for buf, src in bufs:
                            sp.dma_start(buf[:, e % 4, :, :], src[ds(chunk(it, e), 1), :, :, :].rearrange("a p h t -> p (a h) t")).then_inc(ld[e % 4], 16)

                    keys, values = ((kT, kT_d), (qT, qT_d)), ((kN, kN_d), (vN, vN_d))
                    for e in range(4):
                        load(0, e, keys, ldk)
                        if e == 0:
                            sp.dma_start(lv[:, :, :], A["t_lv"]).then_inc(lv_in, 16)
                            sp.dma_start(pair[:, :, :], A["t_pair"]).then_inc(lv_in, 16)
                    for e in range(4):
                        load(0, e, values, ldv)

                    def step(it, w, inverse, more):
                        es = (2 * w, 2 * w + 1)
                        if more:
                            for e in es:
                                sp.wait_ge(kS_mm, item(it, e))
                                load(it, e + 4, keys, ldk)
                        for e in es:
                            sp.wait_ge(o_ok, item(it, e) + 2)
                            sp.dma_start(o_d[e % 2][ds(chunk(it, e), 1), :, :, :].rearrange("a p h t -> p (a h) t"),
                                         O[:, e, :, :]).then_inc(o_st[e], 16)
                            if more:
                                load(it, e + 4, values, ldv)

                    all_steps(sp, step)
                    for q in range(4):
                        sp.wait_ge(o_st[q], 16 * (STEPS // 2 + 1))

                @block.tensor
                def _(pe):
                    def mm4(bank, lhsT, rhs):
                        for h in heads:
                            last = pe.matmul(b4(bank)[:, h, :], lhsT[:, h, :], rhs[:, h, :] if len(rhs.shape) == 3 else rhs,
                                             start=True, stop=True)
                        return last

                    def turn(bank, src):
                        for h in heads:
                            last = pe.transpose(b4(bank)[:, h, :], src[:, h, :], eye[:, :])
                        return last

                    def differences(it, e):
                        d = e % 2
                        pe.wait_ge(gS_ok, item(it, e))
                        pe.wait_ge(TT_ok, TT_before(it, 0, e))
                        mm4(2 * d, Tb[:, e % 4], tri[:, UI + d, :]).then_inc(diff_mm, 1)

                    def gram(it, e):
                        d, q = e % 2, e % 4
                        pe.wait_ge(ldk[q], it * 32 + (e // 4 * 32 + 32))
                        pe.wait_ge(E_ok, item(it, e))
                        mm4(2 * d, kT[:, q], kT[:, q])
                        mm4(2 * d + 1, kT[:, q], qT[:, q]).then_inc(G_mm, 1)

                    def merges(it, es):
                        for e in es:
                            pe.wait_ge(tt0_ok, item(it, e))
                            turn(2 * (e % 2), TT[:, e % 4]).then_inc(T0_mm, 1)
                        for e in es:
                            pe.wait_ge(T0_ok, item(it, e))
                            mm4(2 * (e % 2), N2[:, e % 4], Tb[:, e % 4]).then_inc(P_mm, 1)
                        for l in range(NL):
                            for e in es:
                                pe.wait_ge(P_ok, merge(it, l, e))
                                pe.wait_ge(TT_ok, TT_before(it, l, e))
                                mm4(2 * (e % 2), TT[:, e % 4], Eb[:, e % 4]).then_inc(U_mm, 1)
                            for e in es:
                                pe.wait_ge(up_ok, merge(it, l, e))
                                if l < NL - 1:
                                    mm4(2 * (e % 2), N2[:, e % 4], Tb[:, e % 4]).then_inc(P_mm, 1)
                                if l == 0:
                                    pe.wait_ge(at_ok, item(it, e))
                                turn(2 * (e % 2) + 1, Tb[:, e % 4]).then_inc(T_tr, 1)

                    for e in range(2):
                        differences(0, e)
                    for e in range(2):
                        gram(0, e)
                    merges(0, (0, 1))

                    def step(it, w, inverse, more):
                        es, nx = (2 * w, 2 * w + 1), (2 * w + 2, 2 * w + 3)
                        for e in es:
                            d = e % 2
                            pe.wait_ge(s_ok, item(it, e))
                            pe.wait_ge(o_ok, item(it, e))
                            mm4(4 + 2 * d, kT[:, e], S[:, d])
                            mm4(5 + 2 * d, qT[:, e], S[:, d]).then_inc(kS_mm, 1)
                        if inverse:
                            for e in nx:
                                differences(it, e)
                        for e in es:
                            pe.wait_ge(r_ok, item(it, e))
                            pe.wait_ge(TT_ok, TT_before(it, NL, e))
                            mm4(4 + 2 * (e % 2), TT[:, e], R[:, e % 2]).then_inc(TR_mm, 1)
                        if inverse:
                            for e in nx:
                                gram(it, e)
                        for e in es:
                            d = e % 2
                            pe.wait_ge(v_ok, item(it, e))
                            pe.wait_ge(kd_ok, item(it, e))
                            pe.wait_ge(o1_ok, item(it, e))
                            mm4(5 + 2 * d, kN[:, e], V[:, d])
                            mm4(4 + 2 * d, AT[:, e], V[:, d]).then_inc(upd_mm, 1)
                        if inverse:
                            merges(it, nx)

                    all_steps(pe, step)

                @block.scalar
                def _(act):
                    act.preload_act_table_set("natural_log_exp_and_others")
                    act.sem_inc(TT_ok, 2 * NL + 2)
                    flat = lambda t, e: t[:, e % 4, :, :].rearrange("p h c -> p (h c)")

                    def inverses(it, es):
                        for e in es:
                            act.wait_ge(diff_mm, item(it, e))
                            act.activation(flat(Eb, e), PS[2 * (e % 2)][:, :], ACT.Exp).then_inc(E_ok, 1)
                        for e in es:
                            act.wait_ge(T0_mm, item(it, e))
                            act.activation(flat(Tb, e), PS[2 * (e % 2)][:, :], ACT.Copy).then_inc(T0_ok, 1)
                        for l in range(NL):
                            for e in es:
                                act.wait_ge(T_tr, merge(it, l, e))
                                act.activation(flat(TT, e), PS[2 * (e % 2) + 1][:, :], ACT.Copy).then_inc(TT_ok, 1)

                    inverses(0, (0, 1))

                    def step(it, w, inverse, more):
                        if inverse:
                            inverses(it, (2 * w + 2, 2 * w + 3))

                    all_steps(act, step)

                @block.gpsimd
                def _(pool):
                    def decays(it, e):
                        pool.wait_ge(TT_ok, merge(it, 0, e // 2 * 2 + 1))
                        plainly(pool)
                        pool.tensor_tensor(Tb[:, e % 4], mask4(tri[:, SL - e % 2, :]), per_token(g_all, it, e), ALU.mult).then_inc(gS_ok, 1)

                    def masked(it, e):
                        pool.wait_ge(E_ok, item(it, e))
                        pool.tensor_tensor(Eb[:, e % 4], Eb[:, e % 4], mask4(tri[:, UI + e % 2, :]), ALU.mult).then_inc(Em_ok, 1)

                    def identity(it, e):
                        if e >= 4:
                            pool.wait_ge(TR_mm, item(it, e - 4))
                            plainly(pool)
                        pool.tensor_copy(TT[:, e % 4], mask4(eye[:, :])).then_inc(eye_ok, 1)

                    def decayed_keys(it, e):
                        q = e % 4
                        pool.wait_ge(ldv[q], it * 32 + (e // 4 * 32 + 32))
                        plainly(pool)
                        pool.tensor_tensor(kN[:, q], kN[:, q], per_token(erest, it, e), ALU.mult).then_inc(kd_ok, 1)

                    decays(0, 0)
                    decays(0, 1)
                    pool.wait_ge(lv_in, 32)
                    for stage, first in ((identity, 0), (masked, 0), (decayed_keys, 0), (decays, 2), (identity, 2)):
                        for e in range(2):
                            stage(0, first + e)

                    def step(it, w, inverse, more):
                        es, nx = (2 * w, 2 * w + 1), (2 * w + 2, 2 * w + 3)
                        for e in es:
                            pool.wait_ge(r1_ok, item(it, e))
                            pool.tensor_tensor(R[:, e % 2], vN[:, e], R[:, e % 2], ALU.subtract).then_inc(r_ok, 1)
                        if inverse:
                            for e in nx:
                                masked(it, e)
                        for e in es:
                            plainly(pool)
                            pool.tensor_tensor(S[:, e % 2], S[:, e % 2], per_token(etot, it, e), ALU.mult).then_inc(sx_ok, 1)
                        if inverse:
                            for e in nx:
                                decayed_keys(it, e)
                        if more:
                            for stage in (decays, identity):
                                for e in nx:
                                    stage(it, e + 2)

                    all_steps(pool, step)

                @block.vector
                def _(dve):
                    dve.sem_inc(o_ok, 2)
                    for q in range(4):
                        dve.sem_inc(o_st[q], 16)
                    for d in range(2):
                        dve.memset(S[:, d], 0.0).then_inc(s_ok, 1)

                    dve.wait_ge(lv_in, 32)

                    def gram(it, es):
                        for e in es:
                            d, q = e % 2, e % 4
                            dve.wait_ge(G_mm, item(it, e))
                            dve.wait_ge(Em_ok, item(it, e))
                            for h in heads:
                                col = beta[:, ds(chunk(it, e), 1), d * 4 + h:d * 4 + h + 1].rearrange("p a h -> p (a h)")
                                last = dve.scalar_tensor_tensor(N2[:, q, h, :], Eb[:, q, h, :], col, b4(2 * d)[:, h, :], ALU.mult, ALU.mult)
                            last.then_inc(n_ok, 1)
                        for e in es:
                            d, q = e % 2, e % 4
                            dve.wait_ge(n_ok, item(it, e))
                            dve.tensor_tensor(off[:, d], half(N2[:, q], 1 - d, -1).rearrange("p h n b -> p h (n b)"), mask2(d), ALU.mult).then_inc(off_ok, 1)
                        for e in es:
                            d, q = e % 2, e % 4
                            dve.wait_ge(off_ok, item(it, e))
                            dve.wait_ge(eye_ok, item(it, e))
                            T = half(TT[:, q], 1 - d, -1).rearrange("p h n b -> p h (n b)")
                            dve.tensor_tensor(T, T, off[:, d], ALU.subtract).then_inc(tt0_ok, 1)
                        for e in es:
                            d, q = e % 2, e % 4
                            dve.tensor_tensor(AT[:, q], Eb[:, q], b4(2 * d + 1), ALU.mult).then_inc(at_ok, 1)

                    def mask2(d):
                        return pair[:, d, :].rearrange("p (n t) -> p n t", t=2)[:, :, 1 - d].unsqueeze(1).to_broadcast([P, HEADS, P // 2])

                    def merges(it, es):
                        for l in range(NL):
                            for e in es:
                                d = e % 2
                                if l == 0:
                                    dve.wait_ge(at_ok, item(it, e))
                                dve.wait_ge(P_mm, merge(it, l, e))
                                m = lv[:, 2 * l + d, :].rearrange("p (n b) -> p n b", b=LEVELS[l])
                                dve.tensor_tensor(half(Eb[:, e % 4], d, l), half(b4(2 * d), d, l),
                                                  m.unsqueeze(1).to_broadcast([P, HEADS, *m.shape[1:]]), ALU.mult).then_inc(P_ok, 1)
                            for e in es:
                                d = e % 2
                                dve.wait_ge(U_mm, merge(it, l, e))
                                T = half(Tb[:, e % 4], d, l)
                                dve.tensor_tensor(T, T, half(b4(2 * d), d, l), ALU.subtract).then_inc(up_ok, 1)

                    gram(0, (0, 1))
                    merges(0, (0, 1))

                    def step(it, w, inverse, more):
                        es, nx = (2 * w, 2 * w + 1), (2 * w + 2, 2 * w + 3)
                        for e in es:
                            dve.wait_ge(kS_mm, item(it, e))
                            dve.tensor_tensor(R[:, e % 2], b4(4 + 2 * (e % 2)), per_token(egc, it, e), ALU.mult).then_inc(r1_ok, 1)
                        for e in es:
                            dve.wait_ge(o_st[e], it * 16 + 16)
                            dve.tensor_tensor(O[:, e], b4(5 + 2 * (e % 2)), per_token(egc, it, e), ALU.mult).then_inc(o1_ok, 1)
                        for e in es:
                            dve.wait_ge(TR_mm, item(it, e))
                            dve.tensor_tensor(V[:, e % 2], b4(4 + 2 * (e % 2)), per_token(beta, it, e), ALU.mult).then_inc(v_ok, 1)
                        if inverse:
                            gram(it, nx)
                        for e in es:
                            d = e % 2
                            dve.wait_ge(upd_mm, item(it, e))
                            dve.wait_ge(sx_ok, item(it, e))
                            dve.tensor_tensor(S[:, d], S[:, d], b4(5 + 2 * d), ALU.add).then_inc(s_ok, 1)
                            dve.wait_ge(o1_ok, item(it, e))
                            dve.tensor_tensor(O[:, e], O[:, e], b4(4 + 2 * d), ALU.add).then_inc(o_ok, 1)
                        if inverse:
                            merges(it, nx)

                    all_steps(dve, step)
        if stop == 5:
            return
        gst.close()
        recycle()

        yst = top.enter_context(ExitStack())
        x0T = sbt(yst, "x0T", [P, 2, SEQ])
        ycT = sbt(yst, "ycT", [P, 2, SEQ])
        yaT = sbt(yst, "yaT", [P, HEADS, SEQ])
        zT = yaT[:, 0:2, :]

        with ExitStack() as st:
            wh = sbt(st, "wh", [P, 6, KD, P])
            x1s, cs = sbt(st, "x1s", [P, SEQ]), sbt(st, "cs", [P, SEQ])
            tmp, tm2 = sbt(st, "tmp_h", [P, 2, TW]), sbt(st, "tm2", [P, TW])
            nat = sbt(st, "nat_h", [P, 2, TW])
            NH2 = 24
            w_ok, w_free = [sem(f"wh_ok{k}") for k in range(6)], sem("wh_free")
            mm_ok, ps_free, c1, c2, c3 = sem("mm_ok_h"), sem("ps_free_h"), sem("c1_h"), sem("c2_h"), sem("c3_h")
            z_ok, z_tr, znat_ok, z_st, ch_ok, yc_ok, zc_ok = sem("z_ok"), sem("z_tr"), sem("znat_ok"), [sem("z_st0"), sem("z_st1")], sem("ch_ok"), sem("yc_ok"), sem("zc_ok")
            kinds = [(kind, n) for kind in range(6) for n in range(NT)]
            with nc.Block() as block:
                @block.sync
                def _(sp):
                    with sp.Fori(0, 2) as h:
                        for kind in range(6):
                            sp.wait_ge(w_free, h * 6 + kind + 1)
                            sp.dma_start(wh[:, kind, :, :], A["w_in"][0, :, ds(h * P + (B_OFF + kind * HW), P)]
                                         .rearrange("(k p) c -> p k c", p=P)).then_inc(w_ok[kind], 16)

                @block.tensor
                def _(pe):
                    def turn(h, n):
                        pe.wait_ge(z_ok, h * NT + n + 1)
                        pe.wait_ge(znat_ok, h * NT + n + 1)
                        for j in range(4):
                            last = pe.transpose(PS[4 + n % 2][:, j * P:(j + 1) * P], tmp[:, n % 2, j * P:(j + 1) * P], eye[:, :])
                        last.then_inc(z_tr, 1)

                    with pe.Fori(0, 2) as h:
                        for u, (kind, n) in enumerate(kinds):
                            if n == 0:
                                pe.wait_ge(w_ok[kind], h * 16 + 16)
                            pe.wait_ge(ps_free, h * NH2 + u + 1)
                            for k in range(KD):
                                last = pe.matmul(PS[u % 4][:, :], wh[:, kind, k, :], hT[:, k, toff(n + 1):toff(n + 1) + TW],
                                                 start=(k == 0), stop=(k == KD - 1))
                            last.then_inc(mm_ok, 1)
                            if n == NT - 1:
                                pe.wait_ge(mm_ok, h * NH2 + u + 1)
                                pe.sem_inc(w_free, 1)
                            if 9 <= u < 13:
                                turn(h, u - 9)

                @block.scalar
                def _(act):
                    act.sem_inc(znat_ok, 2)
                    for b in range(2):
                        act.sem_inc(z_st[b], 16)
                    with act.Fori(0, 2) as h:
                        for u, (kind, n) in enumerate(kinds):
                            sl = slice(n * TW, (n + 1) * TW)
                            if kind == 5:
                                act.wait_ge(ch_ok, h * NT + n + 1)
                                act.wait_ge(yc_ok, h * NT + n + 1)
                                plainly(act)
                                act.activation(tm2[:, :], tmp[:, n % 2, :], ACT.Copy,
                                               scale=cols[:, ds(h + (R_SCW + 2), 1)]).then_inc(c1, 1)
                                continue
                            act.wait_ge(mm_ok, h * NH2 + u + 1)
                            plainly(act)
                            src = PS[u % 4][:, :]
                            if kind < 3:
                                if kind == 2:
                                    act.wait_ge(zc_ok, h * NT + n + 1)
                                    act.wait_ge(z_tr, h * NT + n) if n else None
                                    plainly(act)
                                dst = (x0T[:, ds(h, 1), sl].rearrange("p a t -> p (a t)"), x1s[:, sl], tmp[:, n % 2, :])[kind]
                                act.activation(dst, src, ACT.Identity, bias=cols[:, ds(h + (R_HYB + kind * 2), 1)],
                                               scale=cols[:, ds(h + (R_HYW + 6 + kind * 2), 1)]).then_inc(c1, 1)
                            elif kind == 3:
                                act.activation(ycT[:, ds(h, 1), sl].rearrange("p a t -> p (a t)"), src, ACT.Copy).then_inc(c1, 1)
                            else:
                                act.activation(cs[:, sl], src, ACT.Copy).then_inc(c1, 1)
                            if 10 <= u < 14:
                                m = u - 10
                                act.wait_ge(z_tr, h * NT + m + 1)
                                act.wait_ge(z_st[m % 2], h * 32 + (m // 2) * 16 + 16)
                                act.activation(nat[:, m % 2, :], PS[4 + m % 2][:, :], ACT.Copy).then_inc(znat_ok, 1)
                                act.wait_ge(znat_ok, h * NT + m + 3)
                                act.dma_start(z_d[m * TW:(m + 1) * TW, ds(h * P, P)].rearrange("(j p) c -> p j c", p=P),
                                              nat[:, m % 2, :].rearrange("p (j c) -> p j c", c=P)).then_inc(z_st[m % 2], 16)
                    for b in range(2):
                        act.wait_ge(z_st[b], 80)

                @block.gpsimd
                def _(pool):
                    pool.sem_inc(zc_ok, 2)
                    with pool.Fori(0, 2) as h:
                        for n in range(NT):
                            pool.wait_ge(z_ok, h * NT + n + 1)
                            plainly(pool)
                            pool.tensor_copy(zT[:, ds(h, 1), n * TW:(n + 1) * TW].rearrange("p a t -> p (a t)"),
                                             tmp[:, n % 2, :]).then_inc(zc_ok, 1)

                @block.vector
                def _(dve):
                    dve.sem_inc(w_free, 6)
                    dve.sem_inc(yc_ok, 1)
                    dve.sem_inc(ps_free, 4)
                    with dve.Fori(0, 2) as h:
                        for u, (kind, n) in enumerate(kinds):
                            at = h * NH2 + u + 1
                            sl = slice(n * TW, (n + 1) * TW)
                            if kind in (3, 4):
                                dve.wait_ge(c1, at)
                                dve.sem_inc(ps_free, 1)
                                dve.sem_inc(c2, 1)
                                dve.sem_inc(c3, 1)
                                continue
                            grid = lambda v: v.rearrange("p (r c) -> p r c", c=GRID_W)
                            if kind == 5:
                                dve.wait_ge(mm_ok, at)
                                if n == 0:
                                    dve.wait_ge(zc_ok, h * NT + NT + 2)
                                dve.tensor_tensor(tmp[:, n % 2, :], cs[:, sl], PS[u % 4][:, :], ALU.mult).then_inc(ch_ok, 1)
                                src, t, base, step = grid(tmp[:, n % 2, :]), grid(tm2[:, :]), R_SCW, 2
                                dve.wait_ge(ch_ok, h * NT + n + 1)
                                dve.sem_inc(ps_free, 1)
                            else:
                                dst = (x0T[:, ds(h, 1), sl].rearrange("p a t -> p (a t)"), x1s[:, sl], tmp[:, n % 2, :])[kind]
                                src, t, base, step = grid(PS[u % 4][:, :]), grid(dst), R_HYW + kind * 2, 6
                            dve.wait_ge(c1, at)
                            dve.scalar_tensor_tensor(t[:, :, 1:GRID_W], src[:, :, 0:GRID_W - 1], cols[:, ds(h + base, 1)],
                                                     t[:, :, 1:GRID_W], ALU.mult, ALU.add).then_inc(c2, 1)
                            dve.wait_ge(c2, at)
                            dve.scalar_tensor_tensor(t[:, :, 0:GRID_W - 1], src[:, :, 1:GRID_W], cols[:, ds(h + (base + 2 * step), 1)],
                                                     t[:, :, 0:GRID_W - 1], ALU.mult, ALU.add).then_inc(c3, 1)
                            dve.wait_ge(c3, at)
                            if kind < 3:
                                dve.sem_inc(ps_free, 1)
                            if kind == 2:
                                dve.tensor_tensor(tmp[:, n % 2, :], tmp[:, n % 2, :], x1s[:, sl], ALU.mult).then_inc(z_ok, 1)
                            if kind == 5:
                                yc = ycT[:, ds(h, 1), sl].rearrange("p a t -> p (a t)")
                                dve.tensor_tensor(yc, yc, tm2[:, :], ALU.mult).then_inc(yc_ok, 1)
                                dve.wait_ge(yc_ok, h * NT + n + 2)
        if stop == 7:
            return

        EV = NB + NB // 2
        with ExitStack() as st:
            zb = sbt(st, "zb", [P, 2, HW])
            hb = sbt(st, "hb", [P, 2, 2 * HW])
            fw = sbt(st, "fw", [P, 2, NB, 2 * FK])
            az = sbt(st, "az", [2 * FK, 2, 3, NB, HW])
            b_in, b_free, a_mm, a_ev, a_st = [sem("b_in0"), sem("b_in1")], sem("b_free"), sem("a_mm"), sem("a_ev"), [sem("a_st0"), sem("a_st1")]
            NBLK = FN // NB
            LD = 16 * (2 * NB + 1)
            with nc.Block() as block:
                @block.sync
                def _(sp):
                    with sp.Fori(0, NBLK // 2) as i:
                        for b in range(2):
                            sp.wait_ge(b_free, i * 2 + b + 1)
                            for buf, src in ((zb, z_d), (hb, h_d)):
                                for n in range(NB):
                                    sp.dma_start(buf[n * FR:(n + 1) * FR, b], src.rearrange("(a n) c -> n a c", n=FN)[ds(i * 2 * NB + (b * NB + n), 1)]
                                                 .rearrange("n a c -> (n a) c")).then_inc(b_in[b], 16)
                            sp.dma_start(fw[:, b], A["t_fa"][:, ds(i * 2 + b, 1)].rearrange("p a n k -> p (a n) k")).then_inc(b_in[b], 16)

                @block.tensor
                def _(pe):
                    with pe.Fori(0, NBLK // 2) as i:
                        for b in range(2):
                            pe.wait_ge(b_in[b], i * LD + LD)
                            for n in range(NB):
                                pe.wait_ge(a_ev, i * (2 * EV) + b * EV + n + n // 2 + 1)
                                last = pe.matmul(PS[n % 4][0:2 * FK, :], fw[:, b, n, :], hb[:, b, :], start=True, stop=True)
                                last.then_inc(a_mm, 1)
                                last = pe.matmul(PS[4 + n // 2 % 2][0:2 * FK, n % 2 * HW:(n % 2 + 1) * HW], fw[:, b, n, :], zb[:, b, :],
                                                 start=True, stop=True)
                                if n % 2:
                                    last.then_inc(a_mm, 1)
                            pe.wait_ge(a_mm, i * (2 * EV) + b * EV + EV)
                            pe.sem_inc(b_free, 1)

                @block.vector
                def _(dve):
                    dve.sem_inc(b_free, 2)
                    dve.sem_inc(a_ev, 4)
                    for b in range(2):
                        dve.sem_inc(a_st[b], 48)
                    with dve.Fori(0, NBLK // 2) as i:
                        for b in range(2):
                            dve.wait_ge(a_st[b], i * 48 + 48)
                            m = 0
                            for n in range(NB):
                                m += 1
                                dve.wait_ge(a_mm, i * (2 * EV) + b * EV + m)
                                dve.tensor_copy(az[:, b, 1:3, n, :], PS[n % 4][0:2 * FK, :].rearrange("p (s c) -> p s c", s=2)).then_inc(a_ev, 1)
                                if n % 2:
                                    m += 1
                                    dve.wait_ge(a_mm, i * (2 * EV) + b * EV + m)
                                    dve.tensor_copy(az[:, b, 0, n - 1:n + 1, :], PS[4 + n // 2 % 2][0:2 * FK, :].rearrange("p (s c) -> p s c", s=2)).then_inc(a_ev, 1)

                @block.scalar
                def _(act):
                    with act.Fori(0, NBLK // 2) as i:
                        for b in range(2):
                            blk = ds(i * 2 * NB + b * NB, NB)
                            act.wait_ge(a_ev, i * (2 * EV) + b * EV + EV + 4)
                            for s in range(3):
                                act.dma_start(fa_d[s].rearrange("r k n c -> (r k) n c")[:, blk, :], az[:, b, s]).then_inc(a_st[b], 16)
                    for b in range(2):
                        act.wait_ge(a_st[b], 48 * (NBLK // 2 + 1))
        if stop == 8:
            return

        CW = 3 * HW // 2
        with ExitStack() as st:
            gm = sbt(st, "gm", [P, 7, P])
            sp_in = sbt(st, "sp_in", [P, 2, 3, 3, HW])
            xs = sbt(st, "xs", [P, 2, 2, CW])
            yp = sbt(st, "yp", [P, 2, 2, CW])
            bk = sbt(st, "bk", [P, 2, CW])
            g_in, s_in, s_free = sem("g_in"), [sem("s_in0"), sem("s_in1")], sem("s_free")
            sx_mm, sx_cp, sp_pr, sp_y, c_mm, c_cp, c_st = sem("sx_mm"), sem("sx_cp"), sem("sp_pr"), sem("sp_y"), sem("c_mm"), sem("c_cp"), [sem("c_st0"), sem("c_st1")]
            with nc.Block() as block:
                def blocks(eng, body):
                    with eng.Fori(0, FK // 6) as i:
                        for b in range(2):
                            body(i * 2 + b, b, i * 6 + b * 3)
                    body(FK // 6 * 2, 0, FK // 6 * 6)

                @block.sync
                def _(sp):
                    sp.dma_start(gm[:, :, :], A["t_g"]).then_inc(g_in, 16)

                    def body(n, b, k):
                        sp.wait_ge(s_free, n + 1)
                        for s in range(3):
                            for r in range(2):
                                sp.dma_start(sp_in[r * FN:(r + 1) * FN, b, s], fa_d[s, r, ds(k, 3), :, :].rearrange("k n c -> n k c")).then_inc(s_in[b], 16)

                    blocks(sp, body)

                @block.tensor
                def _(pe):
                    pe.wait_ge(g_in, 16)

                    def back(m, v):
                        pe.wait_ge(sp_y, m)
                        pe.wait_ge(c_cp, m)
                        pe.matmul(PS[6 + v][:, 0:CW], gm[:, 6, :], yp[:, v, 0, :], start=True, stop=True).then_inc(c_mm, 1)

                    def body(n, b, k):
                        loads = n * 48 + (96 - 48 * b)
                        pe.wait_ge(s_in[b], loads)
                        for v in range(2):
                            col = slice(v * CW, (v + 1) * CW)
                            sig = [sp_in[:, b, s].rearrange("p k c -> p (k c)")[:, col] for s in range(3)]
                            at = n * 2 + v
                            pe.wait_ge(sx_cp, at * 2 + 1)
                            pe.matmul(PS[0][:, 0:CW], gm[:, 0, :], sig[0], start=True, stop=True)
                            pe.matmul(PS[1][:, 0:CW], gm[:, 1, :], sig[0], start=True, stop=True).then_inc(sx_mm, 1)
                            pe.wait_ge(sp_pr, at * 2 + 1)
                            pe.matmul(PS[2 + 2 * v][:, 0:CW], gm[:, 2, :], sig[1], start=True, stop=False)
                            pe.matmul(PS[2 + 2 * v][:, 0:CW], gm[:, 3, :], sig[2], start=False, stop=True)
                            pe.matmul(PS[3 + 2 * v][:, 0:CW], gm[:, 4, :], sig[1], start=True, stop=False)
                            pe.matmul(PS[3 + 2 * v][:, 0:CW], gm[:, 5, :], sig[2], start=False, stop=True).then_inc(sx_mm, 1)
                            if v == 1:
                                pe.wait_ge(sx_mm, n * 4 + 4)
                                pe.sem_inc(s_free, 1)
                                back(n * 2 + 1, 0)
                        back(n * 2 + 2, 1)

                    blocks(pe, body)

                @block.scalar
                def _(act):
                    act.sem_inc(sx_cp, 1)
                    act.sem_inc(c_cp, 2)
                    for b in range(2):
                        act.sem_inc(c_st[b], 16)

                    def body(n, b, k):
                        for v in range(2):
                            at = n * 2 + v
                            act.wait_ge(sx_mm, at * 2 + 1)
                            for j in range(2):
                                act.activation(xs[:, v, j, :], PS[j][:, 0:CW], ACT.Copy).then_inc(sx_cp, 1)
                        for v in range(2):
                            act.wait_ge(c_mm, n * 2 + v + 1)
                            act.wait_ge(c_st[v], n * 16 + 16)
                            act.activation(bk[:, v, :], PS[6 + v][:, 0:CW], ACT.Copy).then_inc(c_cp, 1)
                            act.wait_ge(c_cp, n * 2 + v + 3)
                            act.dma_start(dst[:, ds(k * HW + v * CW, CW)], bk[:, v, :]).then_inc(c_st[v], 16)

                    dst = fb_d.rearrange("r n k c -> (r n) (k c)")
                    blocks(act, body)
                    for v in range(2):
                        act.wait_ge(c_st[v], 16 * (FK // 3 + 1))

                @block.vector
                def _(dve):
                    dve.sem_inc(s_free, 2)
                    dve.sem_inc(sp_pr, 3)

                    def body(n, b, k):
                        for v in range(2):
                            at = n * 2 + v
                            dve.wait_ge(sx_cp, at * 2 + 3)
                            dve.wait_ge(sx_mm, at * 2 + 2)
                            for j in range(2):
                                dve.tensor_tensor(yp[:, v, j, :], xs[:, v, j, :], PS[2 + 2 * v + j][:, 0:CW], ALU.mult).then_inc(sp_pr, 1)

                    blocks(dve, body)

                @block.gpsimd
                def _(pool):
                    def body(n, b, k):
                        for v in range(2):
                            pool.wait_ge(sp_pr, n * 4 + v * 2 + 5)
                            pool.tensor_tensor(yp[:, v, 0, :], yp[:, v, 0, :], yp[:, v, 1, :], ALU.add).then_inc(sp_y, 1)

                    blocks(pool, body)
        if stop == 9:
            return

        with ExitStack() as st:
            bb = sbt(st, "bb", [P, 2, NB, HW])
            fd = sbt(st, "fd", [P, 2, NB, FR])
            ys = sbt(st, "ys", [FR, 2, NB, HW])
            pad_ok = sem("pad_ok")
            d_in, d_free, d_mm, d_ev, d_st = [sem("d_in0"), sem("d_in1")], sem("d_free"), sem("d_mm"), sem("d_ev"), [sem("d_st0"), sem("d_st1")]
            with nc.Block() as block:
                @block.sync
                def _(sp):
                    sp.wait_ge(pad_ok, 2)
                    with sp.Fori(0, NBLK // 2) as i:
                        for b in range(2):
                            blk = ds(i * 2 * NB + b * NB, NB)
                            sp.wait_ge(d_free, i * 2 + b + 1)
                            for r in range(2):
                                sp.dma_start(bb[r * FK:(r + 1) * FK, b], fb_d[r, blk, :, :].rearrange("n k c -> k n c")).then_inc(d_in[b], 16)
                            sp.dma_start(fd[0:2 * FK, b], A["t_fd"][:, blk, :]).then_inc(d_in[b], 16)

                @block.tensor
                def _(pe):
                    with pe.Fori(0, NBLK // 2) as i:
                        for b in range(2):
                            pe.wait_ge(d_in[b], i * 48 + 48)
                            for n in range(NB):
                                if n % 2 == 0:
                                    pe.wait_ge(d_ev, i * NB + b * (NB // 2) + n // 2 + 1)
                                last = pe.matmul(PS[(b * NB // 2 + n // 2) % 4][0:FR, n % 2 * HW:(n % 2 + 1) * HW], fd[:, b, n, :], bb[:, b, n, :],
                                                 start=True, stop=True)
                                if n % 2:
                                    last.then_inc(d_mm, 1)
                            pe.wait_ge(d_mm, i * NB + b * (NB // 2) + NB // 2)
                            pe.sem_inc(d_free, 1)

                @block.vector
                def _(dve):
                    dve.memset(bb[64:P, :, :, :], 0.0).then_inc(pad_ok, 1)
                    dve.memset(fd[64:P, :, :, :], 0.0).then_inc(pad_ok, 1)
                    dve.sem_inc(d_free, 2)
                    dve.sem_inc(d_ev, 4)
                    for b in range(2):
                        dve.sem_inc(d_st[b], 16)
                    with dve.Fori(0, NBLK // 2) as i:
                        for b in range(2):
                            dve.wait_ge(d_st[b], i * 16 + 16)
                            for m in range(NB // 2):
                                dve.wait_ge(d_mm, i * NB + b * (NB // 2) + m + 1)
                                dve.tensor_copy(ys[:, b, 2 * m:2 * m + 2, :], PS[(b * NB // 2 + m) % 4][0:FR, :].rearrange("p (s c) -> p s c", s=2)).then_inc(d_ev, 1)

                @block.scalar
                def _(act):
                    with act.Fori(0, NBLK // 2) as i:
                        for b in range(2):
                            act.wait_ge(d_ev, i * NB + b * (NB // 2) + NB // 2 + 4)
                            act.dma_start(y_d.rearrange("(a n) c -> a n c", n=FN)[:, ds(i * 2 * NB + b * NB, NB), :], ys[:, b]).then_inc(d_st[b], 16)
                    for b in range(2):
                        act.wait_ge(d_st[b], 16 * (NBLK // 2 + 1))
        if stop == 10:
            return

        recycle()
        TILES = SEQ // P
        with ExitStack() as st:
            ofb, obb, szb, sqb = [sbt(st, n, [P, 2, HEADS, P]) for n in ("ofb", "obb", "szb", "sqb")]
            ss = sbt(st, "ss_o", [P, 2, HEADS])
            yn, ty = sbt(st, "yn", [P, 2, 4, HW]), sbt(st, "ty", [P, 2, TW])
            o_in, o_free, sum_ok, osq_ok, oss_ok = [sem("o_in0"), sem("o_in1")], sem("o_free"), sem("sum_ok"), sem("osq_ok"), sem("oss_ok")
            oln, ort, on_ok, o_tr, ya_ok = sem("oln"), sem("ort"), sem("on_ok"), sem("o_tr"), sem("ya_ok")
            y_in, y_free, y_tr, y_ok1, y_ok2 = [sem("y_in0"), sem("y_in1")], sem("y_free"), sem("y_tr"), sem("y_ok1"), sem("y_ok2")
            with nc.Block() as block:
                @block.sync
                def _(sp):
                    with sp.Fori(0, 2) as i:
                        for b in range(2):
                            sp.wait_ge(y_free, i * 2 + b + 1)
                            sp.dma_start(yn[:, b], y_d[ds(i * 1024 + b * TW, TW), :].rearrange("(j p) c -> p j c", p=P)).then_inc(y_in[b], 16)

                    with sp.Fori(0, TILES // 2) as i:
                        for b in range(2):
                            sp.wait_ge(o_free, i * 2 + b + 1)
                            for buf, src, lead in ((ofb, o_d[0], CTX // P), (obb, o_d[1], CTX // P), (szb, sz_d, 0)):
                                sp.dma_start(buf[:, b], src[ds(i * 2 + (b + lead), 1)].rearrange("a p h t -> p (a h) t")).then_inc(o_in[b], 16)
                @block.gpsimd
                def _(pool):
                    with pool.Fori(0, 2) as i:
                        for b in range(2):
                            for h in range(2):
                                pool.wait_ge(y_ok1, i * 4 + b * 2 + h + 3)
                                plainly(pool)
                                v = x0T[:, h, ds(i * 1024 + b * TW, TW)]
                                pool.tensor_tensor(v, v, ty[:, h, :], ALU.mult).then_inc(y_ok2, 1)

                    with pool.Fori(0, TILES // 2) as i:
                        for b in range(2):
                            pool.wait_ge(o_in[b], i * 48 + 48)
                            pool.tensor_tensor(ofb[:, b], ofb[:, b], obb[:, b], ALU.add).then_inc(sum_ok, 1)
                @block.scalar
                def _(act):
                    act.preload_act_table_set("natural_log_exp_and_others")
                    with act.Fori(0, TILES // 2) as i:
                        for b in range(2):
                            at = i * 2 + b + 1
                            act.wait_ge(sum_ok, at)
                            act.activation(sqb[:, b], ofb[:, b], ACT.Square).then_inc(osq_ok, 1)
                            act.wait_ge(oss_ok, at)
                            act.activation(ss[:, b, :], ss[:, b, :], ACT.Ln, bias=epst[:, 0:1], scale=1.0 / HD).then_inc(oln, 1)
                            act.wait_ge(oln, at)
                            act.activation(ss[:, b, :], ss[:, b, :], ACT.Exp, scale=-0.5).then_inc(ort, 1)

                @block.vector
                def _(dve):
                    dve.sem_inc(o_free, 2)
                    dve.sem_inc(y_free, 2)
                    dve.sem_inc(y_ok1, 2)
                    with dve.Fori(0, 2) as i:
                        for b in range(2):
                            for h in range(2):
                                dve.wait_ge(y_tr, i * 4 + b * 2 + h + 1)
                                dve.wait_ge(y_ok2, i * 4 + b * 2 + h + 1)
                                dve.scalar_tensor_tensor(ty[:, h, :], zT[:, h, ds(i * 1024 + b * TW, TW)], cols[:, R_HYD + h:R_HYD + h + 1],
                                                         PS[4 + h][:, :], ALU.mult, ALU.add).then_inc(y_ok1, 1)

                    with dve.Fori(0, TILES // 2) as i:
                        for b in range(2):
                            at = i * 2 + b + 1
                            dve.wait_ge(osq_ok, at)
                            dve.reduce_sum(ss[:, b, :], sqb[:, b], axis=AXX).then_inc(oss_ok, 1)
                            dve.wait_ge(ort, at)
                            dve.tensor_tensor(ofb[:, b], ofb[:, b], ss[:, b, :].unsqueeze(2).to_broadcast([P, HEADS, P]), ALU.mult).then_inc(on_ok, 1)
                            dve.wait_ge(o_tr, at)
                            dve.scalar_tensor_tensor(yaT[:, :, ds(i * 2 * P + b * P, P)], PS[b][:, :].rearrange("p (h t) -> p h t", t=P),
                                                     cols[:, R_NG:R_NG + 1], szb[:, b], ALU.mult, ALU.mult).then_inc(ya_ok, 1)
                            dve.wait_ge(ya_ok, at)
                            dve.sem_inc(o_free, 1)
                @block.tensor
                def _(pe):
                    pe.sem_inc(y_ok2, 2)
                    with pe.Fori(0, 2) as i:
                        for b in range(2):
                            pe.wait_ge(y_in[b], i * 16 + 16)
                            for h in range(2):
                                pe.wait_ge(y_ok1, i * 4 + b * 2 + h + 1)
                                for j in range(4):
                                    last = pe.transpose(PS[4 + h][:, j * P:(j + 1) * P], yn[:, b, j, h * P:(h + 1) * P], eye[:, :])
                                last.then_inc(y_tr, 1)
                            pe.wait_ge(y_tr, i * 4 + b * 2 + 2)
                            pe.sem_inc(y_free, 1)
                    with pe.Fori(0, TILES // 2) as i:
                        for b in range(2):
                            pe.wait_ge(on_ok, i * 2 + b + 1)
                            for h in range(HEADS):
                                last = pe.transpose(PS[b][:, h * P:(h + 1) * P], ofb[:, b, h, :], eye[:, :])
                            last.then_inc(o_tr, 1)
        if stop == 11:
            return

        with ExitStack() as st:
            gw = sbt(st, "gw", [P, 2, 3, KD, P])
            bw = sbt(st, "bw", [P, 2, 8, P])
            sg, pr = sbt(st, "sg_m", [P, 2, TW]), sbt(st, "pr", [P, 4, TW])
            mg = sbt(st, "mg", [P, 2, TW])
            m_in, m_free, g_mm, sg_ok, pr_ok, add1, add2 = [sem("m_in0"), sem("m_in1")], sem("m_free"), sem("g_mm"), sem("sg_ok"), sem("pr_ok"), sem("add1"), sem("add2")
            mg_st = [sem("mg_st0"), sem("mg_st1")]
            branch = [(yaT, 0, 4), (x0T, 4, 2), (ycT, 6, 2)]
            UM = 3 * NT
            with nc.Block() as block:
                @block.sync
                def _(sp):
                    for b in range(2):
                        sp.sem_inc(mg_st[b], 16)

                    def load(m, b):
                        for j in range(3):
                            sp.dma_start(gw[:, b, j], A["w_in"][0, :, ds(m * P + (G_OFF + j * D), P)].rearrange("(k p) c -> p k c", p=P)).then_inc(m_in[b], 16)
                        for name, at, k in (("w_branch_a", 0, 4), ("w_branch_b", 4, 2), ("w_branch_c", 6, 2)):
                            sp.dma_start(bw[:, b, at:at + k], A[name][0, :, ds(m * P, P)].rearrange("(k p) c -> p k c", p=P)).then_inc(m_in[b], 16)

                    load(0, 0)
                    with sp.Fori(0, KD // 2) as i:
                        for b in range(2):
                            sp.wait_ge(m_free, i * 2 + b + 1)
                            load((i * 2 + b + 1) % KD, 1 - b)
                            for n in range(NT):
                                sp.wait_ge(add2, i * (2 * NT) + b * NT + n + 3)
                                sp.dma_start(mg_d[ds(i * 2 + b, 1), :, n * TW:(n + 1) * TW].rearrange("a p t -> p (a t)"),
                                             mg[:, n % 2, :]).then_inc(mg_st[n % 2], 16)
                    for b in range(2):
                        sp.wait_ge(mg_st[b], 16 * (KD * NT // 2 + 1))
                    sp.wait_ge(m_in[0], 96 * (KD // 2 + 1))

                @block.tensor
                def _(pe):
                    with pe.Fori(0, KD // 2) as i:
                        for b in range(2):
                            pe.wait_ge(m_in[b], i * 96 + 96)
                            for u in range(UM):
                                n, j = u // 3, u % 3
                                at = i * (2 * UM) + b * UM + u
                                g, o = PS[u % 4 * 2], PS[u % 4 * 2 + 1]
                                pe.wait_ge(pr_ok, at + 1)
                                for k in range(KD):
                                    pe.matmul(g[:, :], gw[:, b, j, k, :], hT[:, k, toff(n + 1):toff(n + 1) + TW], start=(k == 0), stop=(k == KD - 1))
                                src, w0, nk = branch[j]
                                for k in range(nk):
                                    last = pe.matmul(o[:, :], bw[:, b, w0 + k, :], src[:, k, n * TW:(n + 1) * TW], start=(k == 0), stop=(k == nk - 1))
                                last.then_inc(g_mm, 1)
                            pe.wait_ge(g_mm, i * (2 * UM) + b * UM + UM)
                            pe.sem_inc(m_free, 1)

                @block.scalar
                def _(act):
                    with act.Fori(0, KD // 2) as i:
                        for b in range(2):
                            for u in range(UM):
                                at = i * (2 * UM) + b * UM + u
                                act.wait_ge(g_mm, at + 1)
                                act.wait_ge(pr_ok, at + 3)
                                act.activation(sg[:, u % 2, :], PS[u % 4 * 2][:, :], ACT.Sigmoid).then_inc(sg_ok, 1)

                @block.vector
                def _(dve):
                    dve.sem_inc(m_free, 1)
                    dve.sem_inc(pr_ok, 4)
                    dve.sem_inc(add2, 2)
                    with dve.Fori(0, KD // 2) as i:
                        for b in range(2):
                            for u in range(UM):
                                n, j = u // 3, u % 3
                                at = i * (2 * UM) + b * UM + u
                                dve.wait_ge(sg_ok, at + 1)
                                dve.wait_ge(add2, i * (2 * NT) + b * NT + (u - 1) // 3 + 2)
                                dve.tensor_tensor(pr[:, u % 4, :], sg[:, u % 2, :], PS[u % 4 * 2 + 1][:, :], ALU.mult).then_inc(pr_ok, 1)

                @block.gpsimd
                def _(pool):
                    with pool.Fori(0, KD // 2) as i:
                        for b in range(2):
                            for n in range(NT):
                                at = i * (2 * NT) + b * NT + n
                                u = 3 * n
                                pool.wait_ge(pr_ok, at * 3 + 6)
                                pool.wait_ge(mg_st[n % 2], i * (16 * NT) + (b * NT // 2 + n // 2) * 16 + 16)
                                pool.tensor_tensor(mg[:, n % 2, :], pr[:, u % 4, :], pr[:, (u + 1) % 4, :], ALU.add).then_inc(add1, 1)
                                pool.wait_ge(pr_ok, at * 3 + 7)
                                pool.wait_ge(add1, at + 1)
                                pool.tensor_tensor(mg[:, n % 2, :], mg[:, n % 2, :], pr[:, (u + 2) % 4, :], ALU.add).then_inc(add2, 1)
        if stop == 12:
            return
        yst.close()
        PH.close()

        fst = top.enter_context(ExitStack())
        affT = sbt(fst, "affT", [NE, SEQ])
        fgb = sbt(fst, "fgb", [P, D])
        with ExitStack() as st:
            wo, rw = sbt(st, "wo", [P, KD, D]), sbt(st, "rw", [P, KD, NE])
            mt = sbt(st, "mt", [P, 2, KD, 2 * P])
            xt, x1 = sbt(st, "xt", [P, 2, D]), sbt(st, "x1", [P, 2, D])
            sqx, h2, h2T = sbt(st, "sqx", [P, 2, D]), sbt(st, "h2", [P, 2, D]), sbt(st, "h2T", [P, 2, KD, P])
            s1 = sbt(st, "s1", [P, 2, 1])
            mx, ex, sm = sbt(st, "mx", [P, 2, 1]), sbt(st, "ex", [P, 2, NE]), sbt(st, "sm", [P, 2, 1])
            wo_in, mt_in, mt_free, xt_in = sem("wo_in"), [sem("mt_in0"), sem("mt_in1")], sem("mt_free"), [sem("xt_in0"), sem("xt_in1")]
            wo_mm, g_ok, x1_ok, x1_st, h2_st = sem("wo_mm"), sem("g_ok"), sem("x1_ok"), [sem("x1_st0"), sem("x1_st1")], [sem("h2_st0"), sem("h2_st1")]
            s_sq, s_ln, s_rt, hm_ok, h2_ok, h2_tr, h2_cp = sem("s_sq"), sem("s_ln"), sem("s_rt"), sem("hm_ok"), sem("h2_ok"), sem("h2_tr"), sem("h2_cp")
            lg_mm, mx_ch, ex_ok, rc_ch, aff_ok, aff_tr, affT_ok = sem("lg_mm"), sem("mx_ch"), sem("ex_ok"), sem("rc_ch"), sem("aff_ok"), sem("aff_tr"), sem("affT_ok")
            with nc.Block() as block:
                @block.sync
                def _(sp):
                    sp.dma_start(wo[:, :, :], A["w_out"][0].rearrange("(k p) c -> p k c", p=P)).then_inc(wo_in, 16)
                    sp.dma_start(rw[:, :, :], A["router_w"][0].rearrange("(k p) c -> p k c", p=P)).then_inc(wo_in, 16)
                    sp.dma_start(fgb[:, :], A["final_norm_g"].unsqueeze(0).to_broadcast([P, D])).then_inc(wo_in, 16)
                    with sp.Fori(0, TILES // 4) as i:
                        for j in range(4):
                            if j % 2 == 0:
                                sp.wait_ge(mt_free, i * 2 + j // 2 + 1)
                                sp.dma_start(mt[:, j // 2], mg_d[:, :, ds(i * 512 + j * P, 2 * P)].rearrange("k p t -> p k t")).then_inc(mt_in[j // 2], 16)
                            sp.wait_ge(x1_ok, i * 4 + j + 1)
                            sp.dma_start(xt[:, j % 2], A["x"][0, ds(i * 512 + j * P, P), :]).then_inc(xt_in[j % 2], 16)

                @block.tensor
                def _(pe):
                    def tail(i, j, at):
                        b = j % 2
                        pe.wait_ge(h2_ok, at)
                        pe.wait_ge(h2_cp, at)
                        for k in range(KD):
                            last = pe.transpose(PS[4 + k // 4][:, k % 4 * P:(k % 4 + 1) * P], h2[:, b, k * P:(k + 1) * P], eye[:, :])
                        last.then_inc(h2_tr, 1)
                        pe.wait_ge(h2_cp, at + 1)
                        for k in range(KD):
                            last = pe.matmul(PS[6][:, 0:NE], h2T[:, b, k, :], rw[:, k, :], start=(k == 0), stop=(k == KD - 1))
                        last.then_inc(lg_mm, 1)
                        pe.wait_ge(aff_ok, at)
                        pe.transpose(PS[7][0:NE, 0:P], ex[:, b, :], eye[:, :]).then_inc(aff_tr, 1)

                    pe.wait_ge(wo_in, 48)
                    with pe.Fori(0, TILES // 4) as i:
                        for j in range(4):
                            at = i * 4 + j
                            b = j % 2
                            if b == 0:
                                pe.wait_ge(mt_in[j // 2], i * 16 + 16)
                            pe.wait_ge(g_ok, at * 2 + 1)
                            for c in range(2):
                                for k in range(KD):
                                    last = pe.matmul(PS[2 * b + c][:, :], mt[:, j // 2, k, b * P:(b + 1) * P], wo[:, k, c * 512:(c + 1) * 512],
                                                     start=(k == 0), stop=(k == KD - 1))
                                last.then_inc(wo_mm, 1)
                            if b == 1:
                                pe.wait_ge(wo_mm, at * 2 + 2)
                                pe.sem_inc(mt_free, 1)
                            tail(i, j, at + 1)

                @block.vector
                def _(dve):
                    dve.sem_inc(mt_free, 2)
                    dve.sem_inc(g_ok, 4)
                    dve.sem_inc(x1_ok, 2)
                    with dve.Fori(0, TILES // 4) as i:
                        for j in range(4):
                            at = i * 4 + j
                            b = j % 2
                            dve.wait_ge(x1_st[b], i * 32 + j // 2 * 16 + 16)
                            for c in range(2):
                                dve.wait_ge(wo_mm, at * 2 + c + 1)
                                dve.tensor_tensor(x1[:, b, c * 512:(c + 1) * 512], PS[2 * b + c][:, :], modb[:, 0, c * 512:(c + 1) * 512],
                                                  ALU.mult).then_inc(g_ok, 1)
                            dve.wait_ge(s_rt, at + 1)
                            dve.wait_ge(h2_st[b], i * 32 + j // 2 * 16 + 16)
                            dve.scalar_tensor_tensor(h2[:, b, :], x1[:, b, :], s1[:, b, :], modb[:, 2, :], ALU.mult, ALU.mult).then_inc(hm_ok, 1)
                            dve.wait_ge(lg_mm, at + 1)
                            dve.reduce_max(mx[:, b, :], PS[6][:, 0:NE], axis=AXX).then_inc(mx_ch, 1)
                            dve.wait_ge(mx_ch, at * 2 + 1)
                            dve.tensor_scalar(mx[:, b, :], mx[:, b, :], -1.0, None, ALU.mult).then_inc(mx_ch, 1)
                            dve.wait_ge(ex_ok, at + 1)
                            dve.reciprocal(sm[:, b, :], sm[:, b, :]).then_inc(rc_ch, 1)
                            dve.wait_ge(rc_ch, at + 1)
                            dve.tensor_scalar(ex[:, b, :], ex[:, b, :], sm[:, b, :], None, ALU.mult).then_inc(aff_ok, 1)
                            dve.wait_ge(aff_tr, at + 1)
                            dve.tensor_copy(affT[:, ds(i * 512 + j * P, P)], PS[7][0:NE, 0:P]).then_inc(affT_ok, 1)

                @block.scalar
                def _(act):
                    act.preload_act_table_set("natural_log_exp_and_others")
                    act.sem_inc(h2_cp, 1)
                    for b in range(2):
                        act.sem_inc(x1_st[b], 16)
                        act.sem_inc(h2_st[b], 16)
                    with act.Fori(0, TILES // 4) as i:
                        for j in range(4):
                            at = i * 4 + j
                            b = j % 2
                            act.wait_ge(x1_ok, at + 3)
                            act.dma_start(x1_d[ds(i * 512 + j * P, P), :], x1[:, b, :]).then_inc(x1_st[b], 16)
                            act.activation(sqx[:, b, :], x1[:, b, :], ACT.Square, accum_out=s1[:, b, :]).then_inc(s_sq, 1)
                            act.wait_ge(s_sq, at + 1)
                            act.activation(s1[:, b, :], s1[:, b, :], ACT.Ln, bias=epst[:, 0:1], scale=1.0 / D).then_inc(s_ln, 1)
                            act.wait_ge(s_ln, at + 1)
                            act.activation(s1[:, b, :], s1[:, b, :], ACT.Exp, scale=-0.5).then_inc(s_rt, 1)
                            act.wait_ge(h2_ok, at + 1)
                            act.dma_start(h2_d[ds(i * 512 + j * P, P), :], h2[:, b, :]).then_inc(h2_st[b], 16)
                            act.wait_ge(h2_tr, at + 1)
                            act.activation(h2T[:, b, 0:4, :].rearrange("p k t -> p (k t)"), PS[4][:, :], ACT.Copy)
                            act.activation(h2T[:, b, 4:8, :].rearrange("p k t -> p (k t)"), PS[5][:, :], ACT.Copy).then_inc(h2_cp, 1)
                            act.wait_ge(mx_ch, at * 2 + 2)
                            act.activation(ex[:, b, :], PS[6][:, 0:NE], ACT.Exp, bias=mx[:, b, :], accum_out=sm[:, b, :]).then_inc(ex_ok, 1)
                    for b in range(2):
                        act.wait_ge(x1_st[b], 16 * (TILES // 2 + 1))
                        act.wait_ge(h2_st[b], 16 * (TILES // 2 + 1))

                @block.gpsimd
                def _(pool):
                    with pool.Fori(0, TILES // 4) as i:
                        for j in range(4):
                            at = i * 4 + j
                            b = j % 2
                            pool.wait_ge(g_ok, at * 2 + 6)
                            pool.wait_ge(xt_in[b], i * 32 + j // 2 * 16 + 16)
                            pool.tensor_tensor(x1[:, b, :], x1[:, b, :], xt[:, b, :], ALU.add).then_inc(x1_ok, 1)
                            pool.wait_ge(hm_ok, at + 1)
                            pool.tensor_tensor(h2[:, b, :], h2[:, b, :], modb[:, 1, :], ALU.add).then_inc(h2_ok, 1)
        if stop == 13:
            return

        idxP, valP = sbt(fst, "idxP", [P, 2, NE], U32), sbt(fst, "valP", [P, 2, NE])
        with ExitStack() as st:
            m8, i8 = sbt(st, "m8", [NE, 2, 8]), sbt(st, "i8", [NE, 2, 8], U32)
            vals, idxf = sbt(st, "vals", [NE, CAP]), sbt(st, "idxf", [NE, CAP])
            k_mx, k_ix, k_rp, k_cp, k_tr, slots_ok = sem("k_mx"), sem("k_ix"), sem("k_rp"), sem("k_cp"), sem("k_tr"), sem("slots_ok")
            wgu = sbt(st, "wgu", [P, 2, 2, KD, FF])
            wd = sbt(st, "wd", [P, FT, D])
            xe, xeT = sbt(st, "xe", [P, 2, 2, D]), sbt(st, "xeT", [P, KD, CAP])
            hid, sgm, gm1 = sbt(st, "hid_e", [P, FT, CAP]), sbt(st, "sgm", [P, 2, CAP]), sbt(st, "gm1", [P, 2, CAP])
            ye = sbt(st, "ye", [P, 2, D])
            idc = sbt(st, "idc", [P, 2, 2], U32)
            wgu_in, wgu_free, wd_in, wd_free = [sem("wgu_in0"), sem("wgu_in1")], sem("wgu_free"), sem("wd_in"), sem("wd_free")
            id_ok, xe_in, xe_tr, xe_cp, gu_mm, sg_ok, gs_ok, hid_ok = sem("id_ok"), [sem("xe_in0"), sem("xe_in1")], sem("xe_tr"), sem("xe_cp"), sem("gu_mm"), sem("sg_e"), sem("gs_ok"), sem("hid_ok")
            dn_mm, ye_ok, ye_st, ye_free = sem("dn_mm"), sem("ye_ok"), sem("ye_st"), sem("ye_free")
            with nc.Block() as block:
                @block.sync
                def _(sp):
                    with sp.Fori(0, NE // 2) as i:
                        for b in range(2):
                            e = ds(i * 2 + b, 1)
                            sp.wait_ge(wgu_free, i * 2 + b + 1)
                            for g, name in enumerate(("exp_w_gate", "exp_w_up")):
                                sp.dma_start(wgu[:, b, g], A[name][0, e, :, :].rearrange("a (k p) f -> p (a k) f", p=P)).then_inc(wgu_in[b], 16)
                            sp.wait_ge(wd_free, i * 2 + b + 1)
                            sp.dma_start(wd[:, :, :], A["exp_w_down"][0, e, :, :].rearrange("a (k p) f -> p (a k) f", p=P)).then_inc(wd_in, 16)

                @block.vector
                def _(dve):
                    dve.sem_inc(k_rp, 1)
                    dve.sem_inc(wgu_free, 2)
                    dve.sem_inc(wd_free, 1)
                    dve.sem_inc(ye_free, 1)
                    dve.sem_inc(hid_ok, 2)
                    dve.sem_inc(gs_ok, 2)
                    with dve.Fori(0, CAP // 16) as i:
                        for b in range(2):
                            at = i * 2 + b
                            dve.wait_ge(k_rp, at + 1)
                            dve.wait_ge(k_cp, at * 2 + 2)
                            plainly(dve)
                            dve.max(m8[:, b, :], affT[:, :]).then_inc(k_mx, 1)
                            dve.wait_ge(k_mx, at + 1)
                            plainly(dve)
                            dve.max_index(i8[:, b, :], m8[:, b, :], affT[:, :]).then_inc(k_ix, 1)
                            dve.wait_ge(k_ix, at + 1)
                            plainly(dve)
                            dve.match_replace(affT[:, :], m8[:, b, :], affT[:, :], -1.0).then_inc(k_rp, 1)
                    dve.wait_ge(k_tr, 1)
                    dve.tensor_copy(idxP[:, :, :].rearrange("p j e -> p (j e)"), PS[0][:, 0:32])
                    dve.tensor_copy(valP[:, :, :].rearrange("p j e -> p (j e)"), PS[0][:, 32:64]).then_inc(slots_ok, 1)

                    with dve.Fori(0, NE // 2) as i:
                        for b in range(2):
                            at = i * 2 + b
                            for f in range(FT):
                                dve.wait_ge(sg_ok, at * FT + f + 1)
                                dve.tensor_tensor(gm1[:, f % 2, :], sgm[:, f % 2, :], PS[4 + f % 2][:, 0:CAP], ALU.mult).then_inc(gs_ok, 1)
                                dve.wait_ge(gs_ok, at * FT + f + 3)
                                dve.tensor_tensor(hid[:, f, :], gm1[:, f % 2, :], PS[4 + f % 2][:, CAP:2 * CAP], ALU.mult).then_inc(hid_ok, 1)
                            dve.wait_ge(ye_free, at + 1)
                            for m in range(4):
                                j, c = m // 2, m % 2
                                dve.wait_ge(dn_mm, at * 4 + m + 1)
                                g2 = modb[:, 3, c * 512:(c + 1) * 512]
                                dve.scalar_tensor_tensor(ye[:, j, c * 512:(c + 1) * 512], PS[6 + c][:, :], valP[:, j, ds(at, 1)], g2,
                                                         ALU.mult, ALU.mult).then_inc(ye_ok, 1)

                @block.scalar
                def _(act):
                    act.sem_inc(k_cp, 4)
                    with act.Fori(0, CAP // 16) as i:
                        for b in range(2):
                            at = i * 2 + b
                            act.wait_ge(k_ix, at + 1)
                            plainly(act)
                            act.activation(vals[:, ds(i * 16 + b * 8, 8)], m8[:, b, :], ACT.Copy).then_inc(k_cp, 1)
                            act.activation(idxf[:, ds(i * 16 + b * 8, 8)], i8[:, b, :], ACT.Copy).then_inc(k_cp, 1)

                    act.sem_inc(xe_cp, 4)
                    with act.Fori(0, NE // 2) as i:
                        for b in range(2):
                            at = i * 2 + b
                            for k2 in range(KD // 2):
                                act.wait_ge(xe_tr, at * 4 + k2 + 1)
                                act.activation(xeT[:, 2 * k2:2 * k2 + 2, :].rearrange("p k t -> p (k t)"), PS[k2][:, :], ACT.Copy).then_inc(xe_cp, 1)
                            for f in range(FT):
                                act.wait_ge(gu_mm, at * FT + f + 1)
                                act.wait_ge(gs_ok, at * FT + f + 1)
                                act.activation(sgm[:, f % 2, :], PS[4 + f % 2][:, 0:CAP], ACT.Sigmoid).then_inc(sg_ok, 1)

                @block.tensor
                def _(pe):
                    pe.wait_ge(k_cp, 4 + 2 * (CAP // 8))
                    for j in range(2):
                        pe.transpose(PS[0][:, j * NE:(j + 1) * NE], idxf[:, j * P:(j + 1) * P], eye[0:NE, 0:NE])
                        last = pe.transpose(PS[0][:, 32 + j * NE:32 + (j + 1) * NE], vals[:, j * P:(j + 1) * P], eye[0:NE, 0:NE])
                    last.then_inc(k_tr, 1)

                    with pe.Fori(0, NE // 2) as i:
                        for b in range(2):
                            at = i * 2 + b
                            pe.wait_ge(xe_in[b], i * 32 + 32)
                            for k2 in range(KD // 2):
                                pe.wait_ge(xe_cp, at * 4 + k2 + 1)
                                for k in (2 * k2, 2 * k2 + 1):
                                    for j in range(2):
                                        last = pe.transpose(PS[k2][:, (k % 2 * 2 + j) * P:(k % 2 * 2 + j + 1) * P], xe[:, b, j, k * P:(k + 1) * P], eye[:, :])
                                last.then_inc(xe_tr, 1)
                            pe.wait_ge(xe_cp, at * 4 + 8)
                            pe.wait_ge(wgu_in[b], i * 32 + 32)
                            for f in range(FT):
                                pe.wait_ge(hid_ok, at * FT + f + 1)
                                for g in range(2):
                                    for k in range(KD):
                                        last = pe.matmul(PS[4 + f % 2][:, g * CAP:(g + 1) * CAP], wgu[:, b, g, k, f * P:(f + 1) * P], xeT[:, k, :],
                                                         start=(k == 0), stop=(k == KD - 1))
                                last.then_inc(gu_mm, 1)
                            pe.wait_ge(gu_mm, at * FT + FT)
                            pe.sem_inc(wgu_free, 1)
                            pe.wait_ge(wd_in, at * 16 + 16)
                            pe.wait_ge(hid_ok, at * FT + FT + 2)
                            for m in range(4):
                                j, c = m // 2, m % 2
                                pe.wait_ge(ye_ok, at * 4 + m - 1) if m >= 2 else None
                                for f in range(FT):
                                    last = pe.matmul(PS[6 + c][:, :], hid[:, f, j * P:(j + 1) * P], wd[:, f, c * 512:(c + 1) * 512],
                                                     start=(f == 0), stop=(f == FT - 1))
                                last.then_inc(dn_mm, 1)
                            pe.wait_ge(dn_mm, at * 4 + 4)
                            pe.sem_inc(wd_free, 1)

                @block.gpsimd
                def _(pool):
                    def gather(e, b, ready):
                        pool.tensor_copy(idc[:, b, :], idxP[:, :, e].rearrange("p j a -> p (j a)")).then_inc(id_ok, 1)
                        pool.wait_ge(id_ok, ready)
                        plainly(pool)
                        for j in range(2):
                            pool.indirect_dma_start(xe[:, b, j, :], None, h2_d, bass.IndirectOffsetOnAxis(idc[:, b, j:j + 1], 0)).then_inc(xe_in[b], 16)

                    pool.wait_ge(slots_ok, 1)
                    gather(ds(0, 1), 0, 1)
                    with pool.Fori(0, NE // 2) as i:
                        for b in range(2):
                            at = i * 2 + b
                            gather(ds((at + 1) % NE, 1), 1 - b, at + 2)
                            for j in range(2):
                                pool.wait_ge(ye_ok, at * 4 + j * 2 + 2)
                                plainly(pool)
                                pool.indirect_dma_start(x1_d, bass.IndirectOffsetOnAxis(idc[:, b, j:j + 1], 0), ye[:, j, :], None,
                                                        compute_op=ALU.add).then_inc(ye_st, 16)
                            pool.wait_ge(ye_st, at * 32 + 32)
                            pool.sem_inc(ye_free, 1)
                    pool.wait_ge(xe_in[0], 32 * (NE // 2 + 1))
        if stop == 15:
            return

        with ExitStack() as st:
            NBUF = 4
            x1b, sqf = sbt(st, "x1b", [P, NBUF, D]), sbt(st, "sqf", [P, 2, D])
            sf = sbt(st, "sf", [P, NBUF, 1])
            n_in, n_sq, n_ln, n_rt, n_ok = [sem(f"n_in{b}") for b in range(NBUF)], sem("n_sq"), sem("n_ln"), sem("n_rt"), sem("nf_ok")
            n_st = [sem(f"n_st{b}") for b in range(NBUF)]
            with nc.Block() as block:
                @block.sync
                def _(sp):
                    for b in range(NBUF):
                        sp.sem_inc(n_st[b], 16)
                    with sp.Fori(0, TILES // NBUF) as i:
                        for b in range(NBUF):
                            sp.wait_ge(n_st[b], i * 16 + 16)
                            sp.dma_start(x1b[:, b, :], x1_d[ds(i * (NBUF * P) + b * P, P), :]).then_inc(n_in[b], 16)

                @block.vector
                def _(dve):
                    with dve.Fori(0, TILES // NBUF) as i:
                        for b in range(NBUF):
                            dve.wait_ge(n_rt, i * NBUF + b + 1)
                            dve.scalar_tensor_tensor(x1b[:, b, :], x1b[:, b, :], sf[:, b, :], fgb[:, :], ALU.mult, ALU.mult).then_inc(n_ok, 1)

                @block.scalar
                def _(act):
                    act.preload_act_table_set("natural_log_exp_and_others")
                    with act.Fori(0, TILES // NBUF) as i:
                        for b in range(NBUF):
                            at = i * NBUF + b
                            act.wait_ge(n_in[b], i * 16 + 16)
                            act.activation(sqf[:, b % 2, :], x1b[:, b, :], ACT.Square, accum_out=sf[:, b, :]).then_inc(n_sq, 1)
                            act.wait_ge(n_sq, at + 1)
                            act.activation(sf[:, b, :], sf[:, b, :], ACT.Ln, bias=epst[:, 0:1], scale=1.0 / D).then_inc(n_ln, 1)
                            act.wait_ge(n_ln, at + 1)
                            act.activation(sf[:, b, :], sf[:, b, :], ACT.Exp, scale=-0.5).then_inc(n_rt, 1)
                            act.wait_ge(n_ok, at + 1)
                            act.dma_start(out[0, ds(i * (NBUF * P) + b * P, P), :], x1b[:, b, :]).then_inc(n_st[b], 16)
                    for b in range(NBUF):
                        act.wait_ge(n_st[b], 16 * (TILES // NBUF + 1))


_INS = ["x", "c", "ctx", "c_ctx", "ada_w", "ada_b", "norm1_g", "norm2_g", "w_in", "dn_conv_w", "dn_a_log", "dn_dt_bias",
        "dn_norm_g", "hy_conv_w", "hy_conv_b", "hy_w1", "hy_b1", "hy_w2", "hy_b2", "hy_w3", "hy_freq", "hy_d_bias",
        "sc_conv_w", "w_branch_a", "w_branch_b", "w_branch_c", "w_out", "router_w", "exp_w_gate", "exp_w_up",
        "exp_w_down", "final_norm_g"]


def kernel(**inputs):
    import concourse.bacc as bacc
    from concourse.bass_utils import run_bass_kernel_spmd

    nc = bacc.Bacc("TRN2", target_bir_lowering=False, num_devices=1)
    given = {n: np.ascontiguousarray(inputs[n]) for n in _INS}
    given.update(shape_tables())
    A = {n: nc.dram_tensor(f"in_{n}", a.shape, F32, kind="ExternalInput").ap() for n, a in given.items()}
    out = nc.dram_tensor("out_x", (1, SEQ, D), F32, kind="ExternalOutput").ap()
    build(nc, A, out)
    r = run_bass_kernel_spmd(nc, [{f"in_{n}": a for n, a in given.items()}], core_ids=[0])
    return r.results[0]["out_x"]
```
